# Optimizing a Trainium2 kernel written in Bass

```python
import jax
import jax.numpy as jnp
from jax import lax
import numpy as np

D_MODEL = 1024
BATCH = 1
SEQ = 256
DEPTH = 4

GRID_W = 64
CTX_LEN = 256
N_MIXERS = 3
N_MLA_LAYERS = (DEPTH + 2) // 3
N_NA_LAYERS = (DEPTH + 1) // 3
N_SWA_LAYERS = DEPTH // 3

D_FF = -(-8 * D_MODEL // (3 * 256)) * 256
NORM_EPS = 1e-6
ROPE_THETA = 10000.0
NEG_INF = -1e30
Q_BLOCK = 128

MLA_HEADS = D_MODEL // 128
MLA_Q_LORA = D_MODEL // 4
MLA_KV_LORA = D_MODEL // 4
MLA_NOPE = 128
MLA_ROPE = 64
MLA_V = 128

NA_HEADS = D_MODEL // 64
NA_HEAD_DIM = 64
NA_WIN_ROWS = 8
NA_WIN_COLS = 16

SWA_HEADS = D_MODEL // 64
SWA_KV_HEADS = SWA_HEADS // 8
SWA_HEAD_DIM = 64
SWA_WINDOW = 128
SWA_BLOCK = 128

kernel_name = "hybrid_mla_na_swa_dit_trunk"

def rms_norm(x, g):
    xf = x.astype(jnp.float32)
    y = xf * lax.rsqrt(jnp.mean(xf * xf, axis=-1, keepdims=True) + NORM_EPS)
    return (y * g.astype(jnp.float32)).astype(x.dtype)

def modulate(h, shift, scale):
    return h * (1 + scale) + shift

def axial_rope_tables(n_tokens, rot_dim):
    t = jnp.arange(n_tokens)
    row = (t // GRID_W).astype(jnp.float32)
    col = (t % GRID_W).astype(jnp.float32)
    n_freq = rot_dim // 4
    inv = ROPE_THETA ** (-jnp.arange(n_freq, dtype=jnp.float32) / n_freq)
    ang = jnp.concatenate([row[:, None] * inv, col[:, None] * inv], axis=-1)
    return jnp.cos(ang), jnp.sin(ang)

def apply_rope(x, cos, sin):
    xf = x.astype(jnp.float32)
    half = xf.shape[-1] // 2
    x1, x2 = xf[..., :half], xf[..., half:]
    cs, sn = cos[None, :, None, :], sin[None, :, None, :]
    return jnp.concatenate([x1 * cs - x2 * sn, x2 * cs + x1 * sn], axis=-1).astype(x.dtype)

def softmax_attend(q, k, v, scale):
    s = jnp.einsum('bqhd,bkhd->bhqk', q, k).astype(jnp.float32) * scale
    p = jax.nn.softmax(s, axis=-1).astype(v.dtype)
    return jnp.einsum('bhqk,bkhd->bqhd', p, v)

def dense_block_attention(q, k, v, scale):
    b, n, h, dk = q.shape
    nb = n // Q_BLOCK
    qb = jnp.moveaxis(q.reshape(b, nb, Q_BLOCK, h, dk), 1, 0)
    out = lax.map(lambda q_blk: softmax_attend(q_blk, k, v, scale), qb)
    return jnp.moveaxis(out, 0, 1).reshape(b, n, h, v.shape[-1])

def swiglu(h, w_in, w_out):
    gate, up = jnp.split(h @ w_in, 2, axis=-1)
    return (jax.nn.silu(gate) * up) @ w_out

def mla_project(h, w_in, g_q, w_uq, g_kv, w_ukv):
    b, n, _ = h.shape
    a = h @ w_in
    q_lat = a[..., :MLA_Q_LORA]
    kv_lat = a[..., MLA_Q_LORA:MLA_Q_LORA + MLA_KV_LORA]
    k_pe = a[..., MLA_Q_LORA + MLA_KV_LORA:][:, :, None, :]
    q = (rms_norm(q_lat, g_q) @ w_uq).reshape(b, n, MLA_HEADS, MLA_NOPE + MLA_ROPE)
    kv = (rms_norm(kv_lat, g_kv) @ w_ukv).reshape(b, n, MLA_HEADS, MLA_NOPE + MLA_V)
    return q[..., :MLA_NOPE], q[..., MLA_NOPE:], kv[..., :MLA_NOPE], k_pe, kv[..., MLA_NOPE:]

def mla_assemble(q_nope, q_pe, k_nope, k_pe):
    q = jnp.concatenate([q_nope, q_pe], axis=-1)
    k = jnp.concatenate([k_nope, jnp.broadcast_to(k_pe, k_nope.shape[:-1] + (MLA_ROPE,))], axis=-1)
    return q, k

def mla_mixer(hx, hc, w_in, g_q, w_uq, g_kv, w_ukv, w_o, ctx_out):
    b, n, _ = hx.shape
    scale = (MLA_NOPE + MLA_ROPE) ** -0.5
    q_nope, q_pe, k_nope, k_pe, v = mla_project(hx, w_in, g_q, w_uq, g_kv, w_ukv)
    cos, sin = axial_rope_tables(n, MLA_ROPE)
    q, k = mla_assemble(q_nope, apply_rope(q_pe, cos, sin), k_nope, apply_rope(k_pe, cos, sin))
    cq_nope, cq_pe, ck_nope, ck_pe, vc = mla_project(hc, w_in, g_q, w_uq, g_kv, w_ukv)
    qc, kc = mla_assemble(cq_nope, cq_pe, ck_nope, ck_pe)
    k_all = jnp.concatenate([kc, k], axis=1)
    v_all = jnp.concatenate([vc, v], axis=1)
    ox = dense_block_attention(q, k_all, v_all, scale).reshape(b, n, MLA_HEADS * MLA_V) @ w_o
    oc = None
    if ctx_out:
        oc = softmax_attend(qc, kc, vc, scale).reshape(b, hc.shape[1], MLA_HEADS * MLA_V) @ w_o
    return ox, oc

def na_mixer(hx, hc, w_qkv, rpb, w_o, ctx_out):
    b, n, _ = hx.shape
    rows = n // GRID_W
    wr = min(NA_WIN_ROWS, rows)
    wc = NA_WIN_COLS
    hd = NA_HEADS * NA_HEAD_DIM
    scale = NA_HEAD_DIM ** -0.5
    qkv = (hx @ w_qkv).reshape(b, rows, GRID_W, 3, NA_HEADS, NA_HEAD_DIM)
    q, k, v = qkv[..., 0, :, :], qkv[..., 1, :, :], qkv[..., 2, :, :]
    lc = hc.shape[1]
    qkv_c = (hc @ w_qkv).reshape(b, lc, 3, NA_HEADS, NA_HEAD_DIM)
    qc, kc, vc = qkv_c[:, :, 0], qkv_c[:, :, 1], qkv_c[:, :, 2]
    cols = jnp.arange(GRID_W)
    col_start = jnp.clip(cols - wc // 2, 0, GRID_W - wc)
    col_ok = (cols[None, :] >= col_start[:, None]) & (cols[None, :] < col_start[:, None] + wc)
    col_idx = jnp.clip(cols[None, :] - cols[:, None], 1 - wc, wc - 1) + (NA_WIN_COLS - 1)

    def one_row(r):
        rs = jnp.clip(r - wr // 2, 0, rows - wr)
        q_r = lax.dynamic_index_in_dim(q, r, axis=1, keepdims=False)
        k_r = lax.dynamic_slice_in_dim(k, rs, wr, axis=1)
        v_r = lax.dynamic_slice_in_dim(v, rs, wr, axis=1)
        s = jnp.einsum('bqhd,bikhd->bhqik', q_r, k_r).astype(jnp.float32) * scale
        row_idx = rs + jnp.arange(wr) - r + (NA_WIN_ROWS - 1)
        bias = rpb[:, row_idx[None, :, None], col_idx[:, None, :]]
        s = jnp.where(col_ok[:, None, :], s + bias.astype(jnp.float32), NEG_INF)
        s_c = jnp.einsum('bqhd,bkhd->bhqk', q_r, kc).astype(jnp.float32) * scale
        logits = jnp.concatenate([s.reshape(b, NA_HEADS, GRID_W, wr * GRID_W), s_c], axis=-1)
        p = jax.nn.softmax(logits, axis=-1).astype(v.dtype)
        p_n = p[..., :wr * GRID_W].reshape(b, NA_HEADS, GRID_W, wr, GRID_W)
        p_c = p[..., wr * GRID_W:]
        return jnp.einsum('bhqik,bikhd->bqhd', p_n, v_r) + jnp.einsum('bhqk,bkhd->bqhd', p_c, vc)

    out = lax.map(one_row, jnp.arange(rows))
    ox = jnp.moveaxis(out, 0, 1).reshape(b, n, hd) @ w_o
    oc = None
    if ctx_out:
        oc = softmax_attend(qc, kc, vc, scale).reshape(b, lc, hd) @ w_o
    return ox, oc

def swa_mixer(hx, hc, w_qkv, sink, w_o, ctx_out):
    b, n, _ = hx.shape
    hq, hk, dh = SWA_HEADS, SWA_KV_HEADS, SWA_HEAD_DIM
    g = hq // hk
    scale = dh ** -0.5

    def split_qkv(h):
        a = h @ w_qkv
        lead = a.shape[:2]
        q_ = a[..., :hq * dh].reshape(lead + (hq, dh))
        k_ = a[..., hq * dh:(hq + hk) * dh].reshape(lead + (hk, dh))
        v_ = a[..., (hq + hk) * dh:].reshape(lead + (hk, dh))
        return q_, k_, v_

    q, k, v = split_qkv(hx)
    qc, kc, vc = split_qkv(hc)
    lc = hc.shape[1]
    cos, sin = axial_rope_tables(n, dh)
    q = apply_rope(q, cos, sin)
    k = apply_rope(k, cos, sin)
    sink_l = sink.astype(jnp.float32).reshape(hk, g)
    pad = ((0, 0), (SWA_WINDOW, SWA_WINDOW), (0, 0), (0, 0))
    kp = jnp.pad(k, pad)
    vp = jnp.pad(v, pad)
    nb = n // SWA_BLOCK
    span = SWA_BLOCK + 2 * SWA_WINDOW
    qb = jnp.moveaxis(q.reshape(b, nb, SWA_BLOCK, hk, g, dh), 1, 0)
    rel = jnp.arange(span)[None, :] - SWA_WINDOW - jnp.arange(SWA_BLOCK)[:, None]

    def one_block(args):
        blk, q_blk = args
        start = blk * SWA_BLOCK
        k_blk = lax.dynamic_slice_in_dim(kp, start, span, axis=1)
        v_blk = lax.dynamic_slice_in_dim(vp, start, span, axis=1)
        kpos = start - SWA_WINDOW + jnp.arange(span)
        ok = (jnp.abs(rel) <= SWA_WINDOW) & ((kpos >= 0) & (kpos < n))[None, :]
        s = jnp.einsum('bqkgd,bjkd->bkgqj', q_blk, k_blk).astype(jnp.float32) * scale
        s = jnp.where(ok, s, NEG_INF)
        s_c = jnp.einsum('bqkgd,bjkd->bkgqj', q_blk, kc).astype(jnp.float32) * scale
        sink_col = jnp.broadcast_to(sink_l[None, :, :, None, None], s.shape[:-1] + (1,))
        p = jax.nn.softmax(jnp.concatenate([s, s_c, sink_col], axis=-1), axis=-1).astype(v.dtype)
        return (jnp.einsum('bkgqj,bjkd->bqkgd', p[..., :span], v_blk)
                + jnp.einsum('bkgqj,bjkd->bqkgd', p[..., span:span + lc], vc))

    out = lax.map(one_block, (jnp.arange(nb), qb))
    ox = jnp.moveaxis(out, 0, 1).reshape(b, n, hq * dh) @ w_o
    oc = None
    if ctx_out:
        qcg = qc.reshape(b, lc, hk, g, dh)
        s = jnp.einsum('bqkgd,bjkd->bkgqj', qcg, kc).astype(jnp.float32) * scale
        sink_col = jnp.broadcast_to(sink_l[None, :, :, None, None], s.shape[:-1] + (1,))
        p = jax.nn.softmax(jnp.concatenate([s, sink_col], axis=-1), axis=-1)[..., :lc].astype(vc.dtype)
        oc = jnp.einsum('bkgqj,bjkd->bqkgd', p, vc).reshape(b, lc, hq * dh) @ w_o
    return ox, oc

def setup_inputs(seed: int = 0) -> dict:
    key = jax.random.key(seed)
    keys = iter(jax.random.split(key, 32))
    D = D_MODEL

    def normal(shape, std=1.0):
        return jax.random.normal(next(keys), shape, jnp.float32) * std

    def weight(shape, fan_in, gain=1.0):
        return normal(shape, gain * fan_in ** -0.5)

    def norm_gain(shape):
        return 1.0 + normal(shape, 0.05)

    return {
        "x": normal((BATCH, SEQ, D)),
        "c": normal((BATCH, D)),
        "ctx": normal((BATCH, CTX_LEN, D)),
        "c_ctx": normal((D,)),
        "w_mod": weight((DEPTH, D, 6 * D), D, 0.5),
        "b_mod": normal((DEPTH, 6 * D), 0.02),
        "g_pre_mix": norm_gain((DEPTH, D)),
        "g_post_mix": norm_gain((DEPTH, D)),
        "g_pre_ffn": norm_gain((DEPTH, D)),
        "g_post_ffn": norm_gain((DEPTH, D)),
        "w_ffn_in": weight((DEPTH, D, 2 * D_FF), D),
        "w_ffn_out": weight((DEPTH, D_FF, D), D_FF),
        "mla_w_in": weight((N_MLA_LAYERS, D, MLA_Q_LORA + MLA_KV_LORA + MLA_ROPE), D),
        "mla_g_q": norm_gain((N_MLA_LAYERS, MLA_Q_LORA)),
        "mla_w_uq": weight((N_MLA_LAYERS, MLA_Q_LORA, MLA_HEADS * (MLA_NOPE + MLA_ROPE)), MLA_Q_LORA),
        "mla_g_kv": norm_gain((N_MLA_LAYERS, MLA_KV_LORA)),
        "mla_w_ukv": weight((N_MLA_LAYERS, MLA_KV_LORA, MLA_HEADS * (MLA_NOPE + MLA_V)), MLA_KV_LORA),
        "mla_w_o": weight((N_MLA_LAYERS, MLA_HEADS * MLA_V, D), MLA_HEADS * MLA_V),
        "na_w_qkv": weight((N_NA_LAYERS, D, 3 * NA_HEADS * NA_HEAD_DIM), D),
        "na_rpb": normal((N_NA_LAYERS, NA_HEADS, 2 * NA_WIN_ROWS - 1, 2 * NA_WIN_COLS - 1), 0.1),
        "na_w_o": weight((N_NA_LAYERS, NA_HEADS * NA_HEAD_DIM, D), NA_HEADS * NA_HEAD_DIM),
        "swa_w_qkv": weight((N_SWA_LAYERS, D, (SWA_HEADS + 2 * SWA_KV_HEADS) * SWA_HEAD_DIM), D),
        "swa_sink": normal((N_SWA_LAYERS, SWA_HEADS), 0.5),
        "swa_w_o": weight((N_SWA_LAYERS, SWA_HEADS * SWA_HEAD_DIM, D), SWA_HEADS * SWA_HEAD_DIM),
    }

def reference(x, c, ctx, c_ctx, w_mod, b_mod, g_pre_mix, g_post_mix, g_pre_ffn, g_post_ffn,
              w_ffn_in, w_ffn_out, mla_w_in, mla_g_q, mla_w_uq, mla_g_kv, mla_w_ukv, mla_w_o,
              na_w_qkv, na_rpb, na_w_o, swa_w_qkv, swa_sink, swa_w_o):
    for i in range(DEPTH):
        last = i == DEPTH - 1
        mod_x = jax.nn.silu(c) @ w_mod[i] + b_mod[i]
        mod_c = jax.nn.silu(c_ctx) @ w_mod[i] + b_mod[i]
        sh_m, sc_m, gt_m, sh_f, sc_f, gt_f = jnp.split(mod_x[:, None, :], 6, axis=-1)
        csh_m, csc_m, cgt_m, csh_f, csc_f, cgt_f = jnp.split(mod_c, 6, axis=-1)

        hx = modulate(rms_norm(x, g_pre_mix[i]), sh_m, sc_m)
        hc = modulate(rms_norm(ctx, g_pre_mix[i]), csh_m, csc_m)
        kind, j = i % N_MIXERS, i // N_MIXERS
        if kind == 0:
            ox, oc = mla_mixer(hx, hc, mla_w_in[j], mla_g_q[j], mla_w_uq[j], mla_g_kv[j],
                               mla_w_ukv[j], mla_w_o[j], not last)
        elif kind == 1:
            ox, oc = na_mixer(hx, hc, na_w_qkv[j], na_rpb[j], na_w_o[j], not last)
        else:
            ox, oc = swa_mixer(hx, hc, swa_w_qkv[j], swa_sink[j], swa_w_o[j], not last)

        x = x + gt_m * rms_norm(ox, g_post_mix[i])
        hx = modulate(rms_norm(x, g_pre_ffn[i]), sh_f, sc_f)
        x = x + gt_f * rms_norm(swiglu(hx, w_ffn_in[i], w_ffn_out[i]), g_post_ffn[i])

        if not last:
            ctx = ctx + cgt_m * rms_norm(oc, g_post_mix[i])
            hc = modulate(rms_norm(ctx, g_pre_ffn[i]), csh_f, csc_f)
            ctx = ctx + cgt_f * rms_norm(swiglu(hc, w_ffn_in[i], w_ffn_out[i]), g_post_ffn[i])
    return x


_drawn_inputs = setup_inputs


def setup_inputs(seed=0):
    import zlib

    import numpy as np

    out = dict(_drawn_inputs(seed))
    spreads = {}
    factors = {'mla_g_q': 6.902, 'na_rpb': 8.0, 'swa_sink': 24.796}
    for name, (base, spread) in spreads.items():
        noise = np.random.default_rng([zlib.crc32(name.encode()), seed]).standard_normal(out[name].shape)
        drawn = base * np.exp(spread * noise) if base else spread * noise
        out[name] = jnp.asarray(drawn.astype(out[name].dtype))
    for name, factor in factors.items():
        out[name] = (out[name] * factor).astype(out[name].dtype)
    return out
```

```python
import concourse.bass as bass
from concourse import mybir
from contextlib import ExitStack

F32 = mybir.dt.float32
F32R = mybir.dt.float32r
ALU = mybir.AluOpType
ACT = mybir.ActivationFunctionType
AX = mybir.AxisListType

D_MODEL, SEQ, CTX, DEPTH = 1024, 256, 256, 4
TOK = SEQ + CTX
DT = D_MODEL // 128
D_FF = -(-8 * D_MODEL // (3 * 256)) * 256
FT = D_FF // 128
GRID_W, EPS = 64, 1e-6
ROPE_THETA = 10000.0
NEG = -1e30
LORA, NOPE, ROPE = D_MODEL // 4, 128, 64
MLA_HEADS, HEADS, HD, KV_HEADS = D_MODEL // 128, D_MODEL // 64, 64, D_MODEL // 64 // 8
WIN_ROWS, WIN_COLS = 8, 16
GRID_ROWS = SEQ // GRID_W
BIAS_ROWS = 2 * GRID_ROWS - 1
BIAS_COLS = 2 * GRID_W - 1
MLA, NA, SWA = 0, 1, 2
KIND = [i % 3 for i in range(DEPTH)]
RAW, SPLIT, AHEAD = 3, 3, 2
MODS = 6 * D_MODEL // 2048

C_ID, C_ROT, C_COS, C_SIN, C_NAM, C_SWAM = 0, 128, 256, 512, 768, 832
C_ONE, C_PD, C_PL, C_EXP, C_FLIP, C_END = 1088, 1216, 1217, 1218, 1222, 1350


class Signal:

    def __init__(self, sem, known):
        self.sem, self.known, self.count = sem, known, 0

    def mark(self, label, by=1):
        self.count += by
        self.known[label] = self.count
        return self.sem, by

    def at(self, label):
        return self.sem, self.value(label)

    def value(self, label):
        return self.known.get(label, 1)

    def here(self, label):
        self.known[label] = self.count

    def looped(self, n):
        self.count += n


def weight_chunks(w):
    def cols(m, c0, n=128, k0=0, kt=DT):
        return m[k0 * 128:(k0 + kt) * 128, c0:c0 + n].rearrange("(k p) n -> p k n", p=128)

    out = []
    for l in range(DEPTH):
        j = l // 3
        if KIND[l] == MLA:
            w_in, w_uq, w_ukv, w_o = w["mla_w_in"][j], w["mla_w_uq"][j], w["mla_w_ukv"][j], w["mla_w_o"][j]
            for t in range(4):
                out.append((l, "lat", t, [((DT, 128, 0, 128), cols(w_in, t * 128))]))
            pe = cols(w_in, 2 * LORA, ROPE)
            out.append((l, "pe", 0, [((DT, 128, 0, 64), pe), ((DT, 128, 64, 64), pe)]))
            for t in range(4):
                head = [cols(w_uq, t * 384 + h * (NOPE + ROPE), NOPE, 0, 2) for h in range(2)]
                turn = [cols(w_uq, t * 384 + h * (NOPE + ROPE) + NOPE, ROPE, 0, 2) for h in range(2)]
                out.append((l, "uq", t, [((2, 384, 0, 128), head[0]), ((2, 384, 128, 128), head[1]),
                                         ((2, 384, 256, 64), turn[0]), ((2, 384, 320, 64), turn[1])]))
            for t in range(4):
                out.append((l, "ukv", t, [((2, 512, 0, 512), cols(w_ukv, t * 512, 512, 0, 2))]))
        elif KIND[l] == NA:
            w_qkv, w_o = w["na_w_qkv"][j], w["na_w_o"][j]
            for t in range(DT):
                out.append((l, "q", t, [((DT, 128, 0, 128), cols(w_qkv, t * 128))]))
            for t in range(DT):
                out.append((l, "k", t, [((DT, 128, 0, 128), cols(w_qkv, D_MODEL + t * 128))]))
            for half in range(2):
                for kk in range(4):
                    out.append((l, "v", half * 4 + kk, [((2, 512, 0, 512),
                                cols(w_qkv, 2 * D_MODEL + half * 512, 512, 2 * kk, 2))]))
        else:
            w_qkv, w_o = w["swa_w_qkv"][j], w["swa_w_o"][j]
            for t in range(DT):
                out.append((l, "q", t, [((DT, 128, 0, 128), cols(w_qkv, t * 128))]))
            for g in range(KV_HEADS):
                kg = cols(w_qkv, (HEADS + g) * HD, HD)
                out.append((l, "kd", g, [((DT, 128, 0, 64), kg), ((DT, 128, 64, 64), kg)]))
            out.append((l, "vs", 0, [((DT, 128, 0, 128), cols(w_qkv, (HEADS + KV_HEADS) * HD))]))
        for t in range(DT):
            out.append((l, "o", t, [((DT, 128, 0, 128), cols(w_o, t * 128))]))
        for j2 in range(FT):
            for side in range(2):
                out.append((l, "in", 2 * j2 + side, [((DT, 128, 0, 128),
                            cols(w["w_ffn_in"][l], side * D_FF + j2 * 128))]))
        for t in range(DT):
            for kg in range(3):
                kt = min(8, FT - 8 * kg)
                out.append((l, "out", 3 * t + kg, [((kt, 128, 0, 128),
                            cols(w["w_ffn_out"][l], t * 128, 128, 8 * kg, kt))]))
    return out


def trunk(nc, a, out, known):
    ctx = ExitStack()
    with ctx:
        def sb(name, shape, dt=F32):
            return ctx.enter_context(nc.sbuf_tensor(name, shape, dt))

        def sig(name):
            return Signal(ctx.enter_context(nc.semaphore(name)), known.setdefault(name, {}))

        x = sb("x", [128, DT, TOK])
        y = sb("y", [128, DT, TOK])
        modw = y[:, :, :].rearrange("p t n -> p (t n)").rearrange("p (s n) -> p s n", s=2)
        hH, hL = sb("hH", [128, DT, TOK], F32R), sb("hL", [128, DT, TOK], F32R)
        wR = sb("wR", [128, RAW, 1024])
        wH, wL = sb("wH", [128, SPLIT, 1024], F32R), sb("wL", [128, SPLIT, 1024], F32R)
        cst = sb("cst", [128, C_END])
        gT, bT, sT = sb("gT", [128, 128]), sb("bT", [128, DEPTH * 48]), sb("sT", [128, 24])
        cpad = sb("cpad", [128, DT, 32])
        modT = sb("modT", [128, 6, DT, 2])
        coefA = sb("coefA", [128, 2, DT, 2])
        coefG = sb("coefG", [128, 2, DT, 2])
        sq = sb("sq", [128, 2, TOK])
        modrow = sq[:, 1, :]
        tmp = sb("tmp", [128, 2, TOK])
        acc = sb("acc", [128, TOK])
        dia = acc
        mean, rstd = sb("mean", [128, 8]), sb("rstd", [128, 8])
        mx, ngm = sb("mx", [128, 2, 2, 2]), sb("ngm", [128, 2, 2, 2])
        esum, rsum, esnk = sb("esum", [128, 2, 2, 2]), sb("rsum", [128, 2, 2, 2]), sb("esnk", [128, 2, 2, 2])
        sink = sb("sink", [128, HEADS])
        base = nc.sbuf_base + (-nc.sbuf_base) % 32
        fence = sb("fence", [128, (FT * TOK * 2 * 4 + 64) // 4])

        def at(name, shape, kib, dt=F32):
            return nc.alloc_sbuf_tensor_at(name, shape, dt, offset=base + kib * 1024)

        aH, aL = at("aH", [128, FT, TOK], 0, F32R), at("aL", [128, FT, TOK], 44, F32R)
        q, k = at("q", [128, DT, TOK], 0), at("k", [128, DT, TOK], 16)
        v = at("v", [128, 4, D_MODEL], 32)
        P = at("P", [128, 2, 2, TOK], 48)
        PT = at("PT", [128, 2, 6, 256], 56)
        BM = at("BM", [128, 2, 2, 256], 68)
        kd = at("kd", [128, 2, TOK], 72)
        latH, latL = at("latH", [128, 4, TOK], 48, F32R), at("latL", [128, 4, TOK], 56, F32R)
        lat = at("lat", [128, 4, TOK], 64)
        qpe = at("qpe", [128, 4, TOK], 76)
        kpe = at("kpe", [128, TOK], 84)
        qpe0 = lat
        xrow = at("xrow", [128, 4, D_MODEL], 0)
        grow, brow, srow = at("grow", [128, 128], 16), at("brow", [96, 2, 128], 17), at("srow", [24, 128], 18)
        zero = at("zero", [HEADS, BIAS_ROWS * BIAS_COLS], 20)

        bank = [ctx.enter_context(nc.psum_tensor(f"bank{i}", [128, 512], F32)) for i in range(8)]
        STAT, RB1, RB2, AUX = bank[4], bank[5], bank[6], bank[7]
        table = nc.dram_tensor("bias_table", (HEADS, BIAS_ROWS * BIAS_COLS), F32, kind="Internal").ap()

        ident, rot = cst[:, C_ID:C_ID + 128], cst[:, C_ROT:C_ROT + 128]
        cos, sin = cst[:, C_COS:C_COS + 256], cst[:, C_SIN:C_SIN + 256]
        ones = cst[:, C_ONE:C_ONE + 128]
        flip = cst[:, C_FLIP:C_FLIP + 128]
        per_d, per_l, expo = cst[:, C_PD:C_PD + 1], cst[:, C_PL:C_PL + 1], cst[:, C_EXP:C_EXP + 4]

        loaded = [ctx.enter_context(nc.semaphore(f"loaded{i}")) for i in range(RAW)]
        modloaded = [sig(f"modloaded{i}") for i in range(2)]
        biasloaded = [sig(f"biasloaded{i}") for i in range(2)]
        inputs_in, rows_in, sink_in = sig("inputs_in"), sig("rows_in"), sig("sink_in")
        table_st, stored = sig("table_st"), sig("stored")
        w_hi, w_lo, w_used = [ctx.enter_context(nc.semaphore(n)) for n in ("w_hi", "w_lo", "w_used")]
        tile_done = sig("tile_done")
        pe_aux = sig("pe_aux")
        pe_s, pe_t, pe_o, pe_mod = sig("pe_s"), sig("pe_t"), sig("pe_o"), sig("pe_mod")
        a_sq, a_h, a_gate, a_exp, a_pt, a_misc = [sig(n) for n in ("a_sq", "a_h", "a_gate", "a_exp", "a_pt", "a_misc")]
        v_copy, v_x, v_h, v_norm, v_step, v_mod = [sig(n) for n in ("v_copy", "v_x", "v_h", "v_norm", "v_step", "v_mod")]
        v_soft, v_ffn = sig("v_soft"), sig("v_ffn")
        g_norm, g_x, g_h, g_soft, g_bias, g_misc = [sig(n) for n in ("g_norm", "g_x", "g_h", "g_soft", "g_bias", "g_misc")]

        chunks = weight_chunks(a)
        first = {}
        for c, (l, what, i, _) in enumerate(chunks):
            first.setdefault((l, what), c)
        load_count, per_slot = [], [0] * RAW
        for c, ch in enumerate(chunks):
            per_slot[c % RAW] += 16 * len(ch[3])
            load_count.append(per_slot[c % RAW])
        size = [sum(s[0] * s[3] for s, _ in ch[3]) for ch in chunks]

        tiles, frees = [], []

        def tile(key, *free):
            tiles.append(key)
            frees.append(free)

        for l in range(DEPTH):
            if KIND[l] == MLA:
                for t in range(4):
                    tile((l, "lat", t), (v_copy, (l, "lat", t)))
                tile((l, "pe", 0), (v_copy, (l, "pe", 0)))
                for t in range(4):
                    for part in range(3):
                        tile((l, "uq", t, part), (v_copy, (l, "uq", t, part)))
                for t in range(4):
                    for part in range(4):
                        tile((l, "ukv", t, part), (v_copy, (l, "ukv", t, part)))
            else:
                for t in range(DT):
                    tile((l, "q", t), (v_copy, (l, "q", t)))
                if KIND[l] == NA:
                    for t in range(DT):
                        tile((l, "k", t), (v_copy, (l, "k", t)))
                    for t in range(8):
                        tile((l, "v", t), (v_copy, (l, "v", t)))
                else:
                    for t in range(KV_HEADS):
                        tile((l, "kd", t), (v_copy, (l, "kd", t)))
                    tile((l, "vs", 0), (v_copy, (l, "vs", 0)))
            for t in range(DT):
                tile((l, "o", t), (v_copy, (l, "o", t)), (a_sq, (l, "o", t)))
            for j in range(2 * FT):
                tile((l, "in", j), (v_ffn, (l, "a", j // 2)))
            for t in range(DT):
                tile((l, "out", t), (v_copy, (l, "out", t)), (a_sq, (l, "out", t)))
        number = {key: g for g, key in enumerate(tiles)}
        whole_with = {}
        for c, (l, what, i, _) in enumerate(chunks):
            if what in ("lat", "pe", "q", "k", "kd", "vs", "o", "in"):
                whole_with[l, what, i] = c
            elif what == "uq":
                whole_with[l, what, i, 2] = c
            elif what == "ukv":
                whole_with[l, what, i, 3] = c
            elif what == "v" and i % 4 == 3:
                whole_with[l, what, i] = c
            elif what == "out" and i % 3 == 2:
                whole_with[l, what, i // 3] = c

        def whole(key):
            return (w_used, whole_with[key] + 1) if key in whole_with else tile_done.at(key)

        def width(l):
            return SEQ if l == DEPTH - 1 else TOK

        def spans(l):
            return [(0, 0, SEQ)] if l == DEPTH - 1 else [(0, 0, SEQ), (1, SEQ, TOK)]

        def units(l):
            nrt = 2 if l == DEPTH - 1 else 3
            return [(g * nrt + rt, g, rt) for g in range(DT) for rt in range(nrt)]

        def heads(l):
            return 1 if KIND[l] == MLA else 2

        def modparts(l):
            rounds = [(l, 1), (l, 2)] + ([(l + 1, 0)] if l < DEPTH - 1 else [])
            return [(m, r, kt) for m, r in rounds for kt in range(DT)]

        modorder = [(0, 0, kt) for kt in range(DT)] + [p for l in range(DEPTH) for p in modparts(l)]
        modindex = {p: n for n, p in enumerate(modorder)}

        block = ctx.enter_context(nc.Block())

        @block.sync
        def _(sp):
            def load_chunk(c):
                if c >= RAW:
                    sp.wait_ge(w_lo, c - RAW + 1)
                for (kt, stride, c0, n), src in chunks[c][3]:
                    dst = wR[:, c % RAW, 0:kt * stride].rearrange("p (k n) -> p k n", k=kt)[:, :, c0:c0 + n]
                    sp.dma_start(dst, src).then_inc(loaded[c % RAW], 16)

            def load_mod(part):
                m, r, kt = part
                n = modindex[part]
                if n >= 2:
                    sp.wait_ge(*pe_mod.at(modorder[n - 2]))
                sp.dma_start(modw[:, n % 2, :], a["w_mod"][m, kt * 128:(kt + 1) * 128, r * 2048:(r + 1) * 2048])\
                    .then_inc(*modloaded[n % 2].mark(part, 16))

            def load_bias(l, u, g, rt):
                prior = bias_units[bias_units.index((u, g, rt)) - 2] if bias_units.index((u, g, rt)) >= 2 else None
                if prior:
                    sp.wait_ge(*v_soft.at((l, "bias", prior[0], 1)))
                n = bias_units.index((u, g, rt))
                for hh in range(2):
                    for r in range(2):
                        start = (2 * g + hh) * BIAS_ROWS * BIAS_COLS + (GRID_ROWS - 2 - 2 * rt + r) * BIAS_COLS
                        src = bass.AP(table.tensor, start, [[1, GRID_W], [BIAS_COLS, GRID_ROWS], [1, GRID_W]])
                        dst = BM[r * 64:r * 64 + 64, n % 2, hh, :].rearrange("p (i n) -> p i n", i=GRID_ROWS)
                        sp.dma_start(dst, src).then_inc(*biasloaded[n % 2].mark((l, u, hh, r), 16))

            sp.dma_start(cst[:, :], a["consts"]).then_inc(*inputs_in.mark("consts", 16))
            sp.dma_start(srow[0:4, :], a["mla_g_q"].rearrange("l (t n) -> (l t) n", n=128)).then_inc(*inputs_in.mark(1, 16))
            sp.dma_start(srow[4:8, :], a["mla_g_kv"].rearrange("l (t n) -> (l t) n", n=128)).then_inc(*inputs_in.mark(2, 16))
            sp.dma_start(srow[8:16, :], a["c"].rearrange("l (t n) -> (l t) n", n=128)).then_inc(*inputs_in.mark(3, 16))
            sp.dma_start(srow[16:24, :], a["c_ctx"].rearrange("(t n) -> t n", n=128)).then_inc(*inputs_in.mark(4, 16))
            for i, g in enumerate(("g_pre_mix", "g_post_mix", "g_pre_ffn", "g_post_ffn")):
                sp.dma_start(grow[32 * i:32 * i + 32, :], a[g].rearrange("l (t n) -> (l t) n", n=128))\
                    .then_inc(*inputs_in.mark(5 + i, 16))
            sp.dma_start(brow[:, :, :], a["b_mod"].rearrange("(u l) (t n) -> (l t) u n", u=2, n=128))\
                .then_inc(*inputs_in.mark("vectors", 16))
            for i in range(2):
                sp.dma_start(xrow[:, i, :], a["x"][0, i * 128:i * 128 + 128, :]).then_inc(*rows_in.mark(("x", i), 16))
            for i in range(2):
                sp.dma_start(xrow[:, 2 + i, :], a["ctx"][0, i * 128:i * 128 + 128, :])\
                    .then_inc(*rows_in.mark("rows" if i else "ctx0", 16))
            for kt in range(2):
                load_mod((0, 0, kt))
            sp.dma_start(sink[:, :], a["swa_sink"][0:1, :].broadcast_to([128, HEADS]))\
                .then_inc(*sink_in.mark("sink", 16))
            sp.wait_ge(*g_misc.at("zero"))
            sp.dma_start(table, zero[:, :]).then_inc(*table_st.mark("zeros", 16))
            for kt in range(2, DT):
                load_mod((0, 0, kt))
            sp.wait_ge(*table_st.at("zeros"))
            mid = table.rearrange("h (r n) -> h r n", n=BIAS_COLS)[:, :, GRID_W - WIN_COLS:GRID_W + WIN_COLS - 1]
            sp.dma_start(mid, a["na_rpb"][0, :, WIN_ROWS - GRID_ROWS:WIN_ROWS + GRID_ROWS - 1, :])\
                .then_inc(*table_st.mark("table", 16))
            sp.wait_ge(*table_st.at("table"))
            for l in range(DEPTH):
                c0 = first[l, "q"] if KIND[l] != MLA else first[l, "lat"]
                start = c0 if l == 0 else c0 + RAW
                for c in range(start, first[l, "o"] + RAW):
                    load_chunk(c)
                parts = modparts(l)
                bias_units = [u for u in units(l) if u[2] < 2] if KIND[l] == NA else []
                for i in range(len(parts)):
                    if i == 0:
                        sp.wait_ge(*v_h.at((l, "mix", "y free")))
                    load_mod(parts[i])
                    if units(l)[i] in bias_units:
                        load_bias(l, *units(l)[i])
                for c in range(first[l, "o"] + RAW, first[l, "in"]):
                    load_chunk(c)
                c0, turns = first[l, "in"], 2 * FT // 6
                w_in = a["w_ffn_in"][l].rearrange("(k p) n -> p k n", p=128)
                with sp.Fori(0, turns) as i:
                    for b in range(6):
                        sp.wait_ge(w_lo, i * 6 + (c0 + b - RAW + 1))
                        slot = wR[:, (c0 + b) % RAW, :].rearrange("p (k n) -> p k n", k=DT)
                        src = w_in[:, :, bass.ds(i * 384 + ((b % 2) * D_FF + (b // 2) * 128), 128)]
                        sp.dma_start(slot, src).then_inc(loaded[(c0 + b) % RAW], 16)
                for c in range(c0 + 6 * turns, first[l, "out"]):
                    load_chunk(c)
                c0 = first[l, "out"]
                w_out = a["w_ffn_out"][l].rearrange("(k p) n -> p k n", p=128)
                with sp.Fori(0, DT // 2) as i:
                    for b in range(6):
                        kg = b % 3
                        kt = min(8, FT - 8 * kg)
                        sp.wait_ge(w_lo, i * 6 + (c0 + b - RAW + 1))
                        slot = wR[:, (c0 + b) % RAW, 0:kt * 128].rearrange("p (k n) -> p k n", k=kt)
                        src = w_out[:, 8 * kg:8 * kg + kt, bass.ds(i * 256 + (b // 3) * 128, 128)]
                        sp.dma_start(slot, src).then_inc(loaded[(c0 + b) % RAW], 16)
                if l < DEPTH - 1:
                    for c in range(c0 + 3 * DT, c0 + 3 * DT + RAW):
                        load_chunk(c)
            for i in range(2):
                sp.wait_ge(*v_copy.at(("out", i, 1)))
                sp.dma_start(out[0, i * 128:i * 128 + 128, :], xrow[:, i, :]).then_inc(*stored.mark(i, 16))
            sp.wait_ge(*stored.at(1))

        @block.scalar
        def _(act):
            def split_hi(c):
                if c >= len(chunks):
                    return
                act.wait_ge(loaded[c % RAW], load_count[c])
                if c >= SPLIT:
                    act.wait_ge(w_used, c - SPLIT + 1)
                act.activation(wH[:, c % SPLIT, 0:size[c]], wR[:, c % RAW, 0:size[c]], ACT.Copy).then_inc(w_hi, 1)

            def norm_squares(key, t, n):
                act.wait_ge(*v_x.at((key, t)))
                if (t, key) not in ():
                    prev = sq_reader.get(t % 2)
                    if prev:
                        act.wait_ge(*prev)
                act.activation(sq[:, t % 2, 0:n], x[:, t, 0:n], ACT.Square).then_inc(*a_sq.mark((key, t)))
                sq_reader[t % 2] = pe_aux.at((key, "stat", t))

            sq_reader = {1: pe_aux.at((0, 0, "modT"))}

            def norm_h(key, n):
                for t in range(DT):
                    act.wait_ge(*v_h.at((key, "h", t)))
                    act.activation(hH[:, t, 0:n], tmp[:, t % 2, 0:n], ACT.Copy).then_inc(*a_h.mark((key, t)))

            def chunk_phase(l, what, after=None):
                c = first[l, what]
                while c < len(chunks) and chunks[c][:2] == (l, what):
                    split_hi(c + AHEAD)
                    if after:
                        after(chunks[c][2])
                    c += 1

            act.wait_ge(*v_copy.at("small"))
            act.wait_ge(*g_misc.at("cpad"))
            for s in range(2):
                act.activation(cpad[:, :, s], sT[:, 8 + 8 * s:16 + 8 * s], ACT.Silu).then_inc(*a_misc.mark(("c", s)))
            for c in range(AHEAD):
                split_hi(c)
            for t in range(DT):
                norm_squares((0, "mix"), t, TOK)
            for l in range(DEPTH):
                N = width(l)
                norm_h((l, "mix"), TOK)
                if KIND[l] == MLA:
                    chunk_phase(l, "lat")
                    split_hi(first[l, "pe"] + AHEAD)
                    for t in range(4):
                        act.wait_ge(*v_copy.at((l, "lat", t)))
                        if t < 2:
                            if sq_reader.get(t):
                                act.wait_ge(*sq_reader[t])
                        else:
                            act.wait_ge(*pe_aux.at((l, "latstat", t - 2)))
                        act.activation(sq[:, t % 2, :], lat[:, t, :], ACT.Square).then_inc(*a_sq.mark((l, "lat", t)))
                        sq_reader[t % 2] = pe_aux.at((l, "latstat", t))
                    for t in range(4):
                        act.wait_ge(*v_h.at((l, "latn", t)))
                        act.activation(latH[:, t, :], tmp[:, t % 2, :], ACT.Copy).then_inc(*a_h.mark((l, "latn", t)))
                    chunk_phase(l, "uq")
                    chunk_phase(l, "ukv")
                elif KIND[l] == NA:
                    for what in ("q", "k", "v"):
                        chunk_phase(l, what)
                else:
                    for what in ("q", "kd", "vs"):
                        chunk_phase(l, what)

                scale = float(NOPE + ROPE) ** -0.5 if KIND[l] == MLA else float(HD) ** -0.5
                todo = units(l)
                H = heads(l)

                def exps(u, g, rt):
                    for hh in range(H):
                        act.wait_ge(*v_soft.at((l, "neg", u, hh)))
                        if u >= 2:
                            act.wait_ge(*pe_t.at((l, u - 2, hh)))
                        S = bank[(2 * (u % 2) + hh) if H == 2 else u % 2]
                        for qh in range(2 if rt == 2 else 1):
                            n = 256 if rt == 2 else 512
                            cut = slice(qh * n, qh * n + n)
                            act.activation(P[:, u % 2, hh, cut], S[:, cut], ACT.Exp, scale=scale,
                                           bias=ngm[:, u % 2, hh, qh:qh + 1],
                                           accum_out=esum[:, u % 2, hh, qh:qh + 1]).then_inc(*a_exp.mark((l, u, hh, qh)))
                        if KIND[l] == SWA:
                            nq = 2 if rt == 2 else 1
                            h = 2 * g + hh
                            act.activation(esnk[:, u % 2, hh, 0:nq], ngm[:, u % 2, hh, 0:nq], ACT.Exp,
                                           bias=sink[:, h:h + 1]).then_inc(*a_exp.mark((l, u, hh, "sink")))

                def evacuate(u, g, rt):
                    for hh in range(H):
                        act.wait_ge(*pe_t.at((l, u, hh)))
                        if g > 0 and rt == 0:
                            act.wait_ge(*pe_o.at((l, g - 1)))
                        T = bank[4 + (hh if H == 2 else u % 2)]
                        if rt < 2:
                            dst = PT[:, hh, 0:4, rt * 128:rt * 128 + 128]
                            src = T[:, :].rearrange("p (k n) -> p k n", k=4)
                        else:
                            dst = PT[:, hh, 4:6, :].rearrange("p k (q n) -> p q k n", q=2)
                            src = T[:, :].rearrange("p (q k n) -> p q k n", q=2, k=2)
                        act.activation(dst, src, ACT.Copy).then_inc(*a_pt.mark((l, u, hh)))

                def output(g):
                    act.wait_ge(*pe_o.at((l, g)))
                    act.activation(hH[:, g, 0:N], bank[6][:, 0:N], ACT.Copy).then_inc(*a_h.mark((l, "o", g)))

                last_rt = todo[-1][2]
                for n in range(len(todo) + 1):
                    if n < len(todo):
                        exps(*todo[n])
                    if n >= 1:
                        evacuate(*todo[n - 1])
                        if todo[n - 1][2] == last_rt and todo[n - 1][1] > 0:
                            output(todo[n - 1][1] - 1)
                output(DT - 1)
                sq_reader[1] = pe_aux.at(modparts(l)[-1][:2] + ("modT",))

                def squares(what):
                    def after(t):
                        act.wait_ge(*whole((l, what, t)))
                        if t >= 2:
                            act.wait_ge(*v_step.at((l, what, "acc", t - 2)))
                        elif sq_reader.get(t % 2):
                            act.wait_ge(*sq_reader[t % 2])
                        g = number[l, what, t]
                        act.wait_ge(*v_copy.at((l, what, t)))
                        act.activation(sq[:, t % 2, 0:N], bank[g % 4][:, 0:N], ACT.Square)\
                            .then_inc(*a_sq.mark((l, what, t)))
                        sq_reader[t % 2] = v_step.at((l, what, "acc", t))
                    return after

                chunk_phase(l, "o", squares("o"))
                for t in range(DT):
                    norm_squares((l, "ffn"), t, N)
                norm_h((l, "ffn"), N)

                c0, g0, turns = first[l, "in"], number[l, "in", 0], 2 * FT // 6
                a_gate.here((l, "gate0"))
                ffn0 = v_ffn.value((l, "in0"))

                def pair(c, j, dst, i):
                    for b in range(2):
                        cc = c + b + AHEAD
                        if cc < len(chunks):
                            n_in_slot = load_count[cc]
                            act.wait_ge(loaded[cc % RAW], i * 32 + n_in_slot)
                            act.wait_ge(w_used, i * 6 + (cc - SPLIT + 1))
                            act.activation(wH[:, cc % SPLIT, 0:size[cc]], wR[:, cc % RAW, 0:size[cc]], ACT.Copy)\
                                .then_inc(w_hi, 1)
                    act.wait_ge(w_used, i * 6 + (c0 + 2 * j + 1))
                    if j >= 2 or i is not ZERO:
                        act.wait_ge(v_ffn.sem, i * 6 + (ffn0 + 2 * j - 2))
                    act.activation(tmp[:, j % 2, 0:N], bank[(g0 + 2 * j) % 4][:, 0:N], ACT.Silu).then_inc(a_gate.sem, 1)
                    act.wait_ge(v_ffn.sem, i * 6 + (ffn0 + 2 * j + 1))
                    act.wait_ge(v_ffn.sem, ffn0 + 1)
                    act.activation(dst, sq[:, j % 2, 0:N], ACT.Copy).then_inc(a_gate.sem, 1)

                for j in range(FT):
                    pair(c0 + 2 * j, j, aH[:, j, 0:N], ZERO)
                a_gate.looped(2 * FT)
                sq_reader[0] = v_ffn.at((l, "lo", FT - 2))
                sq_reader[1] = v_ffn.at((l, "lo", FT - 1))

                for t in range(DT):
                    for kg in range(3):
                        split_hi(first[l, "out"] + 3 * t + kg + AHEAD)
                    squares("out")(t)
                if l < DEPTH - 1:
                    for t in range(DT):
                        norm_squares((l + 1, "mix"), t, TOK)

        @block.gpsimd
        def _(pool):
            def split_lo(c):
                if c >= len(chunks):
                    return
                pool.wait_ge(w_hi, c + 1)
                pool.tensor_tensor(wL[:, c % SPLIT, 0:size[c]], wR[:, c % RAW, 0:size[c]],
                                   wH[:, c % SPLIT, 0:size[c]].bitcast(F32), ALU.subtract).then_inc(w_lo, 1)

            def chunk_phase(l, what):
                c = first[l, what]
                while c < len(chunks) and chunks[c][:2] == (l, what):
                    split_lo(c + AHEAD)
                    c += 1

            def power(key, n=4):
                pool.wait_ge(*v_norm.at((key, "mean")))
                pool.tensor_tensor(rstd[:, 0:n], mean[:, 0:n], expo8[:, 0:n], ALU.pow).then_inc(*g_norm.mark(key))

            def norm_lo(key, n):
                for t in range(1, DT, 2):
                    pool.wait_ge(*a_h.at((key, t)))
                    pool.tensor_tensor(hL[:, t, 0:n], tmp[:, t % 2, 0:n], hH[:, t, 0:n].bitcast(F32), ALU.subtract)\
                        .then_inc(*g_h.mark((key, t)))

            def add_y(key, n):
                for t in range(1, DT, 2):
                    pool.wait_ge(*v_step.at((key, "gy", t)))
                    pool.tensor_tensor(x[:, t, 0:n], x[:, t, 0:n], y[:, t, 0:n], ALU.add).then_inc(*g_x.mark((key, t)))

            pool.memset(cpad[:, :, :], 0.0).then_inc(*g_misc.mark("cpad"))
            pool.memset(zero[:, :], 0.0).then_inc(*g_misc.mark("zero"))
            expo8 = cst[:, C_EXP:C_EXP + 4]
            for c in range(AHEAD):
                split_lo(c)
            power((0, "mix"))
            for l in range(DEPTH):
                N = width(l)
                norm_lo((l, "mix"), TOK)
                if KIND[l] == MLA:
                    chunk_phase(l, "lat")
                    chunk_phase(l, "pe")
                    power((l, "latq"))
                    power((l, "latkv"))
                    chunk_phase(l, "uq")
                    chunk_phase(l, "ukv")
                else:
                    for what in ("q", "k", "v") if KIND[l] == NA else ("q", "kd", "vs"):
                        chunk_phase(l, what)
                if heads(l) == 2:
                    todo = units(l)
                    bias_units = [w for w in todo if w[2] < 2] if KIND[l] == NA else []

                    def mask_bias(w):
                        n, (u, g, rt) = bias_units.index(w), w
                        pool.wait_ge(*biasloaded[n % 2].at((l, u, 1, 1)))
                        for hh in range(2):
                            b4 = BM[:, n % 2, hh, :].rearrange("p (i n) -> p i n", i=GRID_ROWS)
                            m4 = cst[:, C_NAM:C_NAM + 64].unsqueeze(1).broadcast_to([128, GRID_ROWS, GRID_W])
                            pool.tensor_tensor(b4, b4, m4, ALU.add).then_inc(*g_bias.mark((l, u, hh)))

                    for n, w in enumerate(todo):
                        if n == 0 and w in bias_units:
                            mask_bias(w)
                        if n + 1 < len(todo) and todo[n + 1] in bias_units:
                            mask_bias(todo[n + 1])
                        u, g, rt = w
                        for qh in range(2 if rt == 2 else 1):
                            cut = slice(0, 512) if rt < 2 else slice(qh * 256, qh * 256 + 256)
                            pool.wait_ge(*v_soft.at((l, "recip", u, 1)))
                            pool.tensor_scalar(P[:, u % 2, 1, cut], P[:, u % 2, 1, cut],
                                               rsum[:, u % 2, 1, qh:qh + 1], None, ALU.mult)\
                                .then_inc(*g_soft.mark((l, u, 1, qh)))
                chunk_phase(l, "o")
                power((l, "post", "o"))
                add_y((l, "ffn"), N)
                power((l, "ffn"))
                norm_lo((l, "ffn"), N)
                c0 = first[l, "in"]
                n_chunks = 2 * FT + 3 * DT
                turns = (n_chunks - AHEAD - 6) // 6 if l < DEPTH - 1 else (n_chunks - AHEAD - 6) // 6
                for c in range(c0 + AHEAD, c0 + n_chunks + AHEAD):
                    split_lo(c)
                power((l, "post", "out"))
                add_y((l + 1, "mix"), N)
                if l < DEPTH - 1:
                    power((l + 1, "mix"))

        @block.vector
        def _(dve):
            def diagonal(key, n, lo=0):
                dve.wait_ge(*g_norm.at(key))
                blocks = n // 128
                dve.tensor_tensor(dia[:, 0:n].rearrange("p (b m) -> p b m", b=blocks),
                                  ident.unsqueeze(1).broadcast_to([128, blocks, 128]),
                                  rstd[:, 0:blocks].unsqueeze(2).broadcast_to([128, blocks, 128]), ALU.mult)\
                    .then_inc(*v_norm.mark((key, "diag")))

            def mean_eps(key, src, n):
                dve.wait_ge(*pe_aux.at((key, "stats")))
                dve.tensor_scalar(mean[:, 0:n // 128], src[:, 0:n // 128], EPS, None, ALU.add)\
                    .then_inc(*v_norm.mark((key, "mean")))

            def residual(key, post, l, which, n):
                mean_eps(post, STAT, n)
                diagonal(post, n)
                dve.wait_ge(*pe_aux.at((post, "bcast")))
                for t in range(DT):
                    for s, t0, t1 in spans(l):
                        dve.scalar_tensor_tensor(y[:, t, t0:t1], y[:, t, t0:t1], coefG[:, which, t, s:s + 1],
                                                 RB1[:, t0:t1], ALU.mult, ALU.mult)\
                            .then_inc(*v_step.mark((key, "gy", t)))
                    if t % 2 == 0:
                        dve.wait_ge(*v_step.at((key, "gy", t)))
                        dve.tensor_tensor(x[:, t, 0:n], x[:, t, 0:n], y[:, t, 0:n], ALU.add)\
                            .then_inc(*v_x.mark((key, t)))
                    else:
                        dve.wait_ge(*g_x.at((key, t)))
                        dve.engine_nop().then_inc(*v_x.mark((key, t))) if False else \
                            dve.tensor_copy(mx[0:1, 0, 0, 0:1], cst[0:1, 0:1]).then_inc(*v_x.mark((key, t)))

            def modulate(key, which, n, streams):
                shift = 0 if which == 0 else 3
                mean_eps(key, STAT, n)
                diagonal(key, n)
                dve.wait_ge(*pe_aux.at((key, "bcast")))
                for t in range(DT):
                    if t >= 2:
                        if t % 2:
                            dve.wait_ge(*g_h.at((key, t - 2)))
                        else:
                            dve.wait_ge(*v_h.at((key, "lo", t - 2)))
                    dve.tensor_tensor(tmp[:, t % 2, 0:n], x[:, t, 0:n], RB2[:, 0:n], ALU.mult)\
                        .then_inc(*v_step.mark((key, "xr", t)))
                    dve.wait_ge(*v_step.at((key, "xr", t)))
                    for s, t0, t1 in streams:
                        dve.tensor_scalar(tmp[:, t % 2, t0:t1], tmp[:, t % 2, t0:t1], coefA[:, which, t, s:s + 1],
                                          modT[:, shift, t, s:s + 1], ALU.mult, ALU.add)\
                            .then_inc(*v_h.mark((key, "h", t)))
                    if t % 2 == 1:
                        dve.wait_ge(*a_h.at((key, t - 1)))
                        dve.tensor_tensor(hL[:, t - 1, 0:n], tmp[:, 0, 0:n], hH[:, t - 1, 0:n].bitcast(F32),
                                          ALU.subtract).then_inc(*v_h.mark((key, "lo", t - 1)))

            def coefficients(which, l):
                pre, post = (0, 1) if which == 0 else (2, 3)

                def gain(kind):
                    return gT[:, kind * 32 + l * 8:kind * 32 + l * 8 + 8].unsqueeze(2).broadcast_to([128, DT, 2])
                sc, gt = (1, 2) if which == 0 else (4, 5)
                return (sc, gain(pre)), (gt, gain(post))

            def coef_a(which, l):
                (sc, g), _ = coefficients(which, l)
                dve.scalar_tensor_tensor(coefA[:, which, :, :], modT[:, sc, :, :], 1.0, g, ALU.add, ALU.mult)\
                    .then_inc(*v_mod.mark((l, "A", which)))

            def coef_g(which, l):
                _, (gt, g) = coefficients(which, l)
                dve.tensor_tensor(coefG[:, which, :, :], modT[:, gt, :, :], g, ALU.mult)\
                    .then_inc(*v_mod.mark((l, "G", which)))

            def mod_rows(m, r):
                dve.wait_ge(*pe_mod.at((m, r, DT - 1)))
                dve.tensor_copy(modrow, AUX[:, :]).then_inc(*v_mod.mark((m, r, "rows")))

            def mod_columns(m, r):
                dve.wait_ge(*pe_aux.at((m, r, "modT")))
                src = AUX[:, :].rearrange("p (j i u) -> p i j u", j=4, i=4)[:, :, :, 0:2]
                dst = modT[:, 2 * r:2 * r + 2, :, :].rearrange("p a (b j) s -> p (a b) j s", b=2)
                b = bT[:, m * 48 + r * 16:m * 48 + r * 16 + 16].rearrange("p (i j) -> p i j", j=4)
                dve.tensor_tensor(dst, src, b.unsqueeze(3).broadcast_to([128, 4, 4, 2]), ALU.add)\
                    .then_inc(*v_mod.mark((m, r)))
                dve.wait_ge(*v_mod.at((m, r)))

            def copy_tile(dst, key, n0=0, n1=512, m=128):
                g = number[key]
                dve.wait_ge(*whole(key))
                dve.tensor_copy(dst, bank[g % 4][0:m, n0:n1]).then_inc(*v_copy.mark(key))

            def rotate(tl, key):
                dve.wait_ge(*pe_aux.at((key, "rot")))
                if rotated:
                    dve.wait_ge(*v_step.at((rotated[-1], "r3")))
                dve.tensor_tensor(tmp[:, 0, 0:256], AUX[:, 0:256], sin, ALU.mult).then_inc(*v_step.mark((key, "r1")))
                dve.tensor_tensor(tl, tl, cos, ALU.mult).then_inc(*v_step.mark((key, "r2")))
                dve.wait_ge(*v_step.at((key, "r2")))
                dve.tensor_tensor(tl, tl, tmp[:, 0, 0:256], ALU.add).then_inc(*v_step.mark((key, "r3")))
                rotated.append(key)

            rotated = []

            dve.wait_ge(*pe_aux.at("small"))
            dve.tensor_copy(gT[:, :], bank[0][:, 0:128]).then_inc(*v_copy.mark("g"))
            dve.tensor_copy(bT[:, :].rearrange("p (u n) -> p u n", u=2),
                            bank[0][:, 128:320].rearrange("p (u n) -> p u n", u=2)).then_inc(*v_copy.mark("b"))
            dve.tensor_copy(sT[:, :], bank[0][:, 320:344]).then_inc(*v_copy.mark("small"))
            for t in range(DT):
                dve.wait_ge(*pe_aux.at(("x", t)))
                dve.tensor_copy(x[:, t, :], bank[1 + t % 3][:, :]).then_inc(*v_x.mark(((0, "mix"), t)))
            mod_rows(0, 0)
            mod_columns(0, 0)
            coef_a(0, 0)
            dve.wait_ge(*v_mod.at((0, "A", 0)))

            for l in range(DEPTH):
                N = width(l)
                modulate((l, "mix"), 0, TOK, [(0, 0, SEQ), (1, SEQ, TOK)])
                v_h.here((l, "mix", "y free"))
                j = l // 3
                if KIND[l] == MLA:
                    for t in range(4):
                        copy_tile(lat[:, t, :], (l, "lat", t))
                    copy_tile(kpe[:, :], (l, "pe", 0))
                    for w, nm in enumerate(("latq", "latkv")):
                        key = (l, nm)
                        dve.wait_ge(*pe_aux.at(((l, "latkv"), "stats")))
                        if w:
                            dve.wait_ge(*g_norm.at((l, "latq")))
                        dve.tensor_scalar(mean[:, 0:4], STAT[:, 4 * w:4 * w + 4], EPS, None, ALU.add)\
                            .then_inc(*v_norm.mark((key, "mean")))
                        if w:
                            dve.wait_ge(*pe_aux.at(((l, "latq"), "bcast")))
                        diagonal(key, TOK)
                    for t in range(4):
                        nm = "latq" if t < 2 else "latkv"
                        dve.wait_ge(*pe_aux.at(((l, nm), "bcast")))
                        if t >= 2:
                            dve.wait_ge(*v_h.at((l, "latlo", t - 2)))
                        col = (0 if t < 2 else 4) + 2 * j + t % 2
                        dve.scalar_tensor_tensor(tmp[:, t % 2, :], lat[:, t, :], sT[:, col:col + 1],
                                                 (RB1 if t < 2 else RB2)[:, :], ALU.mult, ALU.mult)\
                            .then_inc(*v_h.mark((l, "latn", t)))
                        dve.wait_ge(*a_h.at((l, "latn", t)))
                        dve.tensor_tensor(latL[:, t, :], tmp[:, t % 2, :], latH[:, t, :].bitcast(F32), ALU.subtract)\
                            .then_inc(*v_h.mark((l, "latlo", t)))
                    rotated.clear()
                    dve.wait_ge(*v_h.at((l, "latlo", 3)))
                    rotate(kpe[:, 0:256], (l, "kpe"))
                    for t in range(4):
                        copy_tile(q[:, 2 * t, 0:N], (l, "uq", t, 0), 0, N)
                        copy_tile(q[:, 2 * t + 1, 0:N], (l, "uq", t, 1), 0, N)
                        copy_tile(qpe[:, t, 0:N], (l, "uq", t, 2), 0, N)
                        rotate(qpe[:, t, 0:256], (l, "qpe", t))
                    for t in range(4):
                        copy_tile(k[:, 2 * t, :], (l, "ukv", t, 0))
                        copy_tile(k[:, 2 * t + 1, :], (l, "ukv", t, 1))
                        for half in range(2):
                            key = (l, "ukv", t, 2 + half)
                            dve.wait_ge(*whole(key))
                            dve.tensor_copy(v[:, 2 * half:2 * half + 2, t * 256:t * 256 + 256],
                                            bank[number[key] % 4][:, :].rearrange("p (a n) -> p a n", a=2))\
                                .then_inc(*v_copy.mark(key))
                elif KIND[l] == NA:
                    for t in range(DT):
                        src = bank[number[l, "q", t] % 4]
                        dve.wait_ge(*whole((l, "q", t)))
                        back = bass.AP(q, t * TOK + 127, [[DT * TOK, 128], [128, 2], [-1, 128]])
                        dve.tensor_copy(back, src[:, 0:256].rearrange("p (b n) -> p b n", b=2))\
                            .then_inc(*v_copy.mark((l, "q latents", t)))
                        dve.tensor_copy(q[:, t, 256:512], src[:, 256:512]).then_inc(*v_copy.mark((l, "q", t)))
                    for t in range(DT):
                        copy_tile(k[:, t, :], (l, "k", t))
                    for t in range(8):
                        copy_tile(v[:, t % 4, (t // 4) * 512:(t // 4) * 512 + 512], (l, "v", t))
                else:
                    rotated.clear()
                    for t in range(DT):
                        copy_tile(q[:, t, :], (l, "q", t))
                        rotate(q[:, t, 0:256], (l, "q", t))
                    for t in range(KV_HEADS):
                        copy_tile(kd[:, t, :], (l, "kd", t))
                        rotate(kd[:, t, 0:256], (l, "kd", t))
                    key = (l, "vs", 0)
                    dve.wait_ge(*whole(key))
                    dve.tensor_copy(v[:, :, 0:128], bank[number[key] % 4][:, :].rearrange("p (a n) -> p a n", a=4))\
                        .then_inc(*v_copy.mark(key))

                H = heads(l)
                scale = float(NOPE + ROPE) ** -0.5 if KIND[l] == MLA else float(HD) ** -0.5
                todo = units(l)
                bias_units = [w for w in todo if w[2] < 2] if KIND[l] == NA else []

                def maxima(u, g, rt):
                    for hh in range(H):
                        S = bank[(2 * (u % 2) + hh) if H == 2 else u % 2]
                        dve.wait_ge(*pe_s.at((l, u, hh)))
                        if KIND[l] == NA and rt < 2:
                            dve.wait_ge(*g_bias.at((l, u, hh)))
                            n = bias_units.index((u, g, rt))
                            dve.scalar_tensor_tensor(S[:, 0:256], BM[:, n % 2, hh, :], 1.0 / scale, S[:, 0:256],
                                                     ALU.mult, ALU.add).then_inc(*v_soft.mark((l, "bias", u, hh)))
                            dve.wait_ge(*v_soft.at((l, "bias", u, hh)))
                        if KIND[l] == SWA and rt < 2:
                            far = S[:, 128:256] if rt == 0 else S[:, 0:128]
                            dve.tensor_tensor(far, far, cst[:, C_SWAM + rt * 128:C_SWAM + rt * 128 + 128], ALU.add)\
                                .then_inc(*v_soft.mark((l, "bias", u, hh)))
                            dve.wait_ge(*v_soft.at((l, "bias", u, hh)))
                        nq = 2 if rt == 2 else 1
                        dve.tensor_reduce(mx[:, u % 2, hh, 0:nq], S[:, :].rearrange("p (a n) -> p a n", a=nq),
                                          AX.X, ALU.max).then_inc(*v_soft.mark((l, "max", u, hh)))
                        dve.wait_ge(*v_soft.at((l, "max", u, hh)))
                        if u >= 2:
                            dve.wait_ge(*a_exp.at((l, u - 2, hh, "sink" if KIND[l] == SWA else
                                                   (1 if todo[u - 2][2] == 2 else 0))))
                        if KIND[l] == SWA:
                            h = 2 * g + hh
                            dve.tensor_scalar(mx[:, u % 2, hh, 0:nq], mx[:, u % 2, hh, 0:nq], scale,
                                              sink[:, h:h + 1], ALU.mult, ALU.max)\
                                .then_inc(*v_soft.mark((l, "smax", u, hh)))
                            dve.wait_ge(*v_soft.at((l, "smax", u, hh)))
                            dve.tensor_scalar(ngm[:, u % 2, hh, 0:nq], mx[:, u % 2, hh, 0:nq], -1.0, None, ALU.mult)\
                                .then_inc(*v_soft.mark((l, "neg", u, hh)))
                        else:
                            dve.tensor_scalar(ngm[:, u % 2, hh, 0:nq], mx[:, u % 2, hh, 0:nq], -scale, None, ALU.mult)\
                                .then_inc(*v_soft.mark((l, "neg", u, hh)))

                def divide(u, g, rt):
                    nq = 2 if rt == 2 else 1
                    for hh in range(H):
                        dve.wait_ge(*a_exp.at((l, u, hh, "sink" if KIND[l] == SWA else nq - 1)))
                        if u >= 2 and hh == 1:
                            dve.wait_ge(*g_soft.at((l, u - 2, 1, 0 if todo[u - 2][2] < 2 else 1)))
                        if KIND[l] == SWA:
                            dve.tensor_tensor(esum[:, u % 2, hh, 0:nq], esum[:, u % 2, hh, 0:nq],
                                              esnk[:, u % 2, hh, 0:nq], ALU.add).then_inc(*v_soft.mark((l, "sum", u, hh)))
                            dve.wait_ge(*v_soft.at((l, "sum", u, hh)))
                        dve.reciprocal(rsum[:, u % 2, hh, 0:nq], esum[:, u % 2, hh, 0:nq])\
                            .then_inc(*v_soft.mark((l, "recip", u, hh)))
                        if hh == 0:
                            dve.wait_ge(*v_soft.at((l, "recip", u, hh)))
                            for qh in range(nq):
                                cut = slice(0, 512) if rt < 2 else slice(qh * 256, qh * 256 + 256)
                                dve.tensor_scalar(P[:, u % 2, 0, cut], P[:, u % 2, 0, cut],
                                                  rsum[:, u % 2, 0, qh:qh + 1], None, ALU.mult)\
                                    .then_inc(*v_soft.mark((l, "p", u, 0)))

                def output(g):
                    dve.wait_ge(*a_h.at((l, "o", g)))
                    dve.tensor_tensor(hL[:, g, 0:N], bank[6][:, 0:N], hH[:, g, 0:N].bitcast(F32), ALU.subtract)\
                        .then_inc(*v_h.mark((l, "olo", g)))

                last_rt = todo[-1][2]
                parts = modparts(l)
                for n in range(len(todo) + 1):
                    ended = parts[n - 1][:2] if n >= 1 and parts[n - 1][2] == DT - 1 else None
                    if ended:
                        mod_rows(*ended)
                    if n < len(todo):
                        maxima(*todo[n])
                    if n >= 1:
                        divide(*todo[n - 1])
                    if n >= 2 and todo[n - 2][2] == last_rt and todo[n - 2][1] > 0:
                        output(todo[n - 2][1] - 1)
                    if ended:
                        mod_columns(*ended)
                output(DT - 2)
                output(DT - 1)
                coef_g(0, l)
                coef_a(1, l)
                coef_g(1, l)
                dve.wait_ge(*v_mod.at((l, "G", 1)))

                def outputs(what):
                    for t in range(DT):
                        if t == 0:
                            dve.wait_ge(*pe_mod.at(parts[-1]))
                        copy_tile(y[:, t, 0:N], (l, what, t), 0, N)
                        dve.wait_ge(*a_sq.at((l, what, t)))
                        if t == 0:
                            dve.tensor_copy(acc[:, 0:N], sq[:, 0, 0:N]).then_inc(*v_step.mark((l, what, "acc", 0)))
                        else:
                            dve.wait_ge(*v_step.at((l, what, "acc", t - 1)))
                            dve.tensor_tensor(acc[:, 0:N], acc[:, 0:N], sq[:, t % 2, 0:N], ALU.add)\
                                .then_inc(*v_step.mark((l, what, "acc", t)))

                outputs("o")
                residual((l, "ffn"), (l, "post", "o"), l, 0, N)
                modulate((l, "ffn"), 1, N, spans(l))
                if l < DEPTH - 1:
                    coef_a(0, l + 1)
                    dve.wait_ge(*v_mod.at((l + 1, "A", 0)))

                dve.wait_ge(*v_h.at(((l, "ffn"), "lo", DT - 2)))
                gate0, c0, g0 = a_gate.value((l, "gate0")), first[l, "in"], number[l, "in", 0]
                v_ffn.here((l, "in0"))
                for j2 in range(FT):
                    dve.wait_ge(w_used, c0 + 2 * j2 + 2)
                    dve.wait_ge(a_gate.sem, gate0 + 2 * j2 + 1)
                    if j2 >= 2:
                        dve.wait_ge(*v_ffn.at((l, "lo", j2 - 2)))
                    dve.tensor_tensor(sq[:, j2 % 2, 0:N], bank[(g0 + 2 * j2 + 1) % 4][:, 0:N], tmp[:, j2 % 2, 0:N],
                                      ALU.mult).then_inc(*v_ffn.mark((l, "a", j2)))
                    dve.wait_ge(a_gate.sem, gate0 + 2 * j2 + 2)
                    dve.tensor_tensor(aL[:, j2, 0:N], sq[:, j2 % 2, 0:N], aH[:, j2, 0:N].bitcast(F32), ALU.subtract)\
                        .then_inc(*v_ffn.mark((l, "lo", j2)))
                outputs("out")
                residual((l + 1, "mix"), (l, "post", "out"), l, 1, N)

            for i in range(2):
                for half in range(2):
                    dve.wait_ge(*pe_aux.at(("out", i, half)))
                    dve.tensor_copy(xrow[:, i, half * 512:half * 512 + 512], bank[2 * i + half][:, :])\
                        .then_inc(*v_copy.mark(("out", i, half)))

        @block.tensor
        def _(pe):
            mm = nc.tensor.matmul

            def three(o, wh, wl, mh, ml, start, stop):
                mm(o, wh, mh, start=start, stop=False)
                mm(o, wh, ml, start=False, stop=False)
                return mm(o, wl, mh, start=False, stop=stop)

            def free_bank(g):
                if g >= 4:
                    for s, label in frees[g - 4]:
                        pe.wait_ge(*s.at(label))

            def slot(c, kt, n):
                return [w[:, c % SPLIT, 0:kt * n].rearrange("p (k n) -> p k n", k=kt) for w in (wH, wL)]

            def stats(key, t, n, col=per_d):
                for b in range(n // 128):
                    last = mm(STAT[:, b:b + 1], sq[:, t % 2, b * 128:b * 128 + 128], col,
                              start=(t == 0 and b == 0), stop=(t == DT - 1), skip_group_check=True)
                last.then_inc(*pe_aux.mark((key, "stat", t)))
                if t == DT - 1:
                    pe_aux.known[key, "stats"] = pe_aux.count

            def broadcast(key, n, dst):
                pe.wait_ge(*v_norm.at((key, "diag")))
                mm(dst[:, 0:n], ones, dia[:, 0:n], start=True, stop=True).then_inc(*pe_aux.mark((key, "bcast")))

            def norm_x(key, n):
                for t in range(DT):
                    pe.wait_ge(*a_sq.at((key, t)))
                    stats(key, t, n)
                broadcast(key, n, RB2)

            def norm_y(l, what, n):
                key = (l, "post", what)
                pe.wait_ge(*v_step.at((l, what, "acc", DT - 1)))
                for b in range(n // 128):
                    last = mm(STAT[:, b:b + 1], acc[:, b * 128:b * 128 + 128], per_d, start=True, stop=True)
                last.then_inc(*pe_aux.mark((key, "stats")))
                broadcast(key, n, RB1)

            def h_ready(key, t):
                if t % 2:
                    pe.wait_ge(*g_h.at((key, t)))
                else:
                    pe.wait_ge(*v_h.at((key, "lo", t)))

            def column_tile(c, key, n, mH, mL, ready=None):
                g = number[key]
                free_bank(g)
                pe.wait_ge(w_lo, c + 1)
                wh, wl = slot(c, DT, 128)
                for kt in range(DT):
                    if ready:
                        ready(kt)
                    last = three(bank[g % 4][:, 0:n], wh[:, kt, :], wl[:, kt, :], mH[:, kt, 0:n], mL[:, kt, 0:n],
                                 kt == 0, kt == DT - 1)
                last.then_inc(w_used, 1)

            def mod_product(part):
                m, r, kt = part
                n = modindex[part]
                pe.wait_ge(*modloaded[n % 2].at(part))
                if kt == 0 and n >= DT:
                    pe.wait_ge(*v_mod.at(modorder[n - 1][:2]))
                for i in range(4):
                    last = mm(AUX[32 * i:32 * i + 32, :], cpad[:, kt, :], modw[:, n % 2, i * 512:i * 512 + 512],
                              start=(kt == 0), stop=(kt == DT - 1))
                last.then_inc(*pe_mod.mark(part))
                return last

            def mod_transpose(m, r):
                pe.wait_ge(*v_mod.at((m, r, "rows")))
                for i in range(4):
                    last = nc.tensor.transpose(AUX[:, i * 128:i * 128 + 128], modrow[:, i * 128:i * 128 + 128], ident)
                last.then_inc(*pe_aux.mark((m, r, "modT")))

            def rotation(tl, key, copied):
                pe.wait_ge(*v_copy.at(copied))
                if turned:
                    pe.wait_ge(*v_step.at((turned[-1], "r1")))
                mm(AUX[:, 0:256], rot, tl, start=True, stop=True).then_inc(*pe_aux.mark((key, "rot")))
                turned.append(key)

            turned = []

            pe.wait_ge(*inputs_in.at("vectors"))
            nc.tensor.transpose(bank[0][:, 0:128], grow[:, :], ident)
            for u in range(2):
                nc.tensor.transpose(bank[0][:, 128 + 96 * u:224 + 96 * u], brow[:, u, :], ident[0:96, 0:96])
            nc.tensor.transpose(bank[0][:, 320:344], srow[:, :], ident[0:24, 0:24]).then_inc(*pe_aux.mark("small"))
            pe.wait_ge(*rows_in.at("rows"))
            for t in range(DT):
                if t >= 3:
                    pe.wait_ge(*v_x.at(((0, "mix"), t - 3)))
                for i in range(4):
                    last = nc.tensor.transpose(bank[1 + t % 3][:, i * 128:i * 128 + 128],
                                               xrow[:, i, t * 128:t * 128 + 128], ident)
                last.then_inc(*pe_aux.mark(("x", t)))
            pe.wait_ge(*a_misc.at(("c", 1)))
            for t in range(DT):
                mod_product((0, 0, t))
            mod_transpose(0, 0)
            norm_x((0, "mix"), TOK)

            for l in range(DEPTH):
                N = width(l)
                key = (l, "mix")

                def done(c, ins):
                    pass

                def col_phase(what, n, mH, mL, ready=None):
                    c = first[l, what]
                    i = 0
                    while chunks[c][:2] == (l, what):
                        column_tile(c, (l, what, i), n, mH, mL, ready if i == 0 else None)
                        c += 1
                        i += 1

                ready = lambda kt: h_ready(key, kt)
                if KIND[l] == MLA:
                    col_phase("lat", TOK, hH, hL, ready)
                    col_phase("pe", TOK, hH, hL)
                    for t in range(4):
                        pe.wait_ge(*a_sq.at((l, "lat", t)))
                        for b in range(4):
                            o = STAT[:, (0 if t < 2 else 4) + b:(0 if t < 2 else 4) + b + 1]
                            last = mm(o, sq[:, t % 2, b * 128:b * 128 + 128], per_l, start=(t == 0 and b == 0),
                                      stop=(t % 2 == 1), skip_group_check=True)
                        last.then_inc(*pe_aux.mark((l, "latstat", t)))
                        if t % 2:
                            pe_aux.known[(l, "latq" if t == 1 else "latkv"), "stats"] = pe_aux.count
                    broadcast((l, "latq"), TOK, RB1)
                    broadcast((l, "latkv"), TOK, RB2)
                    turned.clear()
                    rotation(kpe[:, 0:256], (l, "kpe"), (l, "pe", 0))
                    for t in range(4):
                        c = first[l, "uq"] + t
                        wh, wl = slot(c, 2, 384)
                        pe.wait_ge(w_lo, c + 1)
                        if t == 0:
                            pe.wait_ge(*v_h.at((l, "latlo", 1)))
                        for part in range(3):
                            tk = (l, "uq", t, part)
                            g = number[tk]
                            free_bank(g)
                            for kt in range(2):
                                s = [w[:, kt, part * 128:part * 128 + 128] for w in (wh, wl)]
                                last = three(bank[g % 4][:, 0:N], s[0], s[1], latH[:, kt, 0:N], latL[:, kt, 0:N],
                                             kt == 0, kt == 1)
                            last.then_inc(*(tile_done.mark(tk) if part < 2 else (w_used, 1)))
                        if t > 0:
                            rotation(qpe[:, t - 1, 0:256], (l, "qpe", t - 1), (l, "uq", t - 1, 2))
                    for t in range(4):
                        c = first[l, "ukv"] + t
                        wh, wl = slot(c, 2, 512)
                        pe.wait_ge(w_lo, c + 1)
                        if t == 0:
                            pe.wait_ge(*v_h.at((l, "latlo", 3)))
                        for part in range(4):
                            tk = (l, "ukv", t, part)
                            g = number[tk]
                            free_bank(g)
                            if part < 2:
                                for kt in range(2):
                                    s = [w[:, kt, part * 256:part * 256 + 128] for w in (wh, wl)]
                                    last = three(bank[g % 4][:, :], s[0], s[1], latH[:, 2 + kt, :], latL[:, 2 + kt, :],
                                                 kt == 0, kt == 1)
                            else:
                                for tt in range(2):
                                    tok = 2 * (part - 2) + tt
                                    for kt in range(2):
                                        m = [w[:, kt, :].rearrange("p (h n) -> p h n", h=2)[:, :, 128:256] for w in (wh, wl)]
                                        cut = slice(tok * 128, tok * 128 + 128)
                                        last = three(bank[g % 4][:, tt * 256:tt * 256 + 256], latH[:, 2 + kt, cut],
                                                     latL[:, 2 + kt, cut], m[0], m[1], kt == 0, kt == 1)
                            last.then_inc(*(tile_done.mark(tk) if part < 3 else (w_used, 1)))
                        if t == 0:
                            rotation(qpe[:, 3, 0:256], (l, "qpe", 3), (l, "uq", 3, 2))
                elif KIND[l] == NA:
                    col_phase("q", TOK, hH, hL, ready)
                    col_phase("k", TOK, hH, hL)
                    for half in range(2):
                        for kk in range(4):
                            c = first[l, "v"] + half * 4 + kk
                            wh, wl = slot(c, 2, 512)
                            pe.wait_ge(w_lo, c + 1)
                            for tok in range(4):
                                tk = (l, "v", half * 4 + tok)
                                g = number[tk]
                                if kk == 0:
                                    free_bank(g)
                                cut = slice(tok * 128, tok * 128 + 128)
                                for k2 in range(2):
                                    kt = 2 * kk + k2
                                    last = three(bank[g % 4][:, :], hH[:, kt, cut], hL[:, kt, cut], wh[:, k2, :],
                                                 wl[:, k2, :], kt == 0, kt == DT - 1)
                                if kk == 3 and tok < 3:
                                    last.then_inc(*tile_done.mark(tk))
                            last.then_inc(w_used, 1)
                else:
                    turned.clear()
                    for t in range(DT):
                        c = first[l, "q"] + t
                        column_tile(c, (l, "q", t), TOK, hH, hL, ready if t == 0 else None)
                        if t:
                            rotation(q[:, t - 1, 0:256], (l, "q", t - 1), (l, "q", t - 1))
                    for t in range(KV_HEADS):
                        c = first[l, "kd"] + t
                        column_tile(c, (l, "kd", t), TOK, hH, hL)
                        if t == 0:
                            rotation(q[:, DT - 1, 0:256], (l, "q", DT - 1), (l, "q", DT - 1))
                        else:
                            rotation(kd[:, 0, 0:256], (l, "kd", 0), (l, "kd", 0))
                    c = first[l, "vs"]
                    tk = (l, "vs", 0)
                    g = number[tk]
                    wh, wl = slot(c, DT, 128)
                    pe.wait_ge(w_lo, c + 1)
                    free_bank(g)
                    for tok in range(4):
                        cut = slice(tok * 128, tok * 128 + 128)
                        for kt in range(DT):
                            last = three(bank[g % 4][:, cut], hH[:, kt, cut], hL[:, kt, cut], wh[:, kt, :], wl[:, kt, :],
                                         kt == 0, kt == DT - 1)
                    last.then_inc(w_used, 1)
                    rotation(kd[:, 1, 0:256], (l, "kd", 1), (l, "kd", 1))

                H = heads(l)
                todo = units(l)
                parts = modparts(l)
                last_rt = todo[-1][2]
                if KIND[l] == MLA:
                    ready_kv = [(v_copy, (l, "ukv", 3, 3)), (v_step, ((l, "qpe", 3), "r3"))]
                elif KIND[l] == NA:
                    ready_kv = [(v_copy, (l, "v", 7))]
                else:
                    ready_kv = [(v_copy, (l, "vs", 0)), (v_step, ((l, "kd", 1), "r3"))]

                def scores(u, g, rt):
                    if u == 0:
                        for s, label in ready_kv:
                            pe.wait_ge(*s.at(label))
                    for hh in range(H):
                        if u >= 2:
                            pu = todo[u - 2]
                            pe.wait_ge(*a_exp.at((l, u - 2, hh, 1 if pu[2] == 2 else 0)))
                    todo_q = [(rt * 128, 0, 512)] if rt < 2 else [(256, 0, 256), (384, 256, 512)]
                    for q0, s0, s1 in todo_q:
                        k0 = 0 if rt < 2 else 256
                        for hh in range(H):
                            S = bank[(2 * (u % 2) + hh) if H == 2 else u % 2]
                            if KIND[l] == MLA:
                                r = slice(64 * (g % 2), 64 * (g % 2) + 64)
                                mm(S[:, s0:s1], q[:, g, q0:q0 + 128], k[:, g, k0:512], start=True, stop=False)
                                last = mm(S[:, s0:s1], qpe[r, g // 2, q0:q0 + 128], kpe[r, k0:512], start=False, stop=True)
                            else:
                                r = slice(64 * hh, 64 * hh + 64)
                                keys = k[r, g, k0:512] if KIND[l] == NA else kd[r, g // 4, k0:512]
                                last = mm(S[:, s0:s1], q[r, g, q0:q0 + 128], keys, start=True, stop=True)
                            if s1 == 512:
                                last.then_inc(*pe_s.mark((l, u, hh)))

                def transposes(u, g, rt):
                    nq = 2 if rt == 2 else 1
                    for hh in range(H):
                        if hh == 0:
                            pe.wait_ge(*v_soft.at((l, "p", u, 0)))
                        else:
                            pe.wait_ge(*g_soft.at((l, u, 1, nq - 1)))
                        T = bank[4 + (hh if H == 2 else u % 2)]
                        before = u - 1 if H == 2 else u - 2
                        if before >= 0:
                            pe.wait_ge(*a_pt.at((l, before, hh)))
                        for b in range(4):
                            last = nc.tensor.transpose(T[:, b * 128:b * 128 + 128], P[:, u % 2, hh, b * 128:b * 128 + 128],
                                                       flip if KIND[l] == NA and rt < 2 else ident)
                        last.then_inc(*pe_t.mark((l, u, hh)))

                def values(g):
                    u = [w for w in todo if w[1] == g][-1][0]
                    for hh in range(H):
                        pe.wait_ge(*a_pt.at((l, u, hh)))
                    if g:
                        pe.wait_ge(*v_h.at((l, "olo", g - 1)))
                    m = 128 // H
                    for part in range(1 if N == SEQ else 2):
                        tiles_k = [(kt, kt) for kt in range(4)] if part == 0 else [(2, 4), (3, 5)]
                        for i, (kt, pt) in enumerate(tiles_k):
                            for hh in range(H):
                                if KIND[l] == SWA:
                                    vh = v[:, kt, (g // 4) * 64:(g // 4) * 64 + 64]
                                else:
                                    vh = v[:, kt, g * 128 + hh * m:g * 128 + hh * m + m]
                                last = mm(bank[6][hh * m:hh * m + m, part * 256:part * 256 + 256], vh, PT[:, hh, pt, :],
                                          start=(i == 0), stop=(i == len(tiles_k) - 1))
                    last.then_inc(*pe_o.mark((l, g)))

                for n in range(len(todo) + 1):
                    if n < len(todo):
                        scores(*todo[n])
                    if n >= 1:
                        if n >= 2 and todo[n - 2][2] == last_rt:
                            values(todo[n - 2][1])
                        transposes(*todo[n - 1])
                        if parts[n - 1][2] == DT - 1:
                            mod_transpose(*parts[n - 1][:2])
                    if n < len(todo):
                        mod_product(parts[n])
                values(DT - 1)

                def attended(kt):
                    pe.wait_ge(*v_h.at((l, "olo", kt)))
                col_phase("o", N, hH, hL, attended)
                norm_y(l, "o", N)
                norm_x((l, "ffn"), N)

                fk = (l, "ffn")
                for j in range(2 * FT):
                    c = first[l, "in"] + j
                    column_tile(c, (l, "in", j), N, hH, hL, (lambda kt: h_ready(fk, kt)) if j == 0 else None)
                for t in range(DT):
                    g = number[l, "out", t]
                    free_bank(g)
                    for kg in range(3):
                        c = first[l, "out"] + 3 * t + kg
                        kn = min(8, FT - 8 * kg)
                        wh, wl = slot(c, kn, 128)
                        pe.wait_ge(w_lo, c + 1)
                        if t == 0:
                            pe.wait_ge(*v_ffn.at((l, "lo", 8 * kg + kn - 1)))
                        for kt in range(kn):
                            kk = 8 * kg + kt
                            last = three(bank[g % 4][:, 0:N], wh[:, kt, :], wl[:, kt, :], aH[:, kk, 0:N], aL[:, kk, 0:N],
                                         kk == 0, kk == FT - 1)
                        last.then_inc(w_used, 1)
                norm_y(l, "out", N)
                if l < DEPTH - 1:
                    norm_x((l + 1, "mix"), TOK)

            for t in range(DT):
                pe.wait_ge(*v_x.at(((DEPTH, "mix"), t)))
            for i in range(2):
                for half in range(2):
                    for b in range(4):
                        last = nc.tensor.transpose(bank[2 * i + half][:, b * 128:b * 128 + 128],
                                                   x[:, 4 * half + b, i * 128:i * 128 + 128], ident)
                    last.then_inc(*pe_aux.mark(("out", i, half)))


ZERO = 0


def tables():
    import numpy as np
    c = np.zeros((128, C_END), np.float32)
    c[:, C_ID:C_ID + 128] = np.eye(128)
    rot = np.zeros((128, 128), np.float32)
    for m in range(128):
        if m % 64 < 32:
            rot[m + 32, m] = -1.0
        else:
            rot[m - 32, m] = 1.0
    c[:, C_ROT:C_ROT + 128] = rot
    t = np.arange(SEQ)
    n_freq = ROPE // 4
    inv = np.float32(ROPE_THETA) ** (-np.arange(n_freq, dtype=np.float32) / np.float32(n_freq))
    ang = np.concatenate([(t // GRID_W).astype(np.float32)[:, None] * inv,
                          (t % GRID_W).astype(np.float32)[:, None] * inv], -1)
    c[:, C_COS:C_COS + 256] = np.tile(np.cos(ang).T, (4, 1))
    c[:, C_SIN:C_SIN + 256] = np.tile(np.sin(ang).T, (4, 1))
    cols = np.arange(GRID_W)
    start = np.clip(cols - WIN_COLS // 2, 0, GRID_W - WIN_COLS)
    ok = (cols[None, :] >= start[:, None]) & (cols[None, :] < start[:, None] + WIN_COLS)
    c[:, C_NAM:C_NAM + 64] = np.tile(np.where(ok, 0.0, NEG)[::-1], (2, 1))
    i = np.arange(128)
    c[:, C_SWAM:C_SWAM + 128] = np.where(i[None, :] > i[:, None], NEG, 0.0)
    c[:, C_SWAM + 128:C_SWAM + 256] = np.where(i[None, :] < i[:, None], NEG, 0.0)
    c[:, C_ONE:C_ONE + 128] = 1.0
    c[:, C_PD] = 1.0 / D_MODEL
    c[:, C_PL] = 1.0 / LORA
    c[:, C_EXP:C_EXP + 4] = -0.5
    c[:, C_FLIP:C_FLIP + 128] = np.eye(128)[::-1]
    return c


_INS = ["x", "c", "ctx", "c_ctx", "w_mod", "b_mod", "g_pre_mix", "g_post_mix", "g_pre_ffn", "g_post_ffn",
        "w_ffn_in", "w_ffn_out", "mla_w_in", "mla_g_q", "mla_w_uq", "mla_g_kv", "mla_w_ukv", "mla_w_o",
        "na_w_qkv", "na_rpb", "na_w_o", "swa_w_qkv", "swa_sink", "swa_w_o"]


def kernel(**inputs):
    import numpy as _np
    import concourse.bacc as _bacc
    from concourse import mybir as _mybir
    from concourse.bass_utils import run_bass_kernel_spmd as _run

    arrays = {n: _np.ascontiguousarray(inputs[n]) for n in _INS}
    arrays["consts"] = tables()
    known = {}
    for tracing in range(2):
        nc = _bacc.Bacc("TRN2", target_bir_lowering=False, num_devices=1)
        args = {n: nc.dram_tensor(f"in_{n}", a.shape, _mybir.dt.from_np(a.dtype), kind="ExternalInput").ap()
                for n, a in arrays.items()}
        out = nc.dram_tensor("out_0", (1, SEQ, D_MODEL), F32, kind="ExternalOutput").ap()
        trunk(nc, args, out, known)
    r = _run(nc, [{f"in_{n}": a for n, a in arrays.items()}], core_ids=[0])
    return r.results[0]["out_0"]
```

```python
import concourse.bass as bass
from concourse import mybir
from contextlib import ExitStack

F32 = mybir.dt.float32
F32R = mybir.dt.float32r
ALU = mybir.AluOpType
ACT = mybir.ActivationFunctionType
AX = mybir.AxisListType

D_MODEL, SEQ, CTX, DEPTH = 1024, 256, 256, 4
TOK = SEQ + CTX
DT = D_MODEL // 128
D_FF = -(-8 * D_MODEL // (3 * 256)) * 256
FT = D_FF // 128
GRID_W, EPS = 64, 1e-6
ROPE_THETA = 10000.0
NEG = -1e30
LORA, NOPE, ROPE = D_MODEL // 4, 128, 64
MLA_HEADS, HEADS, HD, KV_HEADS = D_MODEL // 128, D_MODEL // 64, 64, D_MODEL // 64 // 8
WIN_ROWS, WIN_COLS = 8, 16
GRID_ROWS = SEQ // GRID_W
BIAS_ROWS = 2 * GRID_ROWS - 1
BIAS_COLS = 2 * GRID_W - 1
MLA, NA, SWA = 0, 1, 2
KIND = [i % 3 for i in range(DEPTH)]
RAW, SPLIT, AHEAD = 3, 3, 2
MODS = 6 * D_MODEL // 2048

C_ID, C_ROT, C_COS, C_SIN, C_NAM, C_SWAM = 0, 128, 256, 512, 768, 832
C_ONE, C_PD, C_PL, C_EXP, C_FLIP, C_END = 1088, 1216, 1217, 1218, 1226, 1354


class Signal:

    def __init__(self, sem, known):
        self.sem, self.known, self.count = sem, known, 0

    def mark(self, label, by=1):
        self.count += by
        self.known[label] = self.count
        return self.sem, by

    def at(self, label):
        return self.sem, self.value(label)

    def value(self, label):
        return self.known.get(label, 1)

    def here(self, label):
        self.known[label] = self.count

    def looped(self, n):
        self.count += n


def weight_chunks(w):
    def cols(m, c0, n=128, k0=0, kt=DT):
        return m[k0 * 128:(k0 + kt) * 128, c0:c0 + n].rearrange("(k p) n -> p k n", p=128)

    out = []
    for l in range(DEPTH):
        j = l // 3
        if KIND[l] == MLA:
            w_in, w_uq, w_ukv, w_o = w["mla_w_in"][j], w["mla_w_uq"][j], w["mla_w_ukv"][j], w["mla_w_o"][j]
            for t in range(4):
                out.append((l, "lat", t, [((DT, 128, 0, 128), cols(w_in, t * 128))]))
            pe = cols(w_in, 2 * LORA, ROPE)
            out.append((l, "pe", 0, [((DT, 128, 0, 64), pe), ((DT, 128, 64, 64), pe)]))
            for t in range(4):
                head = [cols(w_uq, t * 384 + h * (NOPE + ROPE), NOPE, 0, 2) for h in range(2)]
                turn = [cols(w_uq, t * 384 + h * (NOPE + ROPE) + NOPE, ROPE, 0, 2) for h in range(2)]
                out.append((l, "uq", t, [((2, 384, 0, 128), head[0]), ((2, 384, 128, 128), head[1]),
                                         ((2, 384, 256, 64), turn[0]), ((2, 384, 320, 64), turn[1])]))
            for t in range(4):
                out.append((l, "ukv", t, [((2, 512, 0, 512), cols(w_ukv, t * 512, 512, 0, 2))]))
        elif KIND[l] == NA:
            w_qkv, w_o = w["na_w_qkv"][j], w["na_w_o"][j]
            for t in range(DT):
                out.append((l, "q", t, [((DT, 128, 0, 128), cols(w_qkv, t * 128))]))
            for t in range(DT):
                out.append((l, "k", t, [((DT, 128, 0, 128), cols(w_qkv, D_MODEL + t * 128))]))
            for half in range(2):
                for kk in range(4):
                    out.append((l, "v", half * 4 + kk, [((2, 512, 0, 512),
                                cols(w_qkv, 2 * D_MODEL + half * 512, 512, 2 * kk, 2))]))
        else:
            w_qkv, w_o = w["swa_w_qkv"][j], w["swa_w_o"][j]
            for t in range(DT):
                out.append((l, "q", t, [((DT, 128, 0, 128), cols(w_qkv, t * 128))]))
            for g in range(KV_HEADS):
                kg = cols(w_qkv, (HEADS + g) * HD, HD)
                out.append((l, "kd", g, [((DT, 128, 0, 64), kg), ((DT, 128, 64, 64), kg)]))
            out.append((l, "vs", 0, [((DT, 128, 0, 128), cols(w_qkv, (HEADS + KV_HEADS) * HD))]))
        for t in range(DT):
            out.append((l, "o", t, [((DT, 128, 0, 128), cols(w_o, t * 128))]))
        for j2 in range(FT):
            for side in range(2):
                out.append((l, "in", 2 * j2 + side, [((DT, 128, 0, 128),
                            cols(w["w_ffn_in"][l], side * D_FF + j2 * 128))]))
        for t in range(DT):
            for kg in range(3):
                kt = min(8, FT - 8 * kg)
                out.append((l, "out", 3 * t + kg, [((kt, 128, 0, 128),
                            cols(w["w_ffn_out"][l], t * 128, 128, 8 * kg, kt))]))
    return out


def trunk(nc, a, out, known):
    ctx = ExitStack()
    with ctx:
        def sb(name, shape, dt=F32):
            return ctx.enter_context(nc.sbuf_tensor(name, shape, dt))

        def sig(name):
            return Signal(ctx.enter_context(nc.semaphore(name)), known.setdefault(name, {}))

        x = sb("x", [128, DT, TOK])
        y = sb("y", [128, DT, TOK])
        modw = y[:, :, :].rearrange("p t n -> p (t n)").rearrange("p (s n) -> p s n", s=2)
        hH, hL = sb("hH", [128, DT, TOK], F32R), sb("hL", [128, DT, TOK], F32R)
        wR = sb("wR", [128, RAW, 1024])
        wH, wL = sb("wH", [128, SPLIT, 1024], F32R), sb("wL", [128, SPLIT, 1024], F32R)
        cst = sb("cst", [128, C_END])
        gT, bT, sT = sb("gT", [128, 128]), sb("bT", [128, DEPTH * 48]), sb("sT", [128, 24])
        cpad = sb("cpad", [128, DT, 32])
        modT = sb("modT", [128, 6, DT, 2])
        coefA = sb("coefA", [128, 2, DT, 2])
        coefG = sb("coefG", [128, 2, DT, 2])
        sq = sb("sq", [128, 2, TOK])
        modrow = sq[:, 1, :]
        tmp = sb("tmp", [128, 2, TOK])
        acc = sb("acc", [128, TOK])
        mean, rstd = sb("mean", [128, 8]), sb("rstd", [128, 8])
        mx, ngm = sb("mx", [128, 2, 2, 2]), sb("ngm", [128, 2, 2, 2])
        esum, rsum, esnk = sb("esum", [128, 2, 2, 2]), sb("rsum", [128, 2, 2, 2]), sb("esnk", [128, 2, 2, 2])
        sink = sb("sink", [128, HEADS])
        base = nc.sbuf_base + (-nc.sbuf_base) % 32
        fence = sb("fence", [128, (FT * TOK * 2 * 4 + 64) // 4])

        def at(name, shape, kib, dt=F32):
            return nc.alloc_sbuf_tensor_at(name, shape, dt, offset=base + kib * 1024)

        aH, aL = at("aH", [128, FT, TOK], 0, F32R), at("aL", [128, FT, TOK], 44, F32R)
        q, k = at("q", [128, DT, TOK], 0), at("k", [128, DT, TOK], 16)
        v = at("v", [128, 4, D_MODEL], 32)
        P = at("P", [128, 3, 2, TOK], 48)
        PT = at("PT", [128, 2, 6, 256], 60)
        BM = at("BM", [128, 2, 2, 256], 72)
        kd = at("kd", [128, 2, TOK], 76)
        latH, latL = at("latH", [128, 4, TOK], 48, F32R), at("latL", [128, 4, TOK], 56, F32R)
        lat = at("lat", [128, 4, TOK], 64)
        qpe = at("qpe", [128, 4, TOK], 76)
        kpe = at("kpe", [128, TOK], 84)
        qpe0 = lat
        xrow = at("xrow", [128, 4, D_MODEL], 0)
        grow, brow, srow = at("grow", [128, 128], 16), at("brow", [96, 2, 128], 17), at("srow", [24, 128], 18)
        zero = at("zero", [HEADS, BIAS_ROWS * BIAS_COLS], 20)

        bank = [ctx.enter_context(nc.psum_tensor(f"bank{i}", [128, 512], F32)) for i in range(8)]
        STAT, RB1, RB2, AUX = bank[4], bank[5], bank[6], bank[7]
        table = nc.dram_tensor("bias_table", (HEADS, BIAS_ROWS * BIAS_COLS), F32, kind="Internal").ap()

        ident, rot = cst[:, C_ID:C_ID + 128], cst[:, C_ROT:C_ROT + 128]
        cos, sin = cst[:, C_COS:C_COS + 256], cst[:, C_SIN:C_SIN + 256]
        ones = cst[:, C_ONE:C_ONE + 128]
        flip = cst[:, C_FLIP:C_FLIP + 128]
        per_d, per_l, expo = cst[:, C_PD:C_PD + 1], cst[:, C_PL:C_PL + 1], cst[:, C_EXP:C_EXP + 8]

        loaded = [ctx.enter_context(nc.semaphore(f"loaded{i}")) for i in range(RAW)]
        modloaded = [sig(f"modloaded{i}") for i in range(2)]
        biasloaded = [sig(f"biasloaded{i}") for i in range(2)]
        inputs_in, rows_in, sink_in = sig("inputs_in"), sig("rows_in"), sig("sink_in")
        table_st, stored = sig("table_st"), sig("stored")
        w_hi, w_lo, w_used = [ctx.enter_context(nc.semaphore(n)) for n in ("w_hi", "w_lo", "w_used")]
        tile_done = sig("tile_done")
        pe_aux = sig("pe_aux")
        pe_s, pe_t, pe_o, pe_mod = sig("pe_s"), sig("pe_t"), sig("pe_o"), sig("pe_mod")
        a_sq, a_h, a_gate, a_exp, a_pt, a_misc = [sig(n) for n in ("a_sq", "a_h", "a_gate", "a_exp", "a_pt", "a_misc")]
        v_copy, v_x, v_h, v_norm, v_step, v_mod = [sig(n) for n in ("v_copy", "v_x", "v_h", "v_norm", "v_step", "v_mod")]
        v_soft, v_ffn = sig("v_soft"), sig("v_ffn")
        g_norm, g_x, g_h, g_soft, g_bias, g_misc = [sig(n) for n in ("g_norm", "g_x", "g_h", "g_soft", "g_bias", "g_misc")]

        chunks = weight_chunks(a)
        first = {}
        for c, (l, what, i, _) in enumerate(chunks):
            first.setdefault((l, what), c)
        load_count, per_slot = [], [0] * RAW
        for c, ch in enumerate(chunks):
            per_slot[c % RAW] += 16 * len(ch[3])
            load_count.append(per_slot[c % RAW])
        after_norm = [first[l, what] for l in range(DEPTH) for what in (("lat" if KIND[l] == MLA else "q"), "in")]
        size = [sum(s[0] * s[3] for s, _ in ch[3]) for ch in chunks]

        tiles, frees = [], []

        def tile(key, *free):
            tiles.append(key)
            frees.append(free)

        for l in range(DEPTH):
            if KIND[l] == MLA:
                for t in range(4):
                    tile((l, "lat", t), (v_copy, (l, "lat", t)))
                tile((l, "pe", 0), (v_copy, (l, "pe", 0)))
                for t in range(4):
                    for part in range(3):
                        tile((l, "uq", t, part), (v_copy, (l, "uq", t, part)))
                for t in range(4):
                    for part in range(4):
                        tile((l, "ukv", t, part), (v_copy, (l, "ukv", t, part)))
            else:
                for t in range(DT):
                    tile((l, "q", t), (v_copy, (l, "q", t)))
                if KIND[l] == NA:
                    for t in range(DT):
                        tile((l, "k", t), (v_copy, (l, "k", t)))
                    for t in range(8):
                        tile((l, "v", t), (v_copy, (l, "v", t)))
                else:
                    for t in range(KV_HEADS):
                        tile((l, "kd", t), (v_copy, (l, "kd", t)))
                    tile((l, "vs", 0), (v_copy, (l, "vs", 0)))
            for t in range(DT):
                tile((l, "o", t), (v_copy, (l, "o", t)), (a_sq, (l, "o", t)))
            for j in range(2 * FT):
                tile((l, "in", j), (v_ffn, (l, "a", j // 2)))
            for t in range(DT):
                tile((l, "out", t), (v_copy, (l, "out", t)), (a_sq, (l, "out", t)))
        number = {key: g for g, key in enumerate(tiles)}
        whole_with = {}
        for c, (l, what, i, _) in enumerate(chunks):
            if what in ("lat", "pe", "q", "k", "kd", "vs", "o", "in"):
                whole_with[l, what, i] = c
            elif what == "uq":
                whole_with[l, what, i, 2] = c
            elif what == "ukv":
                whole_with[l, what, i, 3] = c
            elif what == "v" and i % 4 == 3:
                whole_with[l, what, i] = c
            elif what == "out" and i % 3 == 2:
                whole_with[l, what, i // 3] = c

        def whole(key):
            return (w_used, whole_with[key] + 1) if key in whole_with else tile_done.at(key)

        def x_ready(key, t):
            return g_x.at((key, t)) if t % 2 and key != (0, "mix") else v_x.at((key, t))

        def width(l):
            return SEQ if l == DEPTH - 1 else TOK

        def spans(l):
            return [(0, 0, SEQ)] if l == DEPTH - 1 else [(0, 0, SEQ), (1, SEQ, TOK)]

        def units(l):
            nrt = 2 if l == DEPTH - 1 else 3
            return [(g * nrt + rt, g, rt) for g in range(DT) for rt in range(nrt)]

        def heads(l):
            return 1 if KIND[l] == MLA else 2

        def modparts(l):
            rounds = [(l, 1), (l, 2)] + ([(l + 1, 0)] if l < DEPTH - 1 else [])
            return [(m, r, kt) for m, r in rounds for kt in range(DT)]

        modorder = [(0, 0, kt) for kt in range(DT)] + [p for l in range(DEPTH) for p in modparts(l)]
        modindex = {p: n for n, p in enumerate(modorder)}

        block = ctx.enter_context(nc.Block())

        @block.sync
        def _(sp):
            def load_chunk(c):
                if c >= RAW:
                    sp.wait_ge(w_lo, c - RAW + 1)
                for (kt, stride, c0, n), src in chunks[c][3]:
                    dst = wR[:, c % RAW, 0:kt * stride].rearrange("p (k n) -> p k n", k=kt)[:, :, c0:c0 + n]
                    sp.dma_start(dst, src).then_inc(loaded[c % RAW], 16)

            def load_mod(part):
                m, r, kt = part
                n = modindex[part]
                if n >= 2:
                    sp.wait_ge(*pe_mod.at(modorder[n - 2]))
                sp.dma_start(modw[:, n % 2, :], a["w_mod"][m, kt * 128:(kt + 1) * 128, r * 2048:(r + 1) * 2048])\
                    .then_inc(*modloaded[n % 2].mark(part, 16))

            def load_bias(l, u, g, rt):
                prior = bias_units[bias_units.index((u, g, rt)) - 2] if bias_units.index((u, g, rt)) >= 2 else None
                if prior:
                    sp.wait_ge(*v_soft.at((l, "bias", prior[0], 1)))
                n = bias_units.index((u, g, rt))
                for hh in range(2):
                    for r in range(2):
                        start = (2 * g + hh) * BIAS_ROWS * BIAS_COLS + (GRID_ROWS - 2 - 2 * rt + r) * BIAS_COLS
                        src = bass.AP(table.tensor, start, [[1, GRID_W], [BIAS_COLS, GRID_ROWS], [1, GRID_W]])
                        dst = BM[r * 64:r * 64 + 64, n % 2, hh, :].rearrange("p (i n) -> p i n", i=GRID_ROWS)
                        sp.dma_start(dst, src).then_inc(*biasloaded[n % 2].mark((l, u, hh, r), 16))

            sp.dma_start(cst[:, :], a["consts"]).then_inc(*inputs_in.mark("consts", 16))
            sp.dma_start(srow[0:4, :], a["mla_g_q"].rearrange("l (t n) -> (l t) n", n=128)).then_inc(*inputs_in.mark(1, 16))
            sp.dma_start(srow[4:8, :], a["mla_g_kv"].rearrange("l (t n) -> (l t) n", n=128)).then_inc(*inputs_in.mark(2, 16))
            sp.dma_start(srow[8:16, :], a["c"].rearrange("l (t n) -> (l t) n", n=128)).then_inc(*inputs_in.mark(3, 16))
            sp.dma_start(srow[16:24, :], a["c_ctx"].rearrange("(t n) -> t n", n=128)).then_inc(*inputs_in.mark(4, 16))
            for i, g in enumerate(("g_pre_mix", "g_post_mix", "g_pre_ffn", "g_post_ffn")):
                sp.dma_start(grow[32 * i:32 * i + 32, :], a[g].rearrange("l (t n) -> (l t) n", n=128))\
                    .then_inc(*inputs_in.mark(5 + i, 16))
            sp.dma_start(brow[:, :, :], a["b_mod"].rearrange("(u l) (t n) -> (l t) u n", u=2, n=128))\
                .then_inc(*inputs_in.mark("vectors", 16))
            for i in range(2):
                sp.dma_start(xrow[:, i, :], a["x"][0, i * 128:i * 128 + 128, :]).then_inc(*rows_in.mark(("x", i), 16))
            for i in range(2):
                sp.dma_start(xrow[:, 2 + i, :], a["ctx"][0, i * 128:i * 128 + 128, :])\
                    .then_inc(*rows_in.mark("rows" if i else "ctx0", 16))
            for kt in range(2):
                load_mod((0, 0, kt))
            sp.dma_start(sink[:, :], a["swa_sink"][0:1, :].broadcast_to([128, HEADS]))\
                .then_inc(*sink_in.mark("sink", 16))
            sp.wait_ge(*g_misc.at("zero"))
            sp.dma_start(table, zero[:, :]).then_inc(*table_st.mark("zeros", 16))
            for kt in range(2, DT):
                load_mod((0, 0, kt))
            sp.wait_ge(*table_st.at("zeros"))
            mid = table.rearrange("h (r n) -> h r n", n=BIAS_COLS)[:, :, GRID_W - WIN_COLS:GRID_W + WIN_COLS - 1]
            sp.dma_start(mid, a["na_rpb"][0, :, WIN_ROWS - GRID_ROWS:WIN_ROWS + GRID_ROWS - 1, :])\
                .then_inc(*table_st.mark("table", 16))
            sp.wait_ge(*table_st.at("table"))
            for l in range(DEPTH):
                c0 = first[l, "q"] if KIND[l] != MLA else first[l, "lat"]
                start = c0 if l == 0 else c0 + RAW
                for c in range(start, first[l, "o"] + RAW):
                    load_chunk(c)
                parts = modparts(l)
                bias_units = [u for u in units(l) if u[2] < 2] if KIND[l] == NA else []
                for i in range(len(parts)):
                    if i == 0:
                        sp.wait_ge(*v_h.at(((l, "mix"), "lo", DT - 1)))
                        sp.wait_ge(*g_h.at(((l, "mix"), DT - 2)))
                    load_mod(parts[i])
                    if units(l)[i] in bias_units:
                        load_bias(l, *units(l)[i])
                for c in range(first[l, "o"] + RAW, first[l, "in"]):
                    load_chunk(c)
                c0, turns = first[l, "in"], 2 * FT // 6
                w_in = a["w_ffn_in"][l].rearrange("(k p) n -> p k n", p=128)
                with sp.Fori(0, turns) as i:
                    for b in range(6):
                        sp.wait_ge(w_lo, i * 6 + (c0 + b - RAW + 1))
                        slot = wR[:, (c0 + b) % RAW, :].rearrange("p (k n) -> p k n", k=DT)
                        src = w_in[:, :, bass.ds(i * 384 + ((b % 2) * D_FF + (b // 2) * 128), 128)]
                        sp.dma_start(slot, src).then_inc(loaded[(c0 + b) % RAW], 16)
                for c in range(c0 + 6 * turns, first[l, "out"]):
                    load_chunk(c)
                c0 = first[l, "out"]
                w_out = a["w_ffn_out"][l].rearrange("(k p) n -> p k n", p=128)
                with sp.Fori(0, DT // 2) as i:
                    for b in range(6):
                        kg = b % 3
                        kt = min(8, FT - 8 * kg)
                        sp.wait_ge(w_lo, i * 6 + (c0 + b - RAW + 1))
                        slot = wR[:, (c0 + b) % RAW, 0:kt * 128].rearrange("p (k n) -> p k n", k=kt)
                        src = w_out[:, 8 * kg:8 * kg + kt, bass.ds(i * 256 + (b // 3) * 128, 128)]
                        sp.dma_start(slot, src).then_inc(loaded[(c0 + b) % RAW], 16)
                if l < DEPTH - 1:
                    for c in range(c0 + 3 * DT, c0 + 3 * DT + RAW):
                        load_chunk(c)
            for i in range(2):
                sp.wait_ge(*v_copy.at(("out", i, 1)))
                sp.dma_start(out[0, i * 128:i * 128 + 128, :], xrow[:, i, :]).then_inc(*stored.mark(i, 16))
            sp.wait_ge(*stored.at(1))

        @block.scalar
        def _(act):
            def split_hi(c):
                if c >= len(chunks):
                    return
                act.wait_ge(loaded[c % RAW], load_count[c])
                if c >= SPLIT:
                    act.wait_ge(w_used, c - SPLIT + 1)
                act.activation(wH[:, c % SPLIT, 0:size[c]], wR[:, c % RAW, 0:size[c]], ACT.Copy).then_inc(w_hi, 1)

            def norm_squares(key, t, n):
                act.wait_ge(*x_ready(key, t))
                if t % 2 in sq_reader:
                    act.wait_ge(*sq_reader[t % 2])
                act.activation(sq[:, t % 2, 0:n], x[:, t, 0:n], ACT.Square).then_inc(*a_sq.mark((key, t)))
                sq_reader[t % 2] = pe_aux.at((key, "stat", t))

            sq_reader = {1: pe_aux.at((0, 0, "modT"))}

            def norm_h(key, which, n, streams):
                shift = 0 if which == 0 else 3
                for t in range(DT):
                    act.wait_ge(*v_h.at((key, "xr", t)))
                    for s, t0, t1 in streams:
                        act.activation(y[:, t, t0:t1], y[:, t, t0:t1], ACT.Identity, scale=coefA[:, which, t, s:s + 1],
                                       bias=modT[:, shift, t, s:s + 1]).then_inc(*a_h.mark((key, "h", t)))
                    if t % 2:
                        act.wait_ge(*a_h.at((key, "h", t)))
                        act.activation(hH[:, t, 0:n], y[:, t, 0:n], ACT.Copy).then_inc(*a_h.mark((key, t)))

            def chunk_phase(l, what, after=None):
                c = first[l, what]
                while c < len(chunks) and chunks[c][:2] == (l, what):
                    if c not in after_norm:
                        split_hi(c + AHEAD)
                    if after:
                        after(chunks[c][2])
                    c += 1

            act.wait_ge(*v_copy.at("small"))
            act.wait_ge(*g_misc.at("cpad"))
            for s in range(2):
                act.activation(cpad[:, :, s], sT[:, 8 + 8 * s:16 + 8 * s], ACT.Silu).then_inc(*a_misc.mark(("c", s)))
            for c in range(AHEAD):
                split_hi(c)
            split_hi(AHEAD)
            for t in range(DT):
                norm_squares((0, "mix"), t, TOK)
            for l in range(DEPTH):
                N = width(l)
                norm_h((l, "mix"), 0, TOK, [(0, 0, SEQ), (1, SEQ, TOK)])
                if KIND[l] == MLA:
                    chunk_phase(l, "lat")
                    split_hi(first[l, "pe"] + AHEAD)
                    for t in range(4):
                        act.wait_ge(*v_copy.at((l, "lat", t)))
                        if t < 2:
                            if sq_reader.get(t):
                                act.wait_ge(*sq_reader[t])
                        else:
                            act.wait_ge(*pe_aux.at((l, "latstat", t - 2)))
                        act.activation(sq[:, t % 2, :], lat[:, t, :], ACT.Square).then_inc(*a_sq.mark((l, "lat", t)))
                        sq_reader[t % 2] = pe_aux.at((l, "latstat", t))
                    for t in range(4):
                        act.wait_ge(*v_h.at((l, "latn", t)))
                        act.activation(latH[:, t, :], tmp[:, t % 2, :], ACT.Copy).then_inc(*a_h.mark((l, "latn", t)))
                    chunk_phase(l, "uq")
                    chunk_phase(l, "ukv")
                elif KIND[l] == NA:
                    for what in ("q", "k", "v"):
                        chunk_phase(l, what)
                else:
                    for what in ("q", "kd", "vs"):
                        chunk_phase(l, what)

                scale = float(NOPE + ROPE) ** -0.5 if KIND[l] == MLA else float(HD) ** -0.5
                todo = units(l)
                H = heads(l)

                def exps(u, g, rt):
                    for hh in range(H):
                        act.wait_ge(*v_soft.at((l, "neg", u, hh)))
                        if u >= 3:
                            act.wait_ge(*pe_t.at((l, u - 3, hh)))
                        S = bank[(2 * (u % 2) + hh) if H == 2 else u % 2]
                        for qh in range(2 if rt == 2 else 1):
                            n = 256 if rt == 2 else 512
                            cut = slice(qh * n, qh * n + n)
                            act.activation(P[:, u % 3, hh, cut], S[:, cut], ACT.Exp, scale=scale,
                                           bias=ngm[:, u % 2, hh, qh:qh + 1],
                                           accum_out=esum[:, u % 2, hh, qh:qh + 1]).then_inc(*a_exp.mark((l, u, hh, qh)))
                        if KIND[l] == SWA:
                            nq = 2 if rt == 2 else 1
                            h = 2 * g + hh
                            act.activation(esnk[:, u % 2, hh, 0:nq], ngm[:, u % 2, hh, 0:nq], ACT.Exp,
                                           bias=sink[:, h:h + 1]).then_inc(*a_exp.mark((l, u, hh, "sink")))

                def evacuate(u, g, rt):
                    for hh in range(H):
                        act.wait_ge(*pe_t.at((l, u, hh)))
                        if g > 0 and rt == 0:
                            act.wait_ge(*pe_o.at((l, g - 1)))
                        T = bank[4 + (hh if H == 2 else u % 2)]
                        if rt < 2:
                            dst = PT[:, hh, 0:4, rt * 128:rt * 128 + 128]
                            src = T[:, :].rearrange("p (k n) -> p k n", k=4)
                        else:
                            dst = PT[:, hh, 4:6, :].rearrange("p k (q n) -> p q k n", q=2)
                            src = T[:, :].rearrange("p (q k n) -> p q k n", q=2, k=2)
                        act.activation(dst, src, ACT.Copy).then_inc(*a_pt.mark((l, u, hh)))

                def output(g):
                    act.wait_ge(*pe_o.at((l, g)))
                    act.activation(hH[:, g, 0:N], bank[6][:, 0:N], ACT.Copy).then_inc(*a_h.mark((l, "o", g)))

                last_rt = todo[-1][2]
                for n in range(len(todo) + 3):
                    if n < len(todo):
                        exps(*todo[n])
                    if 0 <= n - 2 < len(todo):
                        evacuate(*todo[n - 2])
                    if n >= 3 and todo[n - 3][2] == last_rt:
                        output(todo[n - 3][1])
                sq_reader[1] = pe_aux.at(modparts(l)[-1][:2] + ("modT",))

                def squares(what):
                    def after(t):
                        act.wait_ge(*whole((l, what, t)))
                        if t >= 2:
                            act.wait_ge(*v_step.at((l, what, "acc", t - 2)))
                        elif sq_reader.get(t % 2):
                            act.wait_ge(*sq_reader[t % 2])
                        g = number[l, what, t]
                        act.wait_ge(*v_copy.at((l, what, t)))
                        act.activation(sq[:, t % 2, 0:N], bank[g % 4][:, 0:N], ACT.Square)\
                            .then_inc(*a_sq.mark((l, what, t)))
                        sq_reader[t % 2] = v_step.at((l, what, "acc", t))
                    return after

                chunk_phase(l, "o", squares("o"))
                split_hi(first[l, "in"] + AHEAD)
                for t in range(DT):
                    norm_squares((l, "ffn"), t, N)
                norm_h((l, "ffn"), 1, N, spans(l))

                c0, g0, turns = first[l, "in"], number[l, "in", 0], 2 * FT // 6
                a_gate.here((l, "gate0"))
                ffn0 = v_ffn.value((l, "in0"))

                def pair(c, j, dst, i):
                    for b in range(2):
                        cc = c + b + AHEAD
                        if cc < len(chunks) and cc - AHEAD not in after_norm:
                            n_in_slot = load_count[cc]
                            act.wait_ge(loaded[cc % RAW], i * 32 + n_in_slot)
                            act.wait_ge(w_used, i * 6 + (cc - SPLIT + 1))
                            act.activation(wH[:, cc % SPLIT, 0:size[cc]], wR[:, cc % RAW, 0:size[cc]], ACT.Copy)\
                                .then_inc(w_hi, 1)
                    act.wait_ge(w_used, i * 6 + (c0 + 2 * j + 1))
                    if j >= 2 or i is not ZERO:
                        act.wait_ge(v_ffn.sem, i * 6 + (ffn0 + 2 * j - 2))
                    act.activation(tmp[:, j % 2, 0:N], bank[(g0 + 2 * j) % 4][:, 0:N], ACT.Silu).then_inc(a_gate.sem, 1)
                    act.wait_ge(v_ffn.sem, i * 6 + (ffn0 + 2 * j + 1))
                    act.wait_ge(v_ffn.sem, ffn0 + 1)
                    act.activation(dst, sq[:, j % 2, 0:N], ACT.Copy).then_inc(a_gate.sem, 1)

                for j in range(FT):
                    pair(c0 + 2 * j, j, aH[:, j, 0:N], ZERO)
                a_gate.looped(2 * FT)
                sq_reader[0] = v_ffn.at((l, "lo", FT - 2))
                sq_reader[1] = v_ffn.at((l, "lo", FT - 1))

                for t in range(DT):
                    for kg in range(3):
                        split_hi(first[l, "out"] + 3 * t + kg + AHEAD)
                    squares("out")(t)
                if l < DEPTH - 1:
                    split_hi(first[l, "out"] + 3 * DT + AHEAD)
                    for t in range(DT):
                        norm_squares((l + 1, "mix"), t, TOK)

        @block.gpsimd
        def _(pool):
            def split_lo(c):
                if c >= len(chunks):
                    return
                pool.wait_ge(w_hi, c + 1)
                pool.tensor_tensor(wL[:, c % SPLIT, 0:size[c]], wR[:, c % RAW, 0:size[c]],
                                   wH[:, c % SPLIT, 0:size[c]].bitcast(F32), ALU.subtract).then_inc(w_lo, 1)

            def chunk_phase(l, what):
                c = first[l, what]
                while c < len(chunks) and chunks[c][:2] == (l, what):
                    if c not in after_norm:
                        split_lo(c + AHEAD)
                    c += 1

            def power(key, n=4):
                pool.wait_ge(*v_norm.at((key, "mean")))
                pool.tensor_tensor(rstd[:, 0:n], mean[:, 0:n], expo8[:, 0:n], ALU.pow).then_inc(*g_norm.mark(key))

            def norm_lo(key, n):
                for t in range(0, DT, 2):
                    pool.wait_ge(*v_h.at((key, "hi", t)))
                    pool.tensor_tensor(hL[:, t, 0:n], y[:, t, 0:n], hH[:, t, 0:n].bitcast(F32), ALU.subtract)\
                        .then_inc(*g_h.mark((key, t)))

            def add_y(key, n):
                for t in range(1, DT, 2):
                    pool.wait_ge(*v_step.at((key, "gy", t)))
                    pool.tensor_tensor(x[:, t, 0:n], x[:, t, 0:n], y[:, t, 0:n], ALU.add).then_inc(*g_x.mark((key, t)))

            pool.memset(cpad[:, :, :], 0.0).then_inc(*g_misc.mark("cpad"))
            pool.memset(zero[:, :], 0.0).then_inc(*g_misc.mark("zero"))
            expo8 = cst[:, C_EXP:C_EXP + 8]
            for c in range(AHEAD + 1):
                split_lo(c)
            power((0, "mix"))
            for l in range(DEPTH):
                N = width(l)
                norm_lo((l, "mix"), TOK)
                if KIND[l] == MLA:
                    chunk_phase(l, "lat")
                    chunk_phase(l, "pe")
                    power((l, "lat"), 8)
                    chunk_phase(l, "uq")
                    chunk_phase(l, "ukv")
                else:
                    for what in ("q", "k", "v") if KIND[l] == NA else ("q", "kd", "vs"):
                        chunk_phase(l, what)
                if heads(l) == 2:
                    todo = units(l)
                    bias_units = [w for w in todo if w[2] < 2] if KIND[l] == NA else []

                    def mask_bias(w):
                        n, (u, g, rt) = bias_units.index(w), w
                        pool.wait_ge(*biasloaded[n % 2].at((l, u, 1, 1)))
                        for hh in range(2):
                            b4 = BM[:, n % 2, hh, :].rearrange("p (i n) -> p i n", i=GRID_ROWS)
                            m4 = cst[:, C_NAM:C_NAM + 64].unsqueeze(1).broadcast_to([128, GRID_ROWS, GRID_W])
                            pool.tensor_tensor(b4, b4, m4, ALU.add).then_inc(*g_bias.mark((l, u, hh)))

                    for n, w in enumerate(todo):
                        if n == 0 and w in bias_units:
                            mask_bias(w)
                        if n + 1 < len(todo) and todo[n + 1] in bias_units:
                            mask_bias(todo[n + 1])
                        u, g, rt = w
                        for qh in range(2 if rt == 2 else 1):
                            cut = slice(0, 512) if rt < 2 else slice(qh * 256, qh * 256 + 256)
                            pool.wait_ge(*v_soft.at((l, "recip", u, 1)))
                            pool.tensor_scalar(P[:, u % 3, 1, cut], P[:, u % 3, 1, cut],
                                               rsum[:, u % 2, 1, qh:qh + 1], None, ALU.mult)\
                                .then_inc(*g_soft.mark((l, u, 1, qh)))
                chunk_phase(l, "o")
                power((l, "post", "o"))
                split_lo(first[l, "in"] + AHEAD)
                add_y((l, "ffn"), N)
                power((l, "ffn"))
                norm_lo((l, "ffn"), N)
                c0 = first[l, "in"]
                n_chunks = 2 * FT + 3 * DT
                turns = (n_chunks - AHEAD - 6) // 6 if l < DEPTH - 1 else (n_chunks - AHEAD - 6) // 6
                for c in range(c0 + AHEAD + 1, c0 + n_chunks + AHEAD):
                    split_lo(c)
                power((l, "post", "out"))
                split_lo(c0 + n_chunks + AHEAD)
                add_y((l + 1, "mix"), N)
                if l < DEPTH - 1:
                    power((l + 1, "mix"))

        @block.vector
        def _(dve):
            def mean_eps(key, src, n):
                dve.wait_ge(*pe_aux.at((key, "stats")))
                dve.tensor_scalar(mean[:, 0:n // 128], src[:, 0:n // 128], EPS, None, ALU.add)\
                    .then_inc(*v_norm.mark((key, "mean")))

            def residual(key, post, n):
                mean_eps(post, STAT, n)
                dve.wait_ge(*pe_aux.at((post, "bcast")))
                for t in range(DT):
                    dve.tensor_tensor(y[:, t, 0:n], y[:, t, 0:n], RB1[:, 0:n], ALU.mult)\
                        .then_inc(*v_step.mark((key, "gy", t)))
                    if t % 2 == 0:
                        dve.wait_ge(*v_step.at((key, "gy", t)))
                        dve.tensor_tensor(x[:, t, 0:n], x[:, t, 0:n], y[:, t, 0:n], ALU.add)\
                            .then_inc(*v_x.mark((key, t)))

            def modulate(key, n):
                mean_eps(key, STAT, n)
                dve.wait_ge(*pe_aux.at((key, "bcast")))
                for t in range(DT + 2):
                    if t < DT:
                        if t % 2:
                            dve.wait_ge(*x_ready(key, t))
                        dve.tensor_tensor(y[:, t, 0:n], x[:, t, 0:n], RB2[:, 0:n], ALU.mult)\
                            .then_inc(*v_h.mark((key, "xr", t)))
                    if t >= 2 and t % 2 == 0:
                        dve.wait_ge(*a_h.at((key, "h", t - 2)))
                        dve.tensor_copy(hH[:, t - 2, 0:n], y[:, t - 2, 0:n]).then_inc(*v_h.mark((key, "hi", t - 2)))
                    elif t >= 2:
                        dve.wait_ge(*a_h.at((key, t - 2)))
                        dve.tensor_tensor(hL[:, t - 2, 0:n], y[:, t - 2, 0:n], hH[:, t - 2, 0:n].bitcast(F32),
                                          ALU.subtract).then_inc(*v_h.mark((key, "lo", t - 2)))

            def coefficients(which, l):
                pre, post = (0, 1) if which == 0 else (2, 3)

                def gain(kind):
                    return gT[:, kind * 32 + l * 8:kind * 32 + l * 8 + 8].unsqueeze(2).broadcast_to([128, DT, 2])
                sc, gt = (1, 2) if which == 0 else (4, 5)
                return (sc, gain(pre)), (gt, gain(post))

            def coef_a(which, l):
                (sc, g), _ = coefficients(which, l)
                dve.scalar_tensor_tensor(coefA[:, which, :, :], modT[:, sc, :, :], 1.0, g, ALU.add, ALU.mult)\
                    .then_inc(*v_mod.mark((l, "A", which)))

            def coef_g(which, l):
                _, (gt, g) = coefficients(which, l)
                dve.tensor_tensor(coefG[:, which, :, :], modT[:, gt, :, :], g, ALU.mult)\
                    .then_inc(*v_mod.mark((l, "G", which)))

            def mod_rows(m, r):
                dve.wait_ge(*pe_mod.at((m, r, DT - 1)))
                dve.tensor_copy(modrow, AUX[:, :]).then_inc(*v_mod.mark((m, r, "rows")))

            def mod_columns(m, r):
                dve.wait_ge(*pe_aux.at((m, r, "modT")))
                src = AUX[:, :].rearrange("p (j i u) -> p i j u", j=4, i=4)[:, :, :, 0:2]
                dst = modT[:, 2 * r:2 * r + 2, :, :].rearrange("p a (b j) s -> p (a b) j s", b=2)
                b = bT[:, m * 48 + r * 16:m * 48 + r * 16 + 16].rearrange("p (i j) -> p i j", j=4)
                dve.tensor_tensor(dst, src, b.unsqueeze(3).broadcast_to([128, 4, 4, 2]), ALU.add)\
                    .then_inc(*v_mod.mark((m, r)))
                dve.wait_ge(*v_mod.at((m, r)))

            def copy_tile(dst, key, n0=0, n1=512, m=128):
                g = number[key]
                dve.wait_ge(*whole(key))
                dve.tensor_copy(dst, bank[g % 4][0:m, n0:n1]).then_inc(*v_copy.mark(key))

            def rotate(tl, key):
                dve.wait_ge(*pe_aux.at((key, "rot")))
                if rotated:
                    dve.wait_ge(*v_step.at((rotated[-1], "r3")))
                dve.tensor_tensor(tmp[:, 0, 0:256], AUX[:, 0:256], sin, ALU.mult).then_inc(*v_step.mark((key, "r1")))
                dve.tensor_tensor(tl, tl, cos, ALU.mult).then_inc(*v_step.mark((key, "r2")))
                dve.wait_ge(*v_step.at((key, "r2")))
                dve.tensor_tensor(tl, tl, tmp[:, 0, 0:256], ALU.add).then_inc(*v_step.mark((key, "r3")))
                rotated.append(key)

            rotated = []

            dve.wait_ge(*pe_aux.at("small"))
            dve.tensor_copy(gT[:, :], bank[0][:, 0:128]).then_inc(*v_copy.mark("g"))
            dve.tensor_copy(bT[:, :].rearrange("p (u n) -> p u n", u=2),
                            bank[0][:, 128:320].rearrange("p (u n) -> p u n", u=2)).then_inc(*v_copy.mark("b"))
            dve.tensor_copy(sT[:, :], bank[0][:, 320:344]).then_inc(*v_copy.mark("small"))
            for t in range(DT):
                dve.wait_ge(*pe_aux.at(("x", t)))
                dve.tensor_copy(x[:, t, :], bank[1 + t % 3][:, :]).then_inc(*v_x.mark(((0, "mix"), t)))
            mod_rows(0, 0)
            mod_columns(0, 0)
            coef_a(0, 0)
            dve.wait_ge(*v_mod.at((0, "A", 0)))

            for l in range(DEPTH):
                N = width(l)
                modulate((l, "mix"), TOK)
                j = l // 3
                if KIND[l] == MLA:
                    for t in range(4):
                        copy_tile(lat[:, t, :], (l, "lat", t))
                    copy_tile(kpe[:, :], (l, "pe", 0))
                    dve.wait_ge(*pe_aux.at((l, "latstat", 3)))
                    dve.tensor_scalar(mean[:, :], STAT[:, 0:8], EPS, None, ALU.add).then_inc(*v_norm.mark(((l, "lat"), "mean")))
                    for t in range(4):
                        dve.wait_ge(*pe_aux.at(((l, "lat"), "bcast", t // 2)))
                        if t >= 2:
                            dve.wait_ge(*v_h.at((l, "latlo", t - 2)))
                        col = (0 if t < 2 else 4) + 2 * j + t % 2
                        dve.scalar_tensor_tensor(tmp[:, t % 2, :], lat[:, t, :], sT[:, col:col + 1],
                                                 (RB1 if t < 2 else RB2)[:, :], ALU.mult, ALU.mult)\
                            .then_inc(*v_h.mark((l, "latn", t)))
                        dve.wait_ge(*a_h.at((l, "latn", t)))
                        dve.tensor_tensor(latL[:, t, :], tmp[:, t % 2, :], latH[:, t, :].bitcast(F32), ALU.subtract)\
                            .then_inc(*v_h.mark((l, "latlo", t)))
                    rotated.clear()
                    dve.wait_ge(*v_h.at((l, "latlo", 3)))
                    rotate(kpe[:, 0:256], (l, "kpe"))
                    for t in range(4):
                        copy_tile(q[:, 2 * t, 0:N], (l, "uq", t, 0), 0, N)
                        copy_tile(q[:, 2 * t + 1, 0:N], (l, "uq", t, 1), 0, N)
                        copy_tile(qpe[:, t, 0:N], (l, "uq", t, 2), 0, N)
                        rotate(qpe[:, t, 0:256], (l, "qpe", t))
                    for t in range(4):
                        copy_tile(k[:, 2 * t, :], (l, "ukv", t, 0))
                        copy_tile(k[:, 2 * t + 1, :], (l, "ukv", t, 1))
                        for half in range(2):
                            key = (l, "ukv", t, 2 + half)
                            dve.wait_ge(*whole(key))
                            dve.tensor_copy(v[:, 2 * half:2 * half + 2, t * 256:t * 256 + 256],
                                            bank[number[key] % 4][:, :].rearrange("p (a n) -> p a n", a=2))\
                                .then_inc(*v_copy.mark(key))
                elif KIND[l] == NA:
                    for t in range(DT):
                        src = bank[number[l, "q", t] % 4]
                        dve.wait_ge(*whole((l, "q", t)))
                        back = bass.AP(q, t * TOK + 127, [[DT * TOK, 128], [128, 2], [-1, 128]])
                        dve.tensor_copy(back, src[:, 0:256].rearrange("p (b n) -> p b n", b=2))\
                            .then_inc(*v_copy.mark((l, "q latents", t)))
                        dve.tensor_copy(q[:, t, 256:512], src[:, 256:512]).then_inc(*v_copy.mark((l, "q", t)))
                    for t in range(DT):
                        copy_tile(k[:, t, :], (l, "k", t))
                    for t in range(8):
                        copy_tile(v[:, t % 4, (t // 4) * 512:(t // 4) * 512 + 512], (l, "v", t))
                else:
                    rotated.clear()
                    for t in range(DT):
                        copy_tile(q[:, t, :], (l, "q", t))
                        rotate(q[:, t, 0:256], (l, "q", t))
                    for t in range(KV_HEADS):
                        copy_tile(kd[:, t, :], (l, "kd", t))
                        rotate(kd[:, t, 0:256], (l, "kd", t))
                    key = (l, "vs", 0)
                    dve.wait_ge(*whole(key))
                    dve.tensor_copy(v[:, :, 0:128], bank[number[key] % 4][:, :].rearrange("p (a n) -> p a n", a=4))\
                        .then_inc(*v_copy.mark(key))

                H = heads(l)
                scale = float(NOPE + ROPE) ** -0.5 if KIND[l] == MLA else float(HD) ** -0.5
                todo = units(l)
                bias_units = [w for w in todo if w[2] < 2] if KIND[l] == NA else []

                def maxima(u, g, rt):
                    for hh in range(H):
                        S = bank[(2 * (u % 2) + hh) if H == 2 else u % 2]
                        dve.wait_ge(*pe_s.at((l, u, hh)))
                        if KIND[l] == NA and rt < 2:
                            dve.wait_ge(*g_bias.at((l, u, hh)))
                            n = bias_units.index((u, g, rt))
                            dve.scalar_tensor_tensor(S[:, 0:256], BM[:, n % 2, hh, :], 1.0 / scale, S[:, 0:256],
                                                     ALU.mult, ALU.add).then_inc(*v_soft.mark((l, "bias", u, hh)))
                            dve.wait_ge(*v_soft.at((l, "bias", u, hh)))
                        if KIND[l] == SWA and rt < 2:
                            far = S[:, 128:256] if rt == 0 else S[:, 0:128]
                            dve.tensor_tensor(far, far, cst[:, C_SWAM + rt * 128:C_SWAM + rt * 128 + 128], ALU.add)\
                                .then_inc(*v_soft.mark((l, "bias", u, hh)))
                            dve.wait_ge(*v_soft.at((l, "bias", u, hh)))
                        nq = 2 if rt == 2 else 1
                        dve.tensor_reduce(mx[:, u % 2, hh, 0:nq], S[:, :].rearrange("p (a n) -> p a n", a=nq),
                                          AX.X, ALU.max).then_inc(*v_soft.mark((l, "max", u, hh)))
                        dve.wait_ge(*v_soft.at((l, "max", u, hh)))
                        if u >= 2:
                            dve.wait_ge(*a_exp.at((l, u - 2, hh, "sink" if KIND[l] == SWA else
                                                   (1 if todo[u - 2][2] == 2 else 0))))
                        if KIND[l] == SWA:
                            h = 2 * g + hh
                            dve.tensor_scalar(mx[:, u % 2, hh, 0:nq], mx[:, u % 2, hh, 0:nq], scale,
                                              sink[:, h:h + 1], ALU.mult, ALU.max)\
                                .then_inc(*v_soft.mark((l, "smax", u, hh)))
                            dve.wait_ge(*v_soft.at((l, "smax", u, hh)))
                            dve.tensor_scalar(ngm[:, u % 2, hh, 0:nq], mx[:, u % 2, hh, 0:nq], -1.0, None, ALU.mult)\
                                .then_inc(*v_soft.mark((l, "neg", u, hh)))
                        else:
                            dve.tensor_scalar(ngm[:, u % 2, hh, 0:nq], mx[:, u % 2, hh, 0:nq], -scale, None, ALU.mult)\
                                .then_inc(*v_soft.mark((l, "neg", u, hh)))

                def divide(u, g, rt):
                    nq = 2 if rt == 2 else 1
                    for hh in range(H):
                        dve.wait_ge(*a_exp.at((l, u, hh, "sink" if KIND[l] == SWA else nq - 1)))
                        if u >= 2 and hh == 1:
                            dve.wait_ge(*g_soft.at((l, u - 2, 1, 0 if todo[u - 2][2] < 2 else 1)))
                        if KIND[l] == SWA:
                            dve.tensor_tensor(esum[:, u % 2, hh, 0:nq], esum[:, u % 2, hh, 0:nq],
                                              esnk[:, u % 2, hh, 0:nq], ALU.add).then_inc(*v_soft.mark((l, "sum", u, hh)))
                            dve.wait_ge(*v_soft.at((l, "sum", u, hh)))
                        dve.reciprocal(rsum[:, u % 2, hh, 0:nq], esum[:, u % 2, hh, 0:nq])\
                            .then_inc(*v_soft.mark((l, "recip", u, hh)))
                        if hh == 0:
                            dve.wait_ge(*v_soft.at((l, "recip", u, hh)))
                            for qh in range(nq):
                                cut = slice(0, 512) if rt < 2 else slice(qh * 256, qh * 256 + 256)
                                dve.tensor_scalar(P[:, u % 3, 0, cut], P[:, u % 3, 0, cut],
                                                  rsum[:, u % 2, 0, qh:qh + 1], None, ALU.mult)\
                                    .then_inc(*v_soft.mark((l, "p", u, 0)))

                def output(g):
                    dve.wait_ge(*a_h.at((l, "o", g)))
                    dve.tensor_tensor(hL[:, g, 0:N], bank[6][:, 0:N], hH[:, g, 0:N].bitcast(F32), ALU.subtract)\
                        .then_inc(*v_h.mark((l, "olo", g)))

                last_rt = todo[-1][2]
                parts = modparts(l)
                for n in range(len(todo) + 4):
                    ended = parts[n - 1][:2] if 1 <= n <= len(todo) and parts[n - 1][2] == DT - 1 else None
                    if ended:
                        mod_rows(*ended)
                    if n < len(todo):
                        maxima(*todo[n])
                    if 1 <= n <= len(todo):
                        divide(*todo[n - 1])
                    if n >= 4 and todo[n - 4][2] == last_rt:
                        output(todo[n - 4][1])
                    if ended:
                        mod_columns(*ended)
                coef_g(0, l)
                coef_a(1, l)
                coef_g(1, l)
                dve.wait_ge(*v_mod.at((l, "G", 1)))

                def outputs(what, which):
                    for t in range(DT):
                        if t == 0:
                            dve.wait_ge(*pe_mod.at(parts[-1]))
                        dve.wait_ge(*whole((l, what, t)))
                        for s, t0, t1 in spans(l):
                            dve.tensor_scalar(y[:, t, t0:t1], bank[number[l, what, t] % 4][:, t0:t1],
                                              coefG[:, which, t, s:s + 1], None, ALU.mult)\
                                .then_inc(*v_copy.mark((l, what, t)))
                        dve.wait_ge(*a_sq.at((l, what, t)))
                        if t == 0:
                            dve.tensor_copy(acc[:, 0:N], sq[:, 0, 0:N]).then_inc(*v_step.mark((l, what, "acc", 0)))
                        else:
                            dve.wait_ge(*v_step.at((l, what, "acc", t - 1)))
                            dve.tensor_tensor(acc[:, 0:N], acc[:, 0:N], sq[:, t % 2, 0:N], ALU.add)\
                                .then_inc(*v_step.mark((l, what, "acc", t)))

                outputs("o", 0)
                residual((l, "ffn"), (l, "post", "o"), N)
                modulate((l, "ffn"), N)
                if l < DEPTH - 1:
                    coef_a(0, l + 1)
                    dve.wait_ge(*v_mod.at((l + 1, "A", 0)))

                gate0, c0, g0 = a_gate.value((l, "gate0")), first[l, "in"], number[l, "in", 0]
                v_ffn.here((l, "in0"))
                for j2 in range(FT):
                    dve.wait_ge(w_used, c0 + 2 * j2 + 2)
                    dve.wait_ge(a_gate.sem, gate0 + 2 * j2 + 1)
                    if j2 >= 2:
                        dve.wait_ge(*v_ffn.at((l, "lo", j2 - 2)))
                    dve.tensor_tensor(sq[:, j2 % 2, 0:N], bank[(g0 + 2 * j2 + 1) % 4][:, 0:N], tmp[:, j2 % 2, 0:N],
                                      ALU.mult).then_inc(*v_ffn.mark((l, "a", j2)))
                    dve.wait_ge(a_gate.sem, gate0 + 2 * j2 + 2)
                    dve.tensor_tensor(aL[:, j2, 0:N], sq[:, j2 % 2, 0:N], aH[:, j2, 0:N].bitcast(F32), ALU.subtract)\
                        .then_inc(*v_ffn.mark((l, "lo", j2)))
                outputs("out", 1)
                residual((l + 1, "mix"), (l, "post", "out"), N)

            for i in range(2):
                for half in range(2):
                    dve.wait_ge(*pe_aux.at(("out", i, half)))
                    dve.tensor_copy(xrow[:, i, half * 512:half * 512 + 512], bank[2 * i + half][:, :])\
                        .then_inc(*v_copy.mark(("out", i, half)))

        @block.tensor
        def _(pe):
            mm = nc.tensor.matmul

            def three(o, wh, wl, mh, ml, start, stop):
                mm(o, wh, mh, start=start, stop=False)
                mm(o, wh, ml, start=False, stop=False)
                return mm(o, wl, mh, start=False, stop=stop)

            def free_bank(g):
                if g >= 4:
                    for s, label in frees[g - 4]:
                        pe.wait_ge(*s.at(label))

            def slot(c, kt, n):
                return [w[:, c % SPLIT, 0:kt * n].rearrange("p (k n) -> p k n", k=kt) for w in (wH, wL)]

            def stats(key, t, n, col=per_d):
                for b in range(n // 128):
                    last = mm(STAT[:, b:b + 1], sq[:, t % 2, b * 128:b * 128 + 128], col,
                              start=(t == 0 and b == 0), stop=(t == DT - 1), skip_group_check=True)
                last.then_inc(*pe_aux.mark((key, "stat", t)))
                if t == DT - 1:
                    pe_aux.known[key, "stats"] = pe_aux.count

            def broadcast(key, n, dst, col=0, label=("bcast",)):
                pe.wait_ge(*g_norm.at(key))
                for b in range(n // 128):
                    last = mm(dst[:, b * 128:b * 128 + 128], rstd[:, col + b:col + b + 1].broadcast_to([128, 128]),
                              ident, start=True, stop=True)
                last.then_inc(*pe_aux.mark((key,) + label))

            def norm_x(key, n):
                for t in range(DT):
                    pe.wait_ge(*a_sq.at((key, t)))
                    stats(key, t, n)
                broadcast(key, n, RB2)

            def norm_y(l, what, n):
                key = (l, "post", what)
                pe.wait_ge(*v_step.at((l, what, "acc", DT - 1)))
                for b in range(n // 128):
                    last = mm(STAT[:, b:b + 1], acc[:, b * 128:b * 128 + 128], per_d, start=True, stop=True)
                last.then_inc(*pe_aux.mark((key, "stats")))
                broadcast(key, n, RB1)

            def h_ready(key, t):
                if t % 2:
                    pe.wait_ge(*v_h.at((key, "lo", t)))
                else:
                    pe.wait_ge(*g_h.at((key, t)))

            def column_tile(c, key, n, mH, mL):
                g = number[key]
                free_bank(g)
                pe.wait_ge(w_lo, c + 1)
                wh, wl = slot(c, DT, 128)
                for kt in range(DT):
                    last = three(bank[g % 4][:, 0:n], wh[:, kt, :], wl[:, kt, :], mH[:, kt, 0:n], mL[:, kt, 0:n],
                                 kt == 0, kt == DT - 1)
                last.then_inc(w_used, 1)

            def mod_product(part):
                m, r, kt = part
                n = modindex[part]
                pe.wait_ge(*modloaded[n % 2].at(part))
                if kt == 0 and n >= DT:
                    pe.wait_ge(*v_mod.at(modorder[n - 1][:2]))
                for i in range(4):
                    last = mm(AUX[32 * i:32 * i + 32, :], cpad[:, kt, :], modw[:, n % 2, i * 512:i * 512 + 512],
                              start=(kt == 0), stop=(kt == DT - 1))
                last.then_inc(*pe_mod.mark(part))
                return last

            def mod_transpose(m, r):
                pe.wait_ge(*v_mod.at((m, r, "rows")))
                for i in range(4):
                    last = nc.tensor.transpose(AUX[:, i * 128:i * 128 + 128], modrow[:, i * 128:i * 128 + 128], ident)
                last.then_inc(*pe_aux.mark((m, r, "modT")))

            def rotation(tl, key, copied):
                pe.wait_ge(*v_copy.at(copied))
                if turned:
                    pe.wait_ge(*v_step.at((turned[-1], "r1")))
                mm(AUX[:, 0:256], rot, tl, start=True, stop=True).then_inc(*pe_aux.mark((key, "rot")))
                turned.append(key)

            turned = []

            pe.wait_ge(*inputs_in.at("vectors"))
            nc.tensor.transpose(bank[0][:, 0:128], grow[:, :], ident)
            for u in range(2):
                nc.tensor.transpose(bank[0][:, 128 + 96 * u:224 + 96 * u], brow[:, u, :], ident[0:96, 0:96])
            nc.tensor.transpose(bank[0][:, 320:344], srow[:, :], ident[0:24, 0:24]).then_inc(*pe_aux.mark("small"))
            pe.wait_ge(*rows_in.at("rows"))
            for t in range(DT):
                if t >= 3:
                    pe.wait_ge(*v_x.at(((0, "mix"), t - 3)))
                for i in range(4):
                    last = nc.tensor.transpose(bank[1 + t % 3][:, i * 128:i * 128 + 128],
                                               xrow[:, i, t * 128:t * 128 + 128], ident)
                last.then_inc(*pe_aux.mark(("x", t)))
            pe.wait_ge(*a_misc.at(("c", 1)))
            for t in range(DT):
                mod_product((0, 0, t))
            mod_transpose(0, 0)
            norm_x((0, "mix"), TOK)

            for l in range(DEPTH):
                N = width(l)
                key = (l, "mix")

                def done(c, ins):
                    pass

                def first_two(what, n, ready):
                    c, g = first[l, what], number[l, what, 0]
                    for i in range(2):
                        free_bank(g + i)
                    w = [slot(c + i, DT, 128) for i in range(2)]
                    for kt in range(DT):
                        ready(kt)
                        for i in range(2):
                            if kt == 0:
                                pe.wait_ge(w_lo, c + i + 1)
                            last = three(bank[(g + i) % 4][:, 0:n], w[i][0][:, kt, :], w[i][1][:, kt, :],
                                         hH[:, kt, 0:n], hL[:, kt, 0:n], kt == 0, kt == DT - 1)
                            if kt == DT - 1:
                                last.then_inc(w_used, 1)

                def col_phase(what, n, mH, mL, i=0):
                    c = first[l, what] + i
                    while chunks[c][:2] == (l, what):
                        column_tile(c, (l, what, i), n, mH, mL)
                        c += 1
                        i += 1

                ready = lambda kt: h_ready(key, kt)
                if KIND[l] == MLA:
                    first_two("lat", TOK, ready)
                    col_phase("lat", TOK, hH, hL, 2)
                    col_phase("pe", TOK, hH, hL)
                    for t in range(4):
                        pe.wait_ge(*a_sq.at((l, "lat", t)))
                        for b in range(4):
                            o = STAT[:, (0 if t < 2 else 4) + b:(0 if t < 2 else 4) + b + 1]
                            last = mm(o, sq[:, t % 2, b * 128:b * 128 + 128], per_l, start=(t == 0 and b == 0),
                                      stop=(t % 2 == 1), skip_group_check=True)
                        last.then_inc(*pe_aux.mark((l, "latstat", t)))
                    for w in range(2):
                        broadcast((l, "lat"), TOK, (RB1, RB2)[w], 4 * w, ("bcast", w))
                    turned.clear()
                    rotation(kpe[:, 0:256], (l, "kpe"), (l, "pe", 0))
                    for t in range(4):
                        c = first[l, "uq"] + t
                        wh, wl = slot(c, 2, 384)
                        pe.wait_ge(w_lo, c + 1)
                        if t == 0:
                            pe.wait_ge(*v_h.at((l, "latlo", 1)))
                        for part in range(3):
                            tk = (l, "uq", t, part)
                            g = number[tk]
                            free_bank(g)
                            for kt in range(2):
                                s = [w[:, kt, part * 128:part * 128 + 128] for w in (wh, wl)]
                                last = three(bank[g % 4][:, 0:N], s[0], s[1], latH[:, kt, 0:N], latL[:, kt, 0:N],
                                             kt == 0, kt == 1)
                            last.then_inc(*(tile_done.mark(tk) if part < 2 else (w_used, 1)))
                        if t > 0:
                            rotation(qpe[:, t - 1, 0:256], (l, "qpe", t - 1), (l, "uq", t - 1, 2))
                    for t in range(4):
                        c = first[l, "ukv"] + t
                        wh, wl = slot(c, 2, 512)
                        pe.wait_ge(w_lo, c + 1)
                        if t == 0:
                            pe.wait_ge(*v_h.at((l, "latlo", 3)))
                        for part in range(4):
                            tk = (l, "ukv", t, part)
                            g = number[tk]
                            free_bank(g)
                            if part < 2:
                                for kt in range(2):
                                    s = [w[:, kt, part * 256:part * 256 + 128] for w in (wh, wl)]
                                    last = three(bank[g % 4][:, :], s[0], s[1], latH[:, 2 + kt, :], latL[:, 2 + kt, :],
                                                 kt == 0, kt == 1)
                            else:
                                for tt in range(2):
                                    tok = 2 * (part - 2) + tt
                                    for kt in range(2):
                                        m = [w[:, kt, :].rearrange("p (h n) -> p h n", h=2)[:, :, 128:256] for w in (wh, wl)]
                                        cut = slice(tok * 128, tok * 128 + 128)
                                        last = three(bank[g % 4][:, tt * 256:tt * 256 + 256], latH[:, 2 + kt, cut],
                                                     latL[:, 2 + kt, cut], m[0], m[1], kt == 0, kt == 1)
                            last.then_inc(*(tile_done.mark(tk) if part < 3 else (w_used, 1)))
                        if t == 0:
                            rotation(qpe[:, 3, 0:256], (l, "qpe", 3), (l, "uq", 3, 2))
                elif KIND[l] == NA:
                    first_two("q", TOK, ready)
                    col_phase("q", TOK, hH, hL, 2)
                    col_phase("k", TOK, hH, hL)
                    for half in range(2):
                        for kk in range(4):
                            c = first[l, "v"] + half * 4 + kk
                            wh, wl = slot(c, 2, 512)
                            pe.wait_ge(w_lo, c + 1)
                            for tok in range(4):
                                tk = (l, "v", half * 4 + tok)
                                g = number[tk]
                                if kk == 0:
                                    free_bank(g)
                                cut = slice(tok * 128, tok * 128 + 128)
                                for k2 in range(2):
                                    kt = 2 * kk + k2
                                    last = three(bank[g % 4][:, :], hH[:, kt, cut], hL[:, kt, cut], wh[:, k2, :],
                                                 wl[:, k2, :], kt == 0, kt == DT - 1)
                                if kk == 3 and tok < 3:
                                    last.then_inc(*tile_done.mark(tk))
                            last.then_inc(w_used, 1)
                else:
                    turned.clear()
                    first_two("q", TOK, ready)
                    for t in range(1, DT):
                        c = first[l, "q"] + t
                        if t > 1:
                            column_tile(c, (l, "q", t), TOK, hH, hL)
                        if t:
                            rotation(q[:, t - 1, 0:256], (l, "q", t - 1), (l, "q", t - 1))
                    for t in range(KV_HEADS):
                        c = first[l, "kd"] + t
                        column_tile(c, (l, "kd", t), TOK, hH, hL)
                        if t == 0:
                            rotation(q[:, DT - 1, 0:256], (l, "q", DT - 1), (l, "q", DT - 1))
                        else:
                            rotation(kd[:, 0, 0:256], (l, "kd", 0), (l, "kd", 0))
                    c = first[l, "vs"]
                    tk = (l, "vs", 0)
                    g = number[tk]
                    wh, wl = slot(c, DT, 128)
                    pe.wait_ge(w_lo, c + 1)
                    free_bank(g)
                    for tok in range(4):
                        cut = slice(tok * 128, tok * 128 + 128)
                        for kt in range(DT):
                            last = three(bank[g % 4][:, cut], hH[:, kt, cut], hL[:, kt, cut], wh[:, kt, :], wl[:, kt, :],
                                         kt == 0, kt == DT - 1)
                    last.then_inc(w_used, 1)
                    rotation(kd[:, 1, 0:256], (l, "kd", 1), (l, "kd", 1))

                H = heads(l)
                todo = units(l)
                parts = modparts(l)
                last_rt = todo[-1][2]
                if KIND[l] == MLA:
                    ready_kv = [(v_copy, (l, "ukv", 3, 3)), (v_step, ((l, "qpe", 3), "r3"))]
                elif KIND[l] == NA:
                    ready_kv = [(v_copy, (l, "v", 7))]
                else:
                    ready_kv = [(v_copy, (l, "vs", 0)), (v_step, ((l, "kd", 1), "r3"))]

                def scores(u, g, rt):
                    if u == 0:
                        for s, label in ready_kv:
                            pe.wait_ge(*s.at(label))
                    for hh in range(H):
                        if u >= 2:
                            pu = todo[u - 2]
                            pe.wait_ge(*a_exp.at((l, u - 2, hh, 1 if pu[2] == 2 else 0)))
                    todo_q = [(rt * 128, 0, 512)] if rt < 2 else [(256, 0, 256), (384, 256, 512)]
                    for q0, s0, s1 in todo_q:
                        k0 = 0 if rt < 2 else 256
                        for hh in range(H):
                            S = bank[(2 * (u % 2) + hh) if H == 2 else u % 2]
                            if KIND[l] == MLA:
                                r = slice(64 * (g % 2), 64 * (g % 2) + 64)
                                mm(S[:, s0:s1], q[:, g, q0:q0 + 128], k[:, g, k0:512], start=True, stop=False)
                                last = mm(S[:, s0:s1], qpe[r, g // 2, q0:q0 + 128], kpe[r, k0:512], start=False, stop=True)
                            else:
                                r = slice(64 * hh, 64 * hh + 64)
                                keys = k[r, g, k0:512] if KIND[l] == NA else kd[r, g // 4, k0:512]
                                last = mm(S[:, s0:s1], q[r, g, q0:q0 + 128], keys, start=True, stop=True)
                            if s1 == 512:
                                last.then_inc(*pe_s.mark((l, u, hh)))

                def transposes(u, g, rt):
                    nq = 2 if rt == 2 else 1
                    for hh in range(H):
                        if hh == 0:
                            pe.wait_ge(*v_soft.at((l, "p", u, 0)))
                        else:
                            pe.wait_ge(*g_soft.at((l, u, 1, nq - 1)))
                        T = bank[4 + (hh if H == 2 else u % 2)]
                        before = u - 1 if H == 2 else u - 2
                        if before >= 0:
                            pe.wait_ge(*a_pt.at((l, before, hh)))
                        for b in range(4):
                            last = nc.tensor.transpose(T[:, b * 128:b * 128 + 128], P[:, u % 3, hh, b * 128:b * 128 + 128],
                                                       flip if KIND[l] == NA and rt < 2 else ident)
                        last.then_inc(*pe_t.mark((l, u, hh)))

                def values(g):
                    u = [w for w in todo if w[1] == g][-1][0]
                    for hh in range(H):
                        pe.wait_ge(*a_pt.at((l, u, hh)))
                    if g:
                        pe.wait_ge(*v_h.at((l, "olo", g - 1)))
                    m = 128 // H
                    for part in range(1 if N == SEQ else 2):
                        tiles_k = [(kt, kt) for kt in range(4)] if part == 0 else [(2, 4), (3, 5)]
                        for i, (kt, pt) in enumerate(tiles_k):
                            for hh in range(H):
                                if KIND[l] == SWA:
                                    vh = v[:, kt, (g // 4) * 64:(g // 4) * 64 + 64]
                                else:
                                    vh = v[:, kt, g * 128 + hh * m:g * 128 + hh * m + m]
                                last = mm(bank[6][hh * m:hh * m + m, part * 256:part * 256 + 256], vh, PT[:, hh, pt, :],
                                          start=(i == 0), stop=(i == len(tiles_k) - 1))
                    last.then_inc(*pe_o.mark((l, g)))

                for n in range(len(todo) + 3):
                    if n < len(todo):
                        scores(*todo[n])
                    if n >= 3 and todo[n - 3][2] == last_rt:
                        values(todo[n - 3][1])
                    if 0 <= n - 2 < len(todo):
                        transposes(*todo[n - 2])
                    if 1 <= n <= len(todo) and parts[n - 1][2] == DT - 1:
                        mod_transpose(*parts[n - 1][:2])
                    if n < len(todo):
                        mod_product(parts[n])

                pe.wait_ge(*v_h.at((l, "olo", DT - 1)))
                col_phase("o", N, hH, hL)
                norm_y(l, "o", N)
                norm_x((l, "ffn"), N)

                fk = (l, "ffn")
                first_two("in", N, lambda kt: h_ready(fk, kt))
                for j in range(2, 2 * FT):
                    column_tile(first[l, "in"] + j, (l, "in", j), N, hH, hL)
                for t in range(DT):
                    g = number[l, "out", t]
                    free_bank(g)
                    for kg in range(3):
                        c = first[l, "out"] + 3 * t + kg
                        kn = min(8, FT - 8 * kg)
                        wh, wl = slot(c, kn, 128)
                        pe.wait_ge(w_lo, c + 1)
                        if t == 0:
                            pe.wait_ge(*v_ffn.at((l, "lo", 8 * kg + kn - 1)))
                        for kt in range(kn):
                            kk = 8 * kg + kt
                            last = three(bank[g % 4][:, 0:N], wh[:, kt, :], wl[:, kt, :], aH[:, kk, 0:N], aL[:, kk, 0:N],
                                         kk == 0, kk == FT - 1)
                        last.then_inc(w_used, 1)
                norm_y(l, "out", N)
                if l < DEPTH - 1:
                    norm_x((l + 1, "mix"), TOK)

            for t in range(DT):
                pe.wait_ge(*x_ready((DEPTH, "mix"), t))
            for i in range(2):
                for half in range(2):
                    for b in range(4):
                        last = nc.tensor.transpose(bank[2 * i + half][:, b * 128:b * 128 + 128],
                                                   x[:, 4 * half + b, i * 128:i * 128 + 128], ident)
                    last.then_inc(*pe_aux.mark(("out", i, half)))


ZERO = 0


def tables():
    import numpy as np
    c = np.zeros((128, C_END), np.float32)
    c[:, C_ID:C_ID + 128] = np.eye(128)
    rot = np.zeros((128, 128), np.float32)
    for m in range(128):
        if m % 64 < 32:
            rot[m + 32, m] = -1.0
        else:
            rot[m - 32, m] = 1.0
    c[:, C_ROT:C_ROT + 128] = rot
    t = np.arange(SEQ)
    n_freq = ROPE // 4
    inv = np.float32(ROPE_THETA) ** (-np.arange(n_freq, dtype=np.float32) / np.float32(n_freq))
    ang = np.concatenate([(t // GRID_W).astype(np.float32)[:, None] * inv,
                          (t % GRID_W).astype(np.float32)[:, None] * inv], -1)
    c[:, C_COS:C_COS + 256] = np.tile(np.cos(ang).T, (4, 1))
    c[:, C_SIN:C_SIN + 256] = np.tile(np.sin(ang).T, (4, 1))
    cols = np.arange(GRID_W)
    start = np.clip(cols - WIN_COLS // 2, 0, GRID_W - WIN_COLS)
    ok = (cols[None, :] >= start[:, None]) & (cols[None, :] < start[:, None] + WIN_COLS)
    c[:, C_NAM:C_NAM + 64] = np.tile(np.where(ok, 0.0, NEG)[::-1], (2, 1))
    i = np.arange(128)
    c[:, C_SWAM:C_SWAM + 128] = np.where(i[None, :] > i[:, None], NEG, 0.0)
    c[:, C_SWAM + 128:C_SWAM + 256] = np.where(i[None, :] < i[:, None], NEG, 0.0)
    c[:, C_ONE:C_ONE + 128] = 1.0
    c[:, C_PD] = 1.0 / D_MODEL
    c[:, C_PL] = 1.0 / LORA
    c[:, C_EXP:C_EXP + 8] = -0.5
    c[:, C_FLIP:C_FLIP + 128] = np.eye(128)[::-1]
    return c


_INS = ["x", "c", "ctx", "c_ctx", "w_mod", "b_mod", "g_pre_mix", "g_post_mix", "g_pre_ffn", "g_post_ffn",
        "w_ffn_in", "w_ffn_out", "mla_w_in", "mla_g_q", "mla_w_uq", "mla_g_kv", "mla_w_ukv", "mla_w_o",
        "na_w_qkv", "na_rpb", "na_w_o", "swa_w_qkv", "swa_sink", "swa_w_o"]


def kernel(**inputs):
    import numpy as _np
    import concourse.bacc as _bacc
    from concourse import mybir as _mybir
    from concourse.bass_utils import run_bass_kernel_spmd as _run

    arrays = {n: _np.ascontiguousarray(inputs[n]) for n in _INS}
    arrays["consts"] = tables()
    known = {}
    for tracing in range(2):
        nc = _bacc.Bacc("TRN2", target_bir_lowering=False, num_devices=1)
        args = {n: nc.dram_tensor(f"in_{n}", a.shape, _mybir.dt.from_np(a.dtype), kind="ExternalInput").ap()
                for n, a in arrays.items()}
        out = nc.dram_tensor("out_0", (1, SEQ, D_MODEL), F32, kind="ExternalOutput").ap()
        trunk(nc, args, out, known)
    r = _run(nc, [{f"in_{n}": a for n, a in arrays.items()}], core_ids=[0])
    return r.results[0]["out_0"]
```

```python
import concourse.bass as bass
from concourse import mybir
from contextlib import ExitStack

F32 = mybir.dt.float32
F32R = mybir.dt.float32r
ALU = mybir.AluOpType
ACT = mybir.ActivationFunctionType
AX = mybir.AxisListType

D_MODEL, SEQ, CTX, DEPTH = 1024, 256, 256, 4
TOK = SEQ + CTX
DT = D_MODEL // 128
D_FF = -(-8 * D_MODEL // (3 * 256)) * 256
FT = D_FF // 128
GRID_W, EPS = 64, 1e-6
ROPE_THETA = 10000.0
NEG = -1e30
LORA, NOPE, ROPE = D_MODEL // 4, 128, 64
MLA_HEADS, HEADS, HD, KV_HEADS = D_MODEL // 128, D_MODEL // 64, 64, D_MODEL // 64 // 8
WIN_ROWS, WIN_COLS = 8, 16
GRID_ROWS = SEQ // GRID_W
BIAS_ROWS = 2 * GRID_ROWS - 1
BIAS_COLS = 2 * GRID_W - 1
MLA, NA, SWA = 0, 1, 2
YY, XX, XG, GG = 0, 1, 2, 3
KIND = [i % 3 for i in range(DEPTH)]
RAW, SPLIT, AHEAD = 3, 3, 2
LO_V, ADD_V = (1, 3, 5, 7), (0, 2, 4, 6)
LAG = 3
PROBS = LAG + 1
LEAD = 4
PAIRS = 6
TURNS = (FT - 2) // PAIRS
PEELED = FT - TURNS * PAIRS
MODS = 6 * D_MODEL // 2048

C_ID, C_ROT, C_COS, C_SIN, C_NAM, C_SWAM = 0, 128, 256, 512, 768, 832
C_PD, C_PL, C_EXP, C_FLIP, C_END = 1088, 1089, 1090, 1098, 1226


class Signal:

    def __init__(self, sem, known):
        self.sem, self.known, self.count = sem, known, 0

    def mark(self, label, by=1):
        self.count += by
        self.known[label] = self.count
        return self.sem, by

    def at(self, label):
        return self.sem, self.value(label)

    def value(self, label):
        return self.known.get(label, 1)

    def paced(self, i, label, step):
        first, later = self.value(label), self.value(label[:-1] + (label[-1] + step,))
        return self.sem, i * (later - first) + first

    def repeated(self, start, turns, step):
        body = self.count - start
        for label, count in list(self.known.items()):
            if start < count <= self.count:
                for i in range(1, turns):
                    self.known[label[:-1] + (label[-1] + i * step,)] = count + i * body
        self.count = start + turns * body


def weight_chunks(w):
    def cols(m, c0, n=128, k0=0, kt=DT):
        return m[k0 * 128:(k0 + kt) * 128, c0:c0 + n].rearrange("(k p) n -> p k n", p=128)

    out = []
    for l in range(DEPTH):
        j = l // 3
        if KIND[l] == MLA:
            w_in, w_uq, w_ukv, w_o = w["mla_w_in"][j], w["mla_w_uq"][j], w["mla_w_ukv"][j], w["mla_w_o"][j]
            for t in range(4):
                out.append((l, "lat", t, [((DT, 128, 0, 128), cols(w_in, t * 128))]))
            pe = cols(w_in, 2 * LORA, ROPE)
            out.append((l, "pe", 0, [((DT, 128, 0, 64), pe), ((DT, 128, 64, 64), pe)]))
            for t in range(4):
                head = [cols(w_uq, t * 384 + h * (NOPE + ROPE), NOPE, 0, 2) for h in range(2)]
                turn = [cols(w_uq, t * 384 + h * (NOPE + ROPE) + NOPE, ROPE, 0, 2) for h in range(2)]
                out.append((l, "uq", t, [((2, 384, 0, 128), head[0]), ((2, 384, 128, 128), head[1]),
                                         ((2, 384, 256, 64), turn[0]), ((2, 384, 320, 64), turn[1])]))
            for t in range(4):
                out.append((l, "ukv", t, [((2, 512, 0, 512), cols(w_ukv, t * 512, 512, 0, 2))]))
        elif KIND[l] == NA:
            w_qkv, w_o = w["na_w_qkv"][j], w["na_w_o"][j]
            for t in range(DT):
                out.append((l, "q", t, [((DT, 128, 0, 128), cols(w_qkv, t * 128))]))
            for t in range(DT):
                out.append((l, "k", t, [((DT, 128, 0, 128), cols(w_qkv, D_MODEL + t * 128))]))
            for half in range(2):
                for kk in range(4):
                    out.append((l, "v", half * 4 + kk, [((2, 512, 0, 512),
                                cols(w_qkv, 2 * D_MODEL + half * 512, 512, 2 * kk, 2))]))
        else:
            w_qkv, w_o = w["swa_w_qkv"][j], w["swa_w_o"][j]
            for t in range(DT):
                out.append((l, "q", t, [((DT, 128, 0, 128), cols(w_qkv, t * 128))]))
            for g in range(KV_HEADS):
                kg = cols(w_qkv, (HEADS + g) * HD, HD)
                out.append((l, "kd", g, [((DT, 128, 0, 64), kg), ((DT, 128, 64, 64), kg)]))
            out.append((l, "vs", 0, [((DT, 128, 0, 128), cols(w_qkv, (HEADS + KV_HEADS) * HD))]))
        for t in range(DT):
            out.append((l, "o", t, [((DT, 128, 0, 128), cols(w_o, t * 128))]))
        for j2 in range(FT):
            for side in range(2):
                out.append((l, "in", 2 * j2 + side, [((DT, 128, 0, 128),
                            cols(w["w_ffn_in"][l], side * D_FF + j2 * 128))]))
        for t in range(DT):
            for kg in range(3):
                kt = min(8, FT - 8 * kg)
                out.append((l, "out", 3 * t + kg, [((kt, 128, 0, 128),
                            cols(w["w_ffn_out"][l], t * 128, 128, 8 * kg, kt))]))
    return out


def trunk(nc, a, out, known):
    ctx = ExitStack()
    with ctx:
        def sb(name, shape, dt=F32):
            return ctx.enter_context(nc.sbuf_tensor(name, shape, dt))

        def sig(name):
            return Signal(ctx.enter_context(nc.semaphore(name)), known.setdefault(name, {}))

        x = sb("x", [128, DT, TOK])
        y = sb("y", [128, DT, TOK])
        modw = y[:, :, :].rearrange("p t n -> p (t n)").rearrange("p (s n) -> p s n", s=2)
        h_base = nc.sbuf_base + (-nc.sbuf_base) % 32
        hH, hL = sb("hH", [128, DT, TOK], F32R), sb("hL", [128, DT, TOK], F32R)
        wR = sb("wR", [128, RAW, 1024])
        wH, wL = sb("wH", [128, SPLIT, 1024], F32R), sb("wL", [128, SPLIT, 1024], F32R)
        cst = sb("cst", [128, C_END])
        gT, bT, sT = sb("gT", [128, 128]), sb("bT", [128, DEPTH * 48]), sb("sT", [128, 24])
        cpad = sb("cpad", [128, DT, 32])
        modT = sb("modT", [128, 6, DT, 2])
        coefA = sb("coefA", [128, 2, DT, 2])
        coefG = sb("coefG", [128, 2, DT, 2])
        sq = sb("sq", [128, 2, TOK])
        modrow = sq[:, 1, :]
        tmp = sb("tmp", [128, 2, TOK])
        sums = sb("sums", [128, 12])
        mean, rstd = sb("mean", [128, 8]), sb("rstd", [128, 8])
        mx, ngm = sb("mx", [128, 2, 2, 2]), sb("ngm", [128, 2, 2, 2])
        esum, rsum, esnk = sb("esum", [128, 2, 2, 2]), sb("rsum", [128, 2, 2, 2]), sb("esnk", [128, 2, 2, 2])
        sink = sb("sink", [128, HEADS])
        base = nc.sbuf_base + (-nc.sbuf_base) % 32
        fence = sb("fence", [128, (FT * TOK * 2 * 4 + 64) // 4])

        def at(name, shape, kib, dt=F32):
            return nc.alloc_sbuf_tensor_at(name, shape, dt, offset=base + kib * 1024)

        aH, aL = at("aH", [128, FT, TOK], 0, F32R), at("aL", [128, FT, TOK], 44, F32R)
        q, k = at("q", [128, DT, TOK], 0), at("k", [128, DT, TOK], 16)
        v = at("v", [128, 4, D_MODEL], 32)
        P = at("P", [128, PROBS, 2, TOK], 48)
        PT = at("PT", [128, 2, 6, 256], 64)
        BM = at("BM", [128, 2, 2, 256], 76)
        kd = at("kd", [128, 2, TOK], 76)
        latH, latL = at("latH", [128, 4, TOK], 48, F32R), at("latL", [128, 4, TOK], 56, F32R)
        lat = at("lat", [128, 4, TOK], 64)
        qpe = at("qpe", [128, 4, TOK], 76)
        kpe = at("kpe", [128, TOK], 84)
        dots = {"o": at("dots_o", [128, 4, 3, TOK], 0),
                "out": nc.alloc_sbuf_tensor_at("dots_out", [128, 4, 3, TOK], F32, offset=h_base)}
        xrow = at("xrow", [128, 4, D_MODEL], 0)
        grow, brow, srow = at("grow", [128, 128], 16), at("brow", [96, 2, 128], 17), at("srow", [24, 128], 18)
        zero = at("zero", [HEADS, BIAS_COLS], 19)
        modw0 = at("modw0", [128, DT, 2048], 24)

        bank = [ctx.enter_context(nc.psum_tensor(f"bank{i}", [128, 512], F32)) for i in range(8)]
        STAT, RB1, RB2, AUX = bank[4], bank[5], bank[6], bank[7]
        table = nc.dram_tensor("bias_table", (HEADS, BIAS_ROWS * BIAS_COLS), F32, kind="Internal").ap()

        ident, rot = cst[:, C_ID:C_ID + 128], cst[:, C_ROT:C_ROT + 128]
        cos, sin = cst[:, C_COS:C_COS + 256], cst[:, C_SIN:C_SIN + 256]
        flip = cst[:, C_FLIP:C_FLIP + 128]
        per_d, per_l, expo8 = cst[:, C_PD:C_PD + 1], cst[:, C_PL:C_PL + 1], cst[:, C_EXP:C_EXP + 8]

        loaded = [ctx.enter_context(nc.semaphore(f"loaded{i}")) for i in range(RAW)]
        modloaded = [sig(f"modloaded{i}") for i in range(2)]
        modloaded0 = [sig(f"modloaded0_{i}") for i in range(DT)]
        biasloaded = [sig(f"biasloaded{i}") for i in range(2)]
        inputs_in, rows_in, sink_in = sig("inputs_in"), sig("rows_in"), sig("sink_in")
        table_st, stored = sig("table_st"), sig("stored")
        w_hi, w_used = [ctx.enter_context(nc.semaphore(n)) for n in ("w_hi", "w_used")]
        w_lo = [ctx.enter_context(nc.semaphore(f"w_lo{i}")) for i in range(SPLIT)]
        tile_done = sig("tile_done")
        pe_aux = sig("pe_aux")
        pe_s, pe_t, pe_o, pe_mod = sig("pe_s"), sig("pe_t"), sig("pe_o"), sig("pe_mod")
        a_sq, a_h, a_gate, a_exp, a_pt, a_misc, a_copy = [sig(n) for n in (
            "a_sq", "a_h", "a_gate", "a_exp", "a_pt", "a_misc", "a_copy")]
        v_copy, v_x, v_h, v_norm, v_step, v_mod = [sig(n) for n in ("v_copy", "v_x", "v_h", "v_norm", "v_step", "v_mod")]
        v_soft, v_ffn = sig("v_soft"), sig("v_ffn")
        v_dot, g_dot = sig("v_dot"), sig("g_dot")
        g_norm, g_x, g_h, g_soft, g_bias, g_misc = [sig(n) for n in ("g_norm", "g_x", "g_h", "g_soft", "g_bias", "g_misc")]

        chunks = weight_chunks(a)
        first = {}
        for c, (l, what, i, _) in enumerate(chunks):
            first.setdefault((l, what), c)
        load_count, per_slot = [], [0] * RAW
        for c, ch in enumerate(chunks):
            per_slot[c % RAW] += 16 * len(ch[3])
            load_count.append(per_slot[c % RAW])
        after_norm = [first[l, what] for l in range(DEPTH) for what in (("lat" if KIND[l] == MLA else "q"), "in")]
        size = [sum(s[0] * s[3] for s, _ in ch[3]) for ch in chunks]

        def lo_of(c, i=0, step=0):
            return w_lo[c % SPLIT], i * (step // SPLIT) + (c // SPLIT + 1)

        def split_lo(engine, here, c, i=0, step=0):
            if c < len(chunks) and here == (c % SPLIT == SPLIT - 1):
                engine.wait_ge(w_hi, i * step + (c + 1))
                engine.tensor_tensor(wL[:, c % SPLIT, 0:size[c]], wR[:, c % RAW, 0:size[c]],
                                     wH[:, c % SPLIT, 0:size[c]].bitcast(F32), ALU.subtract)\
                    .then_inc(w_lo[c % SPLIT], 1)

        tiles, frees = [], []

        def tile(key, *free):
            tiles.append(key)
            frees.append(free)

        for l in range(DEPTH):
            if KIND[l] == MLA:
                for t in range(4):
                    tile((l, "lat", t), (v_copy, (l, "lat", t)))
                tile((l, "pe", 0), (v_copy, (l, "pe", 0)))
                for t in range(4):
                    for part in range(3):
                        tile((l, "uq", t, part), (a_copy if part == 1 else v_copy, (l, "uq", t, part)))
                for t in range(4):
                    for part in range(4):
                        tile((l, "ukv", t, part), (a_copy if part % 2 else v_copy, (l, "ukv", t, part)))
            else:
                for t in range(DT):
                    tile((l, "q", t), (v_copy, (l, "q", t)))
                if KIND[l] == NA:
                    for t in range(DT):
                        tile((l, "k", t), (v_copy, (l, "k", t)))
                    for t in range(8):
                        tile((l, "v", t), (v_copy, (l, "v", t)))
                else:
                    for t in range(KV_HEADS):
                        tile((l, "kd", t), (v_copy, (l, "kd", t)))
                    tile((l, "vs", 0), (v_copy, (l, "vs", 0)))
            for t in range(DT):
                tile((l, "o", t), (v_copy, (l, "o", t)), (a_sq, (l, "o", t)))
            for j in range(2 * FT):
                tile((l, "in", j), (v_ffn, (l, "hi", j // 2)))
            for t in range(DT):
                tile((l, "out", t), (v_copy, (l, "out", t)), (a_sq, (l, "out", t)))
        number = {key: g for g, key in enumerate(tiles)}
        place = [(g - key[2] + key[2] % 2 if key[1] == "out" else g) % 4 for g, key in enumerate(tiles)]
        prior = [max([p for p in range(g) if place[p] == place[g]], default=None) for g in range(len(tiles))]

        def psum(key):
            return bank[place[number[key]]]

        whole_with = {}
        for c, (l, what, i, _) in enumerate(chunks):
            if what in ("lat", "pe", "q", "k", "kd", "vs", "o", "in"):
                whole_with[l, what, i] = c
            elif what == "uq":
                whole_with[l, what, i, 2] = c
            elif what == "ukv":
                whole_with[l, what, i, 3] = c
            elif what == "v" and i % 4 == 3:
                whole_with[l, what, i] = c
            elif what == "out" and i % 3 == 2:
                whole_with[l, what, i // 3] = c

        def whole(key):
            return (w_used, whole_with[key] + 1) if key in whole_with else tile_done.at(key)

        splits_at = {}
        for c, (l, what, i, _) in enumerate(chunks):
            key = ((l, what, i, 0) if what in ("uq", "ukv") else (l, what, i // 3) if what == "out" else
                   (l, what, 4 * (i // 4)) if what == "v" else (l, what, i))
            if what != "in" and c not in after_norm:
                splits_at.setdefault(key, []).append(c)

        def x_ready(key, t):
            return v_x.at((key, t)) if t in ADD_V or key == (0, "mix") else g_x.at((key, t))

        def hi_ready(key, t):
            return a_h.at((key, t))

        def lo_ready(key, t):
            return v_h.at((key, "lo", t)) if t in LO_V else g_h.at((key, t))

        def kinds(l, what):
            return (XX, YY, XG, GG) if (l, what) != (DEPTH - 1, "out") else (YY,)

        def slot_of(what, kind, t):
            return dots[what][:, kind, 0 if t == 0 else 1 + t % 2, :]

        def width(l):
            return SEQ if l == DEPTH - 1 else TOK

        def spans(l):
            return [(0, 0, SEQ)] if l == DEPTH - 1 else [(0, 0, SEQ), (1, SEQ, TOK)]

        def units(l):
            nrt = 2 if l == DEPTH - 1 else 3
            return [(g * nrt + rt, g, rt) for g in range(DT) for rt in range(nrt)]

        def out_turns(l):
            return DT // 2 - 2

        def heads(l):
            return 1 if KIND[l] == MLA else 2

        def modparts(l):
            return [(l, r, kt) for r in (1, 2) for kt in range(DT)]

        modorder = [p for l in range(DEPTH) for p in modparts(l)]
        modindex = {p: n for n, p in enumerate(modorder)}

        block = ctx.enter_context(nc.Block())

        @block.sync
        def _(sp):
            def load_chunk(c):
                if c >= RAW:
                    sp.wait_ge(*lo_of(c - RAW))
                for (kt, stride, c0, n), src in chunks[c][3]:
                    dst = wR[:, c % RAW, 0:kt * stride].rearrange("p (k n) -> p k n", k=kt)[:, :, c0:c0 + n]
                    sp.dma_start(dst, src).then_inc(loaded[c % RAW], 16)

            def load_mod(part):
                m, r, kt = part
                n = modindex[part]
                if n >= 2:
                    sp.wait_ge(*pe_mod.at(modorder[n - 2]))
                sp.dma_start(modw[:, n % 2, :], a["w_mod"][m, kt * 128:(kt + 1) * 128, r * 2048:(r + 1) * 2048])\
                    .then_inc(*modloaded[n % 2].mark(part, 16))

            def load_bias(l, u, g, rt):
                prior = bias_units[bias_units.index((u, g, rt)) - 2] if bias_units.index((u, g, rt)) >= 2 else None
                if prior:
                    sp.wait_ge(*v_soft.at((l, "bias", prior[0], 1)))
                n = bias_units.index((u, g, rt))
                for hh in range(2):
                    for r in range(2):
                        start = (2 * g + hh) * BIAS_ROWS * BIAS_COLS + (GRID_ROWS - 2 - 2 * rt + r) * BIAS_COLS
                        src = bass.AP(table.tensor, start, [[1, GRID_W], [BIAS_COLS, GRID_ROWS], [1, GRID_W]])
                        dst = BM[r * 64:r * 64 + 64, n % 2, hh, :].rearrange("p (i n) -> p i n", i=GRID_ROWS)
                        sp.dma_start(dst, src).then_inc(*biasloaded[n % 2].mark((l, u, hh, r), 16))

            sp.dma_start(cst[:, :], a["consts"]).then_inc(*inputs_in.mark("consts", 16))
            sp.dma_start(srow[0:4, :], a["mla_g_q"].rearrange("l (t n) -> (l t) n", n=128)).then_inc(*inputs_in.mark(1, 16))
            sp.dma_start(srow[4:8, :], a["mla_g_kv"].rearrange("l (t n) -> (l t) n", n=128)).then_inc(*inputs_in.mark(2, 16))
            sp.dma_start(srow[8:16, :], a["c"].rearrange("l (t n) -> (l t) n", n=128)).then_inc(*inputs_in.mark(3, 16))
            sp.dma_start(srow[16:24, :], a["c_ctx"].rearrange("(t n) -> t n", n=128)).then_inc(*inputs_in.mark(4, 16))
            for i, g in enumerate(("g_pre_mix", "g_post_mix", "g_pre_ffn", "g_post_ffn")):
                sp.dma_start(grow[32 * i:32 * i + 32, :], a[g].rearrange("l (t n) -> (l t) n", n=128))\
                    .then_inc(*inputs_in.mark(5 + i, 16))
            sp.dma_start(brow[:, :, :], a["b_mod"].rearrange("(u l) (t n) -> (l t) u n", u=2, n=128))\
                .then_inc(*inputs_in.mark("vectors", 16))
            for i in range(2):
                sp.dma_start(xrow[:, i, :], a["x"][0, i * 128:i * 128 + 128, :]).then_inc(*rows_in.mark(("x", i), 16))
            for i in range(2):
                sp.dma_start(xrow[:, 2 + i, :], a["ctx"][0, i * 128:i * 128 + 128, :])\
                    .then_inc(*rows_in.mark("rows" if i else "ctx0", 16))
            for c in range(RAW):
                load_chunk(c)
            for kt in range(DT):
                sp.dma_start(modw0[:, kt, :], a["w_mod"][0, kt * 128:(kt + 1) * 128, 0:2048])\
                    .then_inc(*modloaded0[kt].mark((0, 0, kt), 16))
            sp.dma_start(sink[:, :], a["swa_sink"][0:1, :].broadcast_to([128, HEADS]))\
                .then_inc(*sink_in.mark("sink", 16))
            sp.wait_ge(*g_misc.at("zero"))
            sp.dma_start(table.rearrange("h (r n) -> h r n", n=BIAS_COLS),
                         zero[:, :].unsqueeze(1).broadcast_to([HEADS, BIAS_ROWS, BIAS_COLS]))\
                .then_inc(*table_st.mark("zeros", 16))
            sp.wait_ge(*table_st.at("zeros"))
            mid = table.rearrange("h (r n) -> h r n", n=BIAS_COLS)[:, :, GRID_W - WIN_COLS:GRID_W + WIN_COLS - 1]
            sp.dma_start(mid, a["na_rpb"][0, :, WIN_ROWS - GRID_ROWS:WIN_ROWS + GRID_ROWS - 1, :])\
                .then_inc(*table_st.mark("table", 16))
            sp.wait_ge(*table_st.at("table"))
            for l in range(DEPTH):
                c0 = first[l, "q"] if KIND[l] != MLA else first[l, "lat"]
                for c in range(c0 + RAW, first[l, "o"] + RAW):
                    load_chunk(c)
                parts = modparts(l)
                bias_units = [u for u in units(l) if u[2] < 2] if KIND[l] == NA else []
                for i in range(len(units(l))):
                    if i == 0:
                        for t in (max(LO_V), max(t for t in range(DT) if t not in LO_V)):
                            sp.wait_ge(*lo_ready((l, "mix"), t))
                    if i < len(parts):
                        load_mod(parts[i])
                    if units(l)[i] in bias_units:
                        load_bias(l, *units(l)[i])
                for i in range(DT):
                    if l < DEPTH - 1:
                        if i == 0:
                            sp.wait_ge(*pe_o.at((l, DT - 1)))
                        sp.dma_start(modw0[:, i, :], a["w_mod"][l + 1, i * 128:(i + 1) * 128, 0:2048])\
                            .then_inc(*modloaded0[i].mark((l + 1, 0, i), 16))
                    if i + RAW < DT:
                        load_chunk(first[l, "o"] + RAW + i)
                c0, turns = first[l, "in"], 2 * FT // 6
                w_in = a["w_ffn_in"][l].rearrange("(k p) n -> p k n", p=128)
                with sp.Fori(0, turns) as i:
                    for b in range(6):
                        sp.wait_ge(*lo_of(c0 + b - RAW, i, 6))
                        slot = wR[:, (c0 + b) % RAW, :].rearrange("p (k n) -> p k n", k=DT)
                        src = w_in[:, :, bass.ds(i * 384 + ((b % 2) * D_FF + (b // 2) * 128), 128)]
                        sp.dma_start(slot, src).then_inc(loaded[(c0 + b) % RAW], 16)
                for c in range(c0 + 6 * turns, first[l, "out"]):
                    load_chunk(c)
                c0 = first[l, "out"]
                w_out = a["w_ffn_out"][l].rearrange("(k p) n -> p k n", p=128)
                with sp.Fori(0, DT // 2) as i:
                    for b in range(6):
                        kg = b % 3
                        kt = min(8, FT - 8 * kg)
                        sp.wait_ge(*lo_of(c0 + b - RAW, i, 6))
                        slot = wR[:, (c0 + b) % RAW, 0:kt * 128].rearrange("p (k n) -> p k n", k=kt)
                        src = w_out[:, 8 * kg:8 * kg + kt, bass.ds(i * 256 + (b // 3) * 128, 128)]
                        sp.dma_start(slot, src).then_inc(loaded[(c0 + b) % RAW], 16)
                if l < DEPTH - 1:
                    for c in range(c0 + 3 * DT, c0 + 3 * DT + RAW):
                        load_chunk(c)
            for i in range(2):
                sp.wait_ge(*v_copy.at(("out", i, 1)))
                sp.dma_start(out[0, i * 128:i * 128 + 128, :], xrow[:, i, :]).then_inc(*stored.mark(i, 16))
            sp.wait_ge(*stored.at(1))

        @block.scalar
        def _(act):
            def split_hi(c, i=0, step=0):
                if c >= len(chunks):
                    return
                act.wait_ge(loaded[c % RAW], i * (step // RAW * 16) + load_count[c])
                if c >= SPLIT:
                    act.wait_ge(w_used, i * step + (c - SPLIT + 1))
                act.activation(wH[:, c % SPLIT, 0:size[c]], wR[:, c % RAW, 0:size[c]], ACT.Copy).then_inc(w_hi, 1)

            def norm_squares(key, t, n):
                act.wait_ge(*x_ready(key, t))
                if t % 2 in sq_reader:
                    act.wait_ge(*sq_reader[t % 2])
                act.activation(sq[:, t % 2, 0:n], x[:, t, 0:n], ACT.Square).then_inc(*a_sq.mark((key, t)))
                sq_reader[t % 2] = pe_aux.at((key, "stat", t))

            sq_reader = {}

            def norm_h(key, which, n, streams):
                shift = 0 if which == 0 else 3
                for t in range(DT):
                    act.wait_ge(*v_h.at((key, "xr", t)))
                    for s, t0, t1 in streams:
                        act.activation(y[:, t, t0:t1], y[:, t, t0:t1], ACT.Identity, scale=coefA[:, which, t, s:s + 1],
                                       bias=modT[:, shift, t, s:s + 1]).then_inc(*a_h.mark((key, "h", t)))
                    act.wait_ge(*a_h.at((key, "h", t)))
                    act.activation(hH[:, t, 0:n], y[:, t, 0:n], ACT.Copy).then_inc(*a_h.mark((key, t)))

            def chunk_phase(l, what, after=None):
                c = first[l, what]
                while c < len(chunks) and chunks[c][:2] == (l, what):
                    if c not in after_norm:
                        split_hi(c + AHEAD)
                    if after:
                        after(chunks[c][2])
                    c += 1

            act.wait_ge(*v_copy.at("small"))
            act.wait_ge(*g_misc.at("cpad"))
            for s in range(2):
                act.activation(cpad[:, :, s], sT[:, 8 + 8 * s:16 + 8 * s], ACT.Silu).then_inc(*a_misc.mark(("c", s)))
            for t in range(DT):
                norm_squares((0, "mix"), t, TOK)
            for c in range(AHEAD + 1):
                split_hi(c)
            act.wait_ge(*v_mod.at((0, "A", 0)))
            for l in range(DEPTH):
                N = width(l)
                norm_h((l, "mix"), 0, TOK, [(0, 0, SEQ), (1, SEQ, TOK)])
                if KIND[l] == MLA:
                    def latent_square(t):
                        act.wait_ge(*v_copy.at((l, "lat", t)))
                        if t >= 2:
                            act.wait_ge(*pe_aux.at((l, "latstat", t - 2)))
                        elif sq_reader.get(t):
                            act.wait_ge(*sq_reader[t])
                        act.activation(sq[:, t % 2, :], lat[:, t, :], ACT.Square).then_inc(*a_sq.mark((l, "lat", t)))
                        sq_reader[t % 2] = pe_aux.at((l, "latstat", t))

                    def latent_hi(t):
                        act.wait_ge(*v_h.at((l, "latn", t)))
                        act.activation(latH[:, t, :], tmp[:, t % 2, :], ACT.Copy).then_inc(*a_h.mark((l, "latn", t)))

                    chunk_phase(l, "lat", latent_square)
                    latent_hi(0)
                    latent_hi(1)
                    chunk_phase(l, "pe")

                    def odd_queries(t):
                        act.wait_ge(*whole((l, "uq", t, 1)))
                        act.activation(q[:, 2 * t + 1, 0:N], psum((l, "uq", t, 1))[:, 0:N], ACT.Copy)\
                            .then_inc(*a_copy.mark((l, "uq", t, 1)))
                        if t == 0:
                            latent_hi(2)
                            latent_hi(3)

                    def odd_keys_values(t):
                        act.wait_ge(*whole((l, "ukv", t, 1)))
                        act.activation(k[:, 2 * t + 1, :], psum((l, "ukv", t, 1))[:, :], ACT.Copy)\
                            .then_inc(*a_copy.mark((l, "ukv", t, 1)))
                        act.wait_ge(*whole((l, "ukv", t, 3)))
                        act.activation(v[:, 2:4, t * 256:t * 256 + 256],
                                       psum((l, "ukv", t, 3))[:, :].rearrange("p (a n) -> p a n", a=2), ACT.Copy)\
                            .then_inc(*a_copy.mark((l, "ukv", t, 3)))

                    chunk_phase(l, "uq", odd_queries)
                    chunk_phase(l, "ukv", odd_keys_values)
                elif KIND[l] == NA:
                    for what in ("q", "k", "v"):
                        chunk_phase(l, what)
                else:
                    for what in ("q", "kd", "vs"):
                        chunk_phase(l, what)

                scale = float(NOPE + ROPE) ** -0.5 if KIND[l] == MLA else float(HD) ** -0.5
                todo = units(l)
                H = heads(l)

                def exps(u, g, rt):
                    for hh in range(H):
                        act.wait_ge(*v_soft.at((l, "neg", u, hh)))
                        if u >= PROBS:
                            act.wait_ge(*pe_t.at((l, u - PROBS, hh)))
                        S = bank[(2 * (u % 2) + hh) if H == 2 else u % 2]
                        for qh in range(2 if rt == 2 else 1):
                            n = 256 if rt == 2 else 512
                            cut = slice(qh * n, qh * n + n)
                            act.activation(P[:, u % PROBS, hh, cut], S[:, cut], ACT.Exp, scale=scale,
                                           bias=ngm[:, u % 2, hh, qh:qh + 1],
                                           accum_out=esum[:, u % 2, hh, qh:qh + 1]).then_inc(*a_exp.mark((l, u, hh, qh)))
                        if KIND[l] == SWA:
                            nq = 2 if rt == 2 else 1
                            h = 2 * g + hh
                            act.activation(esnk[:, u % 2, hh, 0:nq], ngm[:, u % 2, hh, 0:nq], ACT.Exp,
                                           bias=sink[:, h:h + 1]).then_inc(*a_exp.mark((l, u, hh, "sink")))

                def evacuate(u, g, rt):
                    for hh in range(H):
                        act.wait_ge(*pe_t.at((l, u, hh)))
                        if g > 0 and rt == 0:
                            act.wait_ge(*pe_o.at((l, g - 1)))
                        T = bank[4 + (hh if H == 2 else u % 2)]
                        if rt < 2:
                            dst = PT[:, hh, 0:4, rt * 128:rt * 128 + 128]
                            src = T[:, :].rearrange("p (k n) -> p k n", k=4)
                        else:
                            dst = PT[:, hh, 4:6, :].rearrange("p k (q n) -> p q k n", q=2)
                            src = T[:, :].rearrange("p (q k n) -> p q k n", q=2, k=2)
                        act.activation(dst, src, ACT.Copy).then_inc(*a_pt.mark((l, u, hh)))

                def output(g):
                    act.wait_ge(*pe_o.at((l, g)))
                    act.activation(hH[:, g, 0:N], bank[6][:, 0:N], ACT.Copy).then_inc(*a_h.mark((l, "o", g)))

                last_rt = todo[-1][2]
                for n in range(len(todo) + LAG + 1):
                    if 0 <= n - LAG < len(todo):
                        evacuate(*todo[n - LAG])
                    if n < len(todo):
                        exps(*todo[n])
                    if n > LAG and todo[n - LAG - 1][2] == last_rt:
                        output(todo[n - LAG - 1][1])
                sq_reader[1] = pe_aux.at(modparts(l)[-1][:2] + ("modT",))

                def squares(what):
                    def after(t):
                        for kind in kinds(l, what):
                            if kind == XG:
                                continue
                            if t >= 3:
                                act.wait_ge(*v_dot.at((l, what, kind, t - 2)))
                            else:
                                act.wait_ge(w_used, first[l, what] + 1)
                            if kind != XX:
                                act.wait_ge(*v_copy.at((l, what, t)))
                            src = {XX: x[:, t, 0:N], YY: psum((l, what, t))[:, 0:N], GG: y[:, t, 0:N]}[kind]
                            act.activation(slot_of(what, kind, t)[:, 0:N], src, ACT.Square)\
                                .then_inc(*a_sq.mark((l, what, t) if kind == YY else (l, what, kind, t)))
                    return after

                chunk_phase(l, "o", squares("o"))
                split_hi(first[l, "in"] + AHEAD)
                norm_h((l, "ffn"), 1, N, spans(l))

                def gates(j0, n, i=0):
                    for j in range(j0, j0 + n):
                        c = first[l, "in"] + 2 * j
                        for b in range(2):
                            if c + b not in after_norm:
                                split_hi(c + b + AHEAD, i, 2 * n)
                        act.wait_ge(w_used, i * (2 * n) + (c + 1))
                        if j >= 2:
                            act.wait_ge(*v_ffn.paced(i, (l, "hi", j - 2), n))
                        act.activation(tmp[:, j % 2, 0:N], psum((l, "in", 2 * j))[:, 0:N], ACT.Silu)\
                            .then_inc(*a_gate.mark((l, "silu", j)))

                gates(0, PEELED)
                start = a_gate.count
                with act.Fori(0, TURNS) as i:
                    gates(PEELED, PAIRS, i)
                a_gate.repeated(start, TURNS, PAIRS)
                sq_reader[0] = v_ffn.at((l, "lo", FT - 2))
                sq_reader[1] = v_ffn.at((l, "lo", FT - 1))

                for t in range(DT):
                    for kg in range(3):
                        split_hi(first[l, "out"] + 3 * t + kg + AHEAD)
                    squares("out")(t)
                split_hi(first[l, "out"] + 3 * DT + AHEAD)

        @block.gpsimd
        def _(pool):
            def dot(l, what, t, n):
                if t == DT - 1 or XG not in kinds(l, what):
                    return
                pool.wait_ge(*v_copy.at((l, what, t)))
                if t >= 3:
                    pool.wait_ge(*g_dot.at((l, what, "sum", t - 2)))
                pool.tensor_tensor(slot_of(what, XG, t)[:, 0:n], x[:, t, 0:n], y[:, t, 0:n], ALU.mult)\
                    .then_inc(*g_dot.mark((l, what, "sum", 0) if t == 0 else (l, what, t)))
                if t:
                    pool.wait_ge(*g_dot.at((l, what, t)))
                    total = dots[what][:, XG, 0, 0:n]
                    pool.tensor_tensor(total, total, slot_of(what, XG, t)[:, 0:n], ALU.add)\
                        .then_inc(*g_dot.mark((l, what, "sum", t)))

            def chunk_phase(l, what, after=None):
                c = first[l, what]
                while c < len(chunks) and chunks[c][:2] == (l, what):
                    if c not in after_norm:
                        split_lo(pool, False, c + AHEAD)
                    if after:
                        after(chunks[c][2])
                    c += 1

            def power(key, n=4, c=0):
                pool.wait_ge(*v_norm.at((key, "mean")))
                pool.tensor_tensor(rstd[:, c:c + n], mean[:, c:c + n], expo8[:, 0:n], ALU.pow).then_inc(*g_norm.mark(key))

            def lo(key, t, n):
                pool.wait_ge(*hi_ready(key, t))
                pool.tensor_tensor(hL[:, t, 0:n], y[:, t, 0:n], hH[:, t, 0:n].bitcast(F32), ALU.subtract)\
                    .then_inc(*g_h.mark((key, t)))

            def add_y(key, t, n):
                pool.wait_ge(*v_step.at((key, "gy", t)))
                pool.tensor_tensor(x[:, t, 0:n], x[:, t, 0:n], y[:, t, 0:n], ALU.add).then_inc(*g_x.mark((key, t)))

            def adds_and_lows(key, n, adds=True):
                for t in range(-2, DT):
                    if adds and t + 2 < DT and t + 2 not in ADD_V:
                        add_y(key, t + 2, n)
                    if t >= 0 and t not in LO_V:
                        lo(key, t, n)

            pool.memset(cpad[:, :, :], 0.0).then_inc(*g_misc.mark("cpad"))
            pool.memset(zero[:, :], 0.0).then_inc(*g_misc.mark("zero"))
            power((0, "mix"))
            for c in range(AHEAD + 1):
                split_lo(pool, False, c)
            adds_and_lows((0, "mix"), TOK, adds=False)
            for l in range(DEPTH):
                N = width(l)
                if KIND[l] == MLA:
                    chunk_phase(l, "lat", lambda t: power((l, "lat", 0)) if t == 2 else None)
                    chunk_phase(l, "pe")
                    power((l, "lat", 1), 4, 4)
                    chunk_phase(l, "uq")
                    chunk_phase(l, "ukv")
                else:
                    for what in ("q", "k", "v") if KIND[l] == NA else ("q", "kd", "vs"):
                        chunk_phase(l, what)
                if heads(l) == 2:
                    todo = units(l)
                    bias_units = [w for w in todo if w[2] < 2] if KIND[l] == NA else []

                    def mask_bias(w):
                        n, (u, g, rt) = bias_units.index(w), w
                        pool.wait_ge(*biasloaded[n % 2].at((l, u, 1, 1)))
                        for hh in range(2):
                            b4 = BM[:, n % 2, hh, :].rearrange("p (i n) -> p i n", i=GRID_ROWS)
                            m4 = cst[:, C_NAM:C_NAM + 64].unsqueeze(1).broadcast_to([128, GRID_ROWS, GRID_W])
                            pool.tensor_tensor(b4, b4, m4, ALU.add).then_inc(*g_bias.mark((l, u, hh)))

                    for n, w in enumerate(todo):
                        if n == 0 and w in bias_units:
                            mask_bias(w)
                        if n + 1 < len(todo) and todo[n + 1] in bias_units:
                            mask_bias(todo[n + 1])
                        u, g, rt = w
                        for qh in range(2 if rt == 2 else 1):
                            cut = slice(0, 512) if rt < 2 else slice(qh * 256, qh * 256 + 256)
                            pool.wait_ge(*v_soft.at((l, "recip", u, 1)))
                            pool.tensor_scalar(P[:, u % PROBS, 1, cut], P[:, u % PROBS, 1, cut],
                                               rsum[:, u % 2, 1, qh:qh + 1], None, ALU.mult)\
                                .then_inc(*g_soft.mark((l, u, 1, qh)))
                chunk_phase(l, "o", lambda t: dot(l, "o", t, N))
                power((l, "post", "o"))
                power((l, "ffn"), 4, 4)
                split_lo(pool, False, first[l, "in"] + AHEAD)
                adds_and_lows((l, "ffn"), N)
                c0 = first[l, "in"] + AHEAD
                for b in range(1, 2 * PEELED):
                    split_lo(pool, False, c0 + b)
                with pool.Fori(0, TURNS) as i:
                    for b in range(2 * PEELED, 2 * PEELED + 2 * PAIRS):
                        split_lo(pool, False, c0 + b, i, 2 * PAIRS)
                for t in range(DT):
                    for kg in range(3):
                        split_lo(pool, False, first[l, "out"] + 3 * t + kg + AHEAD)
                    dot(l, "out", t, N)
                power((l, "post", "out"))
                if l < DEPTH - 1:
                    power((l + 1, "mix"), 4, 4)
                    split_lo(pool, False, first[l, "out"] + 3 * DT + AHEAD)
                    adds_and_lows((l + 1, "mix"), N)
                else:
                    for t in (t for t in range(DT) if t not in ADD_V):
                        add_y((DEPTH, "mix"), t, N)

        @block.vector
        def _(dve):
            def mean_eps(key, src, n):
                dve.wait_ge(*pe_aux.at((key, "stats")))
                dve.tensor_scalar(mean[:, 0:n // 128], src[:, 0:n // 128], EPS, None, ALU.add)\
                    .then_inc(*v_norm.mark((key, "mean")))

            def residual(key, t, n):
                dve.tensor_tensor(y[:, t, 0:n], y[:, t, 0:n], RB1[:, 0:n], ALU.mult)\
                    .then_inc(*v_step.mark((key, "gy", t)))
                if t in ADD_V:
                    dve.wait_ge(*v_step.at((key, "gy", t)))
                    dve.tensor_tensor(x[:, t, 0:n], x[:, t, 0:n], y[:, t, 0:n], ALU.add)\
                        .then_inc(*v_x.mark((key, t)))

            def scaled(key, t, n):
                dve.wait_ge(*x_ready(key, t))
                dve.tensor_tensor(y[:, t, 0:n], x[:, t, 0:n], RB2[:, 0:n], ALU.mult).then_inc(*v_h.mark((key, "xr", t)))

            def low(key, t, n):
                if t in LO_V:
                    dve.wait_ge(*hi_ready(key, t))
                    dve.tensor_tensor(hL[:, t, 0:n], y[:, t, 0:n], hH[:, t, 0:n].bitcast(F32), ALU.subtract)\
                        .then_inc(*v_h.mark((key, "lo", t)))

            def mean_of_sum(key, post, n):
                nb = n // 128
                xx, xg, gg, r = sums[:, 0:nb], sums[:, 4:4 + nb], sums[:, 8:8 + nb], rstd[:, 0:nb]
                dve.wait_ge(*pe_aux.at((post, "sums")))
                dve.tensor_scalar(xx, STAT[:, 4:4 + nb], EPS, None, ALU.add).then_inc(*v_norm.mark((key, "xx")))
                dve.tensor_copy(sums[:, 4:12], STAT[:, 8:16]).then_inc(*v_norm.mark((key, "sums")))
                dve.wait_ge(*g_norm.at(post))
                dve.wait_ge(*v_norm.at((key, "sums")))
                dve.tensor_tensor(gg, gg, r, ALU.mult).then_inc(*v_norm.mark((key, 1)))
                dve.wait_ge(*v_norm.at((key, 1)))
                dve.scalar_tensor_tensor(xg, xg, 2.0, gg, ALU.mult, ALU.add).then_inc(*v_norm.mark((key, 2)))
                dve.wait_ge(*v_norm.at((key, 2)))
                dve.tensor_tensor(xg, xg, r, ALU.mult).then_inc(*v_norm.mark((key, 3)))
                dve.wait_ge(*v_norm.at((key, 3)))
                dve.tensor_tensor(xx, xx, xg, ALU.add).then_inc(*v_norm.mark((key, 4)))
                dve.wait_ge(*v_norm.at((key, 4)))
                dve.tensor_scalar(mean[:, 4:4 + nb], xx, EPS, None, ALU.max).then_inc(*v_norm.mark((key, "mean")))

            def sandwich(key, post, n, c):
                mean_eps(post, AUX, n)
                mean_of_sum(key, post, n)
                dve.wait_ge(*pe_aux.at((post, "bcast")))
                for t in range(LEAD):
                    residual(key, t, n)
                dve.wait_ge(*pe_aux.at((key, "bcast")))
                for t in range(DT + 2):
                    if t < DT:
                        scaled(key, t, n)
                    low(key, t - 2, n)
                    if t + LEAD < DT:
                        residual(key, t + LEAD, n)
                    if t == DT - 1:
                        split_lo(dve, True, c)

            def coefficients(which, l):
                pre, post = (0, 1) if which == 0 else (2, 3)

                def gain(kind):
                    return gT[:, kind * 32 + l * 8:kind * 32 + l * 8 + 8].unsqueeze(2).broadcast_to([128, DT, 2])
                sc, gt = (1, 2) if which == 0 else (4, 5)
                return (sc, gain(pre)), (gt, gain(post))

            def coef_a(which, l):
                (sc, g), _ = coefficients(which, l)
                dve.scalar_tensor_tensor(coefA[:, which, :, :], modT[:, sc, :, :], 1.0, g, ALU.add, ALU.mult)\
                    .then_inc(*v_mod.mark((l, "A", which)))

            def coef_g(which, l):
                _, (gt, g) = coefficients(which, l)
                dve.tensor_tensor(coefG[:, which, :, :], modT[:, gt, :, :], g, ALU.mult)\
                    .then_inc(*v_mod.mark((l, "G", which)))

            def mod_rows(m, r):
                dve.wait_ge(*pe_mod.at((m, r, DT - 1)))
                dve.tensor_copy(modrow, AUX[:, :]).then_inc(*v_mod.mark((m, r, "rows")))

            def mod_columns(m, r):
                dve.wait_ge(*pe_aux.at((m, r, "modT")))
                src = AUX[:, :].rearrange("p (j i u) -> p i j u", j=4, i=4)[:, :, :, 0:2]
                dst = modT[:, 2 * r:2 * r + 2, :, :].rearrange("p a (b j) s -> p (a b) j s", b=2)
                b = bT[:, m * 48 + r * 16:m * 48 + r * 16 + 16].rearrange("p (i j) -> p i j", j=4)
                dve.tensor_tensor(dst, src, b.unsqueeze(3).broadcast_to([128, 4, 4, 2]), ALU.add)\
                    .then_inc(*v_mod.mark((m, r)))
                dve.wait_ge(*v_mod.at((m, r)))

            def ahead(key):
                c = splits_at.get(key)
                for cc in c or ():
                    split_lo(dve, True, cc + AHEAD)

            def copy_tile(dst, key, n0=0, n1=512):
                ahead(key)
                dve.wait_ge(*whole(key))
                dve.tensor_copy(dst, psum(key)[:, n0:n1]).then_inc(*v_copy.mark(key))

            def rotate(tl, key):
                dve.wait_ge(*pe_aux.at((key, "rot")))
                if rotated:
                    dve.wait_ge(*v_step.at((rotated[-1], "r3")))
                dve.tensor_tensor(tmp[:, 0, 0:256], AUX[:, 0:256], sin, ALU.mult).then_inc(*v_step.mark((key, "r1")))
                dve.tensor_tensor(tl, tl, cos, ALU.mult).then_inc(*v_step.mark((key, "r2")))
                dve.wait_ge(*v_step.at((key, "r2")))
                dve.tensor_tensor(tl, tl, tmp[:, 0, 0:256], ALU.add).then_inc(*v_step.mark((key, "r3")))
                rotated.append(key)

            rotated = []

            dve.wait_ge(*pe_aux.at("small"))
            dve.tensor_copy(gT[:, :], bank[0][:, 0:128]).then_inc(*v_copy.mark("g"))
            dve.tensor_copy(bT[:, :].rearrange("p (u n) -> p u n", u=2),
                            bank[0][:, 128:320].rearrange("p (u n) -> p u n", u=2)).then_inc(*v_copy.mark("b"))
            dve.tensor_copy(sT[:, :], bank[0][:, 320:344]).then_inc(*v_copy.mark("small"))
            for t in range(DT):
                dve.wait_ge(*pe_aux.at(("x", t)))
                dve.tensor_copy(x[:, t, :], bank[1 + t % 3][:, :]).then_inc(*v_x.mark(((0, "mix"), t)))
            mean_eps((0, "mix"), STAT, TOK)
            dve.wait_ge(*pe_aux.at(((0, "mix"), "bcast")))
            for t in range(DT):
                scaled((0, "mix"), t, TOK)
            mod_rows(0, 0)
            mod_columns(0, 0)
            coef_a(0, 0)
            split_lo(dve, True, AHEAD)
            for t in range(DT):
                low((0, "mix"), t, TOK)

            for l in range(DEPTH):
                N = width(l)
                j = l // 3
                if KIND[l] == MLA:
                    def latent_mean(w):
                        dve.wait_ge(*pe_aux.at((l, "latstat", 2 * w + 1)))
                        dve.tensor_scalar(mean[:, 4 * w:4 * w + 4], STAT[:, 4 * w:4 * w + 4], EPS, None, ALU.add)\
                            .then_inc(*v_norm.mark(((l, "lat", w), "mean")))

                    def latent_norm(w):
                        dve.wait_ge(*pe_aux.at(((l, "lat", w), "bcast")))
                        for t in (2 * w, 2 * w + 1):
                            if t >= 2:
                                dve.wait_ge(*v_h.at((l, "latlo", t - 2)))
                            col = 4 * w + 2 * j + t % 2
                            dve.scalar_tensor_tensor(tmp[:, t % 2, :], lat[:, t, :], sT[:, col:col + 1],
                                                     (RB1, RB2)[w][:, :], ALU.mult, ALU.mult)\
                                .then_inc(*v_h.mark((l, "latn", t)))
                        for t in (2 * w, 2 * w + 1):
                            dve.wait_ge(*a_h.at((l, "latn", t)))
                            dve.tensor_tensor(latL[:, t, :], tmp[:, t % 2, :], latH[:, t, :].bitcast(F32), ALU.subtract)\
                                .then_inc(*v_h.mark((l, "latlo", t)))

                    for t in range(3):
                        copy_tile(lat[:, t, :], (l, "lat", t))
                    latent_mean(0)
                    copy_tile(lat[:, 3, :], (l, "lat", 3))
                    latent_norm(0)
                    copy_tile(kpe[:, :], (l, "pe", 0))
                    latent_mean(1)
                    rotated.clear()
                    for t in range(4):
                        copy_tile(q[:, 2 * t, 0:N], (l, "uq", t, 0), 0, N)
                        copy_tile(qpe[:, t, 0:N], (l, "uq", t, 2), 0, N)
                        if t == 0:
                            latent_norm(1)
                            dve.wait_ge(*v_h.at((l, "latlo", 3)))
                            rotate(kpe[:, 0:256], (l, "kpe"))
                        else:
                            rotate(qpe[:, t - 1, 0:256], (l, "qpe", t - 1))
                    for t in range(4):
                        copy_tile(k[:, 2 * t, :], (l, "ukv", t, 0))
                        key = (l, "ukv", t, 2)
                        dve.wait_ge(*whole(key))
                        dve.tensor_copy(v[:, 0:2, t * 256:t * 256 + 256],
                                        psum(key)[:, :].rearrange("p (a n) -> p a n", a=2)).then_inc(*v_copy.mark(key))
                        if t == 0:
                            rotate(qpe[:, 3, 0:256], (l, "qpe", 3))
                elif KIND[l] == NA:
                    for t in range(DT):
                        src = psum((l, "q", t))
                        ahead((l, "q", t))
                        dve.wait_ge(*whole((l, "q", t)))
                        back = bass.AP(q, t * TOK + 127, [[DT * TOK, 128], [128, 2], [-1, 128]])
                        dve.tensor_copy(back, src[:, 0:256].rearrange("p (b n) -> p b n", b=2))\
                            .then_inc(*v_copy.mark((l, "q latents", t)))
                        dve.tensor_copy(q[:, t, 256:512], src[:, 256:512]).then_inc(*v_copy.mark((l, "q", t)))
                    for t in range(DT):
                        copy_tile(k[:, t, :], (l, "k", t))
                    for t in range(8):
                        copy_tile(v[:, t % 4, (t // 4) * 512:(t // 4) * 512 + 512], (l, "v", t))
                else:
                    rotated.clear()
                    for t in range(DT):
                        copy_tile(q[:, t, :], (l, "q", t))
                        if t:
                            rotate(q[:, t - 1, 0:256], (l, "q", t - 1))
                    copy_tile(kd[:, 0, :], (l, "kd", 0))
                    rotate(q[:, DT - 1, 0:256], (l, "q", DT - 1))
                    copy_tile(kd[:, 1, :], (l, "kd", 1))
                    rotate(kd[:, 0, 0:256], (l, "kd", 0))
                    key = (l, "vs", 0)
                    ahead(key)
                    dve.wait_ge(*whole(key))
                    dve.tensor_copy(v[:, :, 0:128], psum(key)[:, :].rearrange("p (a n) -> p a n", a=4))\
                        .then_inc(*v_copy.mark(key))
                    rotate(kd[:, 1, 0:256], (l, "kd", 1))

                H = heads(l)
                scale = float(NOPE + ROPE) ** -0.5 if KIND[l] == MLA else float(HD) ** -0.5
                todo = units(l)
                bias_units = [w for w in todo if w[2] < 2] if KIND[l] == NA else []

                def maxima(u, g, rt):
                    for hh in range(H):
                        S = bank[(2 * (u % 2) + hh) if H == 2 else u % 2]
                        dve.wait_ge(*pe_s.at((l, u, hh)))
                        if KIND[l] == NA and rt < 2:
                            dve.wait_ge(*g_bias.at((l, u, hh)))
                            n = bias_units.index((u, g, rt))
                            dve.scalar_tensor_tensor(S[:, 0:256], BM[:, n % 2, hh, :], 1.0 / scale, S[:, 0:256],
                                                     ALU.mult, ALU.add).then_inc(*v_soft.mark((l, "bias", u, hh)))
                            dve.wait_ge(*v_soft.at((l, "bias", u, hh)))
                        if KIND[l] == SWA and rt < 2:
                            far = S[:, 128:256] if rt == 0 else S[:, 0:128]
                            dve.tensor_tensor(far, far, cst[:, C_SWAM + rt * 128:C_SWAM + rt * 128 + 128], ALU.add)\
                                .then_inc(*v_soft.mark((l, "bias", u, hh)))
                            dve.wait_ge(*v_soft.at((l, "bias", u, hh)))
                        nq = 2 if rt == 2 else 1
                        dve.tensor_reduce(mx[:, u % 2, hh, 0:nq], S[:, :].rearrange("p (a n) -> p a n", a=nq),
                                          AX.X, ALU.max).then_inc(*v_soft.mark((l, "max", u, hh)))
                        dve.wait_ge(*v_soft.at((l, "max", u, hh)))
                        if u >= 2:
                            dve.wait_ge(*a_exp.at((l, u - 2, hh, "sink" if KIND[l] == SWA else
                                                   (1 if todo[u - 2][2] == 2 else 0))))
                        if KIND[l] == SWA:
                            h = 2 * g + hh
                            dve.tensor_scalar(mx[:, u % 2, hh, 0:nq], mx[:, u % 2, hh, 0:nq], scale,
                                              sink[:, h:h + 1], ALU.mult, ALU.max)\
                                .then_inc(*v_soft.mark((l, "smax", u, hh)))
                            dve.wait_ge(*v_soft.at((l, "smax", u, hh)))
                            dve.tensor_scalar(ngm[:, u % 2, hh, 0:nq], mx[:, u % 2, hh, 0:nq], -1.0, None, ALU.mult)\
                                .then_inc(*v_soft.mark((l, "neg", u, hh)))
                        else:
                            dve.tensor_scalar(ngm[:, u % 2, hh, 0:nq], mx[:, u % 2, hh, 0:nq], -scale, None, ALU.mult)\
                                .then_inc(*v_soft.mark((l, "neg", u, hh)))

                def divide(u, g, rt):
                    nq = 2 if rt == 2 else 1
                    for hh in range(H):
                        dve.wait_ge(*a_exp.at((l, u, hh, "sink" if KIND[l] == SWA else nq - 1)))
                        if u >= 2 and hh == 1:
                            dve.wait_ge(*g_soft.at((l, u - 2, 1, 0 if todo[u - 2][2] < 2 else 1)))
                        if KIND[l] == SWA:
                            dve.tensor_tensor(esum[:, u % 2, hh, 0:nq], esum[:, u % 2, hh, 0:nq],
                                              esnk[:, u % 2, hh, 0:nq], ALU.add).then_inc(*v_soft.mark((l, "sum", u, hh)))
                            dve.wait_ge(*v_soft.at((l, "sum", u, hh)))
                        dve.reciprocal(rsum[:, u % 2, hh, 0:nq], esum[:, u % 2, hh, 0:nq])\
                            .then_inc(*v_soft.mark((l, "recip", u, hh)))
                        if hh == 0:
                            dve.wait_ge(*v_soft.at((l, "recip", u, hh)))
                            for qh in range(nq):
                                cut = slice(0, 512) if rt < 2 else slice(qh * 256, qh * 256 + 256)
                                dve.tensor_scalar(P[:, u % PROBS, 0, cut], P[:, u % PROBS, 0, cut],
                                                  rsum[:, u % 2, 0, qh:qh + 1], None, ALU.mult)\
                                    .then_inc(*v_soft.mark((l, "p", u, 0)))

                def output(g):
                    dve.wait_ge(*a_h.at((l, "o", g)))
                    dve.tensor_tensor(hL[:, g, 0:N], bank[6][:, 0:N], hH[:, g, 0:N].bitcast(F32), ALU.subtract)\
                        .then_inc(*v_h.mark((l, "olo", g)))

                last_rt = todo[-1][2]
                parts = modparts(l)
                for n in range(len(todo) + LAG + 2):
                    ended = parts[n - 1][:2] if 1 <= n <= len(parts) and parts[n - 1][2] == DT - 1 else None
                    if ended:
                        mod_rows(*ended)
                    if 1 <= n <= len(todo):
                        divide(*todo[n - 1])
                    if n < len(todo):
                        maxima(*todo[n])
                    if n >= LAG + 2 and todo[n - LAG - 2][2] == last_rt:
                        output(todo[n - LAG - 2][1])
                    if ended:
                        mod_columns(*ended)
                coef_g(0, l)
                coef_a(1, l)
                coef_g(1, l)
                dve.wait_ge(*v_mod.at((l, "G", 1)))

                def outputs(what, which):
                    def add_up(kind, t):
                        if kind == XG:
                            dve.wait_ge(*v_dot.at((l, what, "product")))
                        else:
                            dve.wait_ge(*a_sq.at((l, what, t) if kind == YY else (l, what, kind, t)))
                            if t >= 2:
                                dve.wait_ge(*v_dot.at((l, what, kind, t - 1)))
                        total = dots[what][:, kind, 0, 0:N]
                        dve.tensor_tensor(total, total, slot_of(what, kind, t)[:, 0:N], ALU.add)\
                            .then_inc(*v_dot.mark((l, what, kind, t)))

                    for t in range(DT):
                        if t == 0:
                            dve.wait_ge(*pe_mod.at(parts[-1]))
                        if t >= 2:
                            for kind in kinds(l, what):
                                if kind != XG:
                                    add_up(kind, t - 1)
                        if t == DT - 1 and XX in kinds(l, what):
                            add_up(XX, t)
                        ahead((l, what, t))
                        dve.wait_ge(*whole((l, what, t)))
                        for s, t0, t1 in spans(l):
                            dve.tensor_scalar(y[:, t, t0:t1], psum((l, what, t))[:, t0:t1],
                                              coefG[:, which, t, s:s + 1], None, ALU.mult)\
                                .then_inc(*v_copy.mark((l, what, t)))
                    t = DT - 1
                    if XG in kinds(l, what):
                        dve.wait_ge(*v_copy.at((l, what, t)))
                        dve.wait_ge(*g_dot.at((l, what, "sum", t - 1)))
                        dve.tensor_tensor(slot_of(what, XG, t)[:, 0:N], x[:, t, 0:N], y[:, t, 0:N], ALU.mult)\
                            .then_inc(*v_dot.mark((l, what, "product")))
                    for kind in kinds(l, what):
                        if kind != XX:
                            add_up(kind, t)

                outputs("o", 0)
                sandwich((l, "ffn"), (l, "post", "o"), N, first[l, "in"] + AHEAD)

                def products(j0, n, i=0):
                    for j in range(j0, j0 + n):
                        c = first[l, "in"] + 2 * j
                        for b in range(2):
                            if c + b not in after_norm:
                                split_lo(dve, True, c + b + AHEAD, i, 2 * n)
                        up = psum((l, "in", 2 * j + 1))[:, 0:N]
                        inner = [p[:, :, :].rearrange("p t n -> p (t n)")[:, bass.ds(i * (n * TOK) + j * TOK, N)]
                                 for p in (aH, aL)]
                        dve.wait_ge(w_used, i * (2 * n) + (c + 2))
                        dve.wait_ge(*a_gate.paced(i, (l, "silu", j), n))
                        if j >= 2:
                            dve.wait_ge(*v_ffn.paced(i, (l, "lo", j - 2), n))
                        dve.tensor_tensor(sq[:, j % 2, 0:N], up, tmp[:, j % 2, 0:N], ALU.mult)\
                            .then_inc(*v_ffn.mark((l, "a", j)))
                        dve.tensor_tensor(inner[0], up, tmp[:, j % 2, 0:N], ALU.mult).then_inc(*v_ffn.mark((l, "hi", j)))
                        dve.wait_ge(*v_ffn.paced(i, (l, "hi", j), n))
                        dve.tensor_tensor(inner[1], sq[:, j % 2, 0:N], inner[0].bitcast(F32), ALU.subtract)\
                            .then_inc(*v_ffn.mark((l, "lo", j)))

                if l < DEPTH - 1:
                    mod_rows(l + 1, 0)
                products(0, 1)
                if l < DEPTH - 1:
                    mod_columns(l + 1, 0)
                    coef_a(0, l + 1)
                    dve.wait_ge(*v_mod.at((l + 1, "A", 0)))
                products(1, PEELED - 1)
                start = v_ffn.count
                with dve.Fori(0, TURNS) as i:
                    products(PEELED, PAIRS, i)
                v_ffn.repeated(start, TURNS, PAIRS)
                outputs("out", 1)
                if l < DEPTH - 1:
                    sandwich((l + 1, "mix"), (l, "post", "out"), N, first[l, "out"] + 3 * DT + AHEAD)
                else:
                    mean_eps((l, "post", "out"), AUX, N)
                    dve.wait_ge(*pe_aux.at(((l, "post", "out"), "bcast")))
                    for t in range(DT):
                        residual((DEPTH, "mix"), t, N)

            for i in range(2):
                for half in range(2):
                    dve.wait_ge(*pe_aux.at(("out", i, half)))
                    dve.tensor_copy(xrow[:, i, half * 512:half * 512 + 512], bank[2 * i + half][:, :])\
                        .then_inc(*v_copy.mark(("out", i, half)))

        @block.tensor
        def _(pe):
            mm = nc.tensor.matmul

            def three(o, wh, wl, mh, ml, start, stop):
                mm(o, wh, mh, start=start, stop=False)
                mm(o, wh, ml, start=False, stop=False)
                return mm(o, wl, mh, start=False, stop=stop)

            def free_bank(key):
                p = prior[number[key]]
                if p is not None:
                    for s, label in frees[p]:
                        pe.wait_ge(*s.at(label))

            def slot(c, kt, n):
                return [w[:, c % SPLIT, 0:kt * n].rearrange("p (k n) -> p k n", k=kt) for w in (wH, wL)]

            def stats(key, t, n, col=per_d):
                for b in range(n // 128):
                    last = mm(STAT[:, b:b + 1], sq[:, t % 2, b * 128:b * 128 + 128], col,
                              start=(t == 0 and b == 0), stop=(t == DT - 1), skip_group_check=True)
                last.then_inc(*pe_aux.mark((key, "stat", t)))
                if t == DT - 1:
                    pe_aux.known[key, "stats"] = pe_aux.count

            def broadcast(key, n, dst, col=0, label=("bcast",)):
                pe.wait_ge(*g_norm.at(key))
                for b in range(n // 128):
                    last = nc.tensor.transpose(dst[:, b * 128:b * 128 + 128],
                                               rstd[:, col + b:col + b + 1].broadcast_to([128, 128]), ident)
                last.then_inc(*pe_aux.mark((key,) + label))

            def norm_x(key, n):
                for t in range(DT):
                    pe.wait_ge(*a_sq.at((key, t)))
                    stats(key, t, n)
                broadcast(key, n, RB2)

            def means(l, what, n, kind):
                pe.wait_ge(*v_dot.at((l, what, kind, DT - 1)))
                if kind == YY and what == "o":
                    pe.wait_ge(*v_mod.at(modparts(l)[-1][:2]))
                src = dots[what][:, kind, 0, :]
                for b in range(n // 128):
                    last = mm((AUX if kind == YY else STAT)[:, 4 * kind + b:4 * kind + b + 1],
                              src[:, b * 128:b * 128 + 128], per_d, start=True, stop=True)
                return last

            def norms(l, what, n, key, mods=False):
                if key:
                    means(l, what, n, XX)
                means(l, what, n, YY).then_inc(*pe_aux.mark(((l, "post", what), "stats")))
                if key:
                    means(l, what, n, XG)
                    means(l, what, n, GG).then_inc(*pe_aux.mark(((l, "post", what), "sums")))
                broadcast((l, "post", what), n, RB1)
                if mods:
                    mod_product((l + 1, 0, 0))
                if key:
                    broadcast(key, n, RB2, 4)
                if mods:
                    for kt in range(1, DT):
                        mod_product((l + 1, 0, kt))

            def h_ready(key, t):
                pe.wait_ge(*lo_ready(key, t))

            def column_tile(c, key, n, mH, mL, i=0, step=0):
                if step:
                    pe.wait_ge(*v_ffn.paced(i, frees[prior[number[key]]][0][1], step // 2))
                else:
                    free_bank(key)
                pe.wait_ge(*lo_of(c, i, step))
                wh, wl = slot(c, DT, 128)
                for kt in range(DT):
                    last = three(psum(key)[:, 0:n], wh[:, kt, :], wl[:, kt, :], mH[:, kt, 0:n], mL[:, kt, 0:n],
                                 kt == 0, kt == DT - 1)
                last.then_inc(w_used, 1)

            def mod_product(part):
                m, r, kt = part
                if r == 0:
                    pe.wait_ge(*modloaded0[kt].at(part))
                    w = modw0[:, kt, :]
                else:
                    n = modindex[part]
                    pe.wait_ge(*modloaded[n % 2].at(part))
                    w = modw[:, n % 2, :]
                if kt == 0 and (m, r) != (0, 0):
                    pe.wait_ge(*v_mod.at((m, r - 1) if r else (m - 1, 2)))
                for i in range(4):
                    last = mm(AUX[32 * i:32 * i + 32, :], cpad[:, kt, :], w[:, i * 512:i * 512 + 512],
                              start=(kt == 0), stop=(kt == DT - 1))
                last.then_inc(*pe_mod.mark(part))

            def mod_transpose(m, r):
                pe.wait_ge(*v_mod.at((m, r, "rows")))
                for i in range(4):
                    last = nc.tensor.transpose(AUX[:, i * 128:i * 128 + 128], modrow[:, i * 128:i * 128 + 128], ident)
                last.then_inc(*pe_aux.mark((m, r, "modT")))

            def rotation(tl, key, copied):
                pe.wait_ge(*v_copy.at(copied))
                if turned:
                    pe.wait_ge(*v_step.at((turned[-1], "r1")))
                mm(AUX[:, 0:256], rot, tl, start=True, stop=True).then_inc(*pe_aux.mark((key, "rot")))
                turned.append(key)

            turned = []

            pe.wait_ge(*inputs_in.at("vectors"))
            nc.tensor.transpose(bank[0][:, 0:128], grow[:, :], ident)
            for u in range(2):
                nc.tensor.transpose(bank[0][:, 128 + 96 * u:224 + 96 * u], brow[:, u, :], ident[0:96, 0:96])
            nc.tensor.transpose(bank[0][:, 320:344], srow[:, :], ident[0:24, 0:24]).then_inc(*pe_aux.mark("small"))
            pe.wait_ge(*rows_in.at("rows"))
            for t in range(DT):
                if t >= 3:
                    pe.wait_ge(*v_x.at(((0, "mix"), t - 3)))
                for i in range(4):
                    last = nc.tensor.transpose(bank[1 + t % 3][:, i * 128:i * 128 + 128],
                                               xrow[:, i, t * 128:t * 128 + 128], ident)
                last.then_inc(*pe_aux.mark(("x", t)))
            norm_x((0, "mix"), TOK)
            pe.wait_ge(*a_misc.at(("c", 1)))
            for t in range(DT):
                mod_product((0, 0, t))
            mod_transpose(0, 0)

            for l in range(DEPTH):
                N = width(l)
                key = (l, "mix")

                def first_two(what, n, ready):
                    c = first[l, what]
                    for i in range(2):
                        free_bank((l, what, i))
                    w = [slot(c + i, DT, 128) for i in range(2)]
                    for kt in range(DT):
                        ready(kt)
                        for i in range(2):
                            if kt == 0:
                                pe.wait_ge(*lo_of(c + i))
                            last = three(psum((l, what, i))[:, 0:n], w[i][0][:, kt, :], w[i][1][:, kt, :],
                                         hH[:, kt, 0:n], hL[:, kt, 0:n], kt == 0, kt == DT - 1)
                            if kt == DT - 1:
                                last.then_inc(w_used, 1)

                def col_phase(what, n, mH, mL, i=0):
                    c = first[l, what] + i
                    while chunks[c][:2] == (l, what):
                        column_tile(c, (l, what, i), n, mH, mL)
                        c += 1
                        i += 1

                def ready(kt):
                    h_ready(key, kt)

                if KIND[l] == MLA:
                    first_two("lat", TOK, ready)
                    def latent_stats(w):
                        for t in (2 * w, 2 * w + 1):
                            pe.wait_ge(*a_sq.at((l, "lat", t)))
                            for b in range(4):
                                last = mm(STAT[:, 4 * w + b:4 * w + b + 1], sq[:, t % 2, b * 128:b * 128 + 128], per_l,
                                          start=(t % 2 == 0 and b == 0), stop=(t % 2 == 1), skip_group_check=True)
                            last.then_inc(*pe_aux.mark((l, "latstat", t)))

                    column_tile(first[l, "lat"] + 2, (l, "lat", 2), TOK, hH, hL)
                    latent_stats(0)
                    column_tile(first[l, "lat"] + 3, (l, "lat", 3), TOK, hH, hL)
                    broadcast((l, "lat", 0), TOK, RB1)
                    col_phase("pe", TOK, hH, hL)
                    pe.wait_ge(*v_norm.at(((l, "lat", 0), "mean")))
                    latent_stats(1)
                    turned.clear()
                    rotation(kpe[:, 0:256], (l, "kpe"), (l, "pe", 0))
                    for t in range(4):
                        c = first[l, "uq"] + t
                        wh, wl = slot(c, 2, 384)
                        pe.wait_ge(*lo_of(c))
                        if t == 0:
                            pe.wait_ge(*v_h.at((l, "latlo", 1)))
                        for part in range(3):
                            tk = (l, "uq", t, part)
                            free_bank(tk)
                            for kt in range(2):
                                s = [w[:, kt, part * 128:part * 128 + 128] for w in (wh, wl)]
                                last = three(psum(tk)[:, 0:N], s[0], s[1], latH[:, kt, 0:N], latL[:, kt, 0:N],
                                             kt == 0, kt == 1)
                            last.then_inc(*(tile_done.mark(tk) if part < 2 else (w_used, 1)))
                        if t == 0:
                            broadcast((l, "lat", 1), TOK, RB2, 4)
                        else:
                            rotation(qpe[:, t - 1, 0:256], (l, "qpe", t - 1), (l, "uq", t - 1, 2))
                    for t in range(4):
                        c = first[l, "ukv"] + t
                        wh, wl = slot(c, 2, 512)
                        pe.wait_ge(*lo_of(c))
                        if t == 0:
                            pe.wait_ge(*v_h.at((l, "latlo", 3)))
                        for part in range(4):
                            tk = (l, "ukv", t, part)
                            free_bank(tk)
                            if part < 2:
                                for kt in range(2):
                                    s = [w[:, kt, part * 256:part * 256 + 128] for w in (wh, wl)]
                                    last = three(psum(tk)[:, :], s[0], s[1], latH[:, 2 + kt, :], latL[:, 2 + kt, :],
                                                 kt == 0, kt == 1)
                            else:
                                for tt in range(2):
                                    tok = 2 * (part - 2) + tt
                                    for kt in range(2):
                                        m = [w[:, kt, :].rearrange("p (h n) -> p h n", h=2)[:, :, 128:256] for w in (wh, wl)]
                                        cut = slice(tok * 128, tok * 128 + 128)
                                        last = three(psum(tk)[:, tt * 256:tt * 256 + 256], latH[:, 2 + kt, cut],
                                                     latL[:, 2 + kt, cut], m[0], m[1], kt == 0, kt == 1)
                            last.then_inc(*(tile_done.mark(tk) if part < 3 else (w_used, 1)))
                        if t == 0:
                            rotation(qpe[:, 3, 0:256], (l, "qpe", 3), (l, "uq", 3, 2))
                elif KIND[l] == NA:
                    first_two("q", TOK, ready)
                    col_phase("q", TOK, hH, hL, 2)
                    col_phase("k", TOK, hH, hL)
                    for half in range(2):
                        for kk in range(4):
                            c = first[l, "v"] + half * 4 + kk
                            wh, wl = slot(c, 2, 512)
                            pe.wait_ge(*lo_of(c))
                            for tok in range(4):
                                tk = (l, "v", half * 4 + tok)
                                if kk == 0:
                                    free_bank(tk)
                                cut = slice(tok * 128, tok * 128 + 128)
                                for k2 in range(2):
                                    kt = 2 * kk + k2
                                    last = three(psum(tk)[:, :], hH[:, kt, cut], hL[:, kt, cut], wh[:, k2, :],
                                                 wl[:, k2, :], kt == 0, kt == DT - 1)
                                if kk == 3 and tok < 3:
                                    last.then_inc(*tile_done.mark(tk))
                            last.then_inc(w_used, 1)
                else:
                    turned.clear()
                    first_two("q", TOK, ready)
                    for t in range(1, DT):
                        c = first[l, "q"] + t
                        if t > 1:
                            column_tile(c, (l, "q", t), TOK, hH, hL)
                        if t:
                            rotation(q[:, t - 1, 0:256], (l, "q", t - 1), (l, "q", t - 1))
                    for t in range(KV_HEADS):
                        c = first[l, "kd"] + t
                        column_tile(c, (l, "kd", t), TOK, hH, hL)
                        if t == 0:
                            rotation(q[:, DT - 1, 0:256], (l, "q", DT - 1), (l, "q", DT - 1))
                        else:
                            rotation(kd[:, 0, 0:256], (l, "kd", 0), (l, "kd", 0))
                    c = first[l, "vs"]
                    tk = (l, "vs", 0)
                    wh, wl = slot(c, DT, 128)
                    pe.wait_ge(*lo_of(c))
                    free_bank(tk)
                    for tok in range(4):
                        cut = slice(tok * 128, tok * 128 + 128)
                        for kt in range(DT):
                            last = three(psum(tk)[:, cut], hH[:, kt, cut], hL[:, kt, cut], wh[:, kt, :], wl[:, kt, :],
                                         kt == 0, kt == DT - 1)
                    last.then_inc(w_used, 1)
                    rotation(kd[:, 1, 0:256], (l, "kd", 1), (l, "kd", 1))

                H = heads(l)
                todo = units(l)
                parts = modparts(l)
                last_rt = todo[-1][2]
                if KIND[l] == MLA:
                    ready_kv = [(v_copy, (l, "ukv", 3, 2)), (a_copy, (l, "ukv", 3, 3)), (v_step, ((l, "qpe", 3), "r3"))]
                elif KIND[l] == NA:
                    ready_kv = [(v_copy, (l, "v", 7))]
                else:
                    ready_kv = [(v_copy, (l, "vs", 0)), (v_step, ((l, "kd", 1), "r3"))]

                def scores(u, g, rt):
                    if u == 0:
                        for s, label in ready_kv:
                            pe.wait_ge(*s.at(label))
                    for hh in range(H):
                        if u >= 2:
                            pu = todo[u - 2]
                            pe.wait_ge(*a_exp.at((l, u - 2, hh, 1 if pu[2] == 2 else 0)))
                    todo_q = [(rt * 128, 0, 512)] if rt < 2 else [(256, 0, 256), (384, 256, 512)]
                    for q0, s0, s1 in todo_q:
                        k0 = 0 if rt < 2 else 256
                        for hh in range(H):
                            S = bank[(2 * (u % 2) + hh) if H == 2 else u % 2]
                            if KIND[l] == MLA:
                                r = slice(64 * (g % 2), 64 * (g % 2) + 64)
                                mm(S[:, s0:s1], q[:, g, q0:q0 + 128], k[:, g, k0:512], start=True, stop=False)
                                last = mm(S[:, s0:s1], qpe[r, g // 2, q0:q0 + 128], kpe[r, k0:512], start=False, stop=True)
                            else:
                                r = slice(64 * hh, 64 * hh + 64)
                                keys = k[r, g, k0:512] if KIND[l] == NA else kd[r, g // 4, k0:512]
                                last = mm(S[:, s0:s1], q[r, g, q0:q0 + 128], keys, start=True, stop=True)
                            if s1 == 512:
                                last.then_inc(*pe_s.mark((l, u, hh)))

                def transposes(u, g, rt):
                    nq = 2 if rt == 2 else 1
                    for hh in range(H):
                        if hh == 0:
                            pe.wait_ge(*v_soft.at((l, "p", u, 0)))
                        else:
                            pe.wait_ge(*g_soft.at((l, u, 1, nq - 1)))
                        T = bank[4 + (hh if H == 2 else u % 2)]
                        before = u - 1 if H == 2 else u - 2
                        if before >= 0:
                            pe.wait_ge(*a_pt.at((l, before, hh)))
                        for b in range(4):
                            last = nc.tensor.transpose(T[:, b * 128:b * 128 + 128], P[:, u % PROBS, hh, b * 128:b * 128 + 128],
                                                       flip if KIND[l] == NA and rt < 2 else ident)
                        last.then_inc(*pe_t.mark((l, u, hh)))

                def values(g):
                    u = [w for w in todo if w[1] == g][-1][0]
                    for hh in range(H):
                        pe.wait_ge(*a_pt.at((l, u, hh)))
                    if g:
                        pe.wait_ge(*v_h.at((l, "olo", g - 1)))
                    m = 128 // H
                    for part in range(1 if N == SEQ else 2):
                        tiles_k = [(kt, kt) for kt in range(4)] if part == 0 else [(2, 4), (3, 5)]
                        for i, (kt, pt) in enumerate(tiles_k):
                            for hh in range(H):
                                if KIND[l] == SWA:
                                    vh = v[:, kt, (g // 4) * 64:(g // 4) * 64 + 64]
                                else:
                                    vh = v[:, kt, g * 128 + hh * m:g * 128 + hh * m + m]
                                last = mm(bank[6][hh * m:hh * m + m, part * 256:part * 256 + 256], vh, PT[:, hh, pt, :],
                                          start=(i == 0), stop=(i == len(tiles_k) - 1))
                    last.then_inc(*pe_o.mark((l, g)))

                for n in range(len(todo) + LAG + 1):
                    if n < len(todo):
                        scores(*todo[n])
                    if n > LAG and todo[n - LAG - 1][2] == last_rt:
                        values(todo[n - LAG - 1][1])
                    if 0 <= n - LAG < len(todo):
                        transposes(*todo[n - LAG])
                    if 1 <= n <= len(parts) and parts[n - 1][2] == DT - 1:
                        mod_transpose(*parts[n - 1][:2])
                    if n < len(parts):
                        mod_product(parts[n])

                pe.wait_ge(*v_h.at((l, "olo", DT - 1)))
                col_phase("o", N, hH, hL)
                norms(l, "o", N, (l, "ffn"), mods=l < DEPTH - 1)

                fk = (l, "ffn")
                first_two("in", N, lambda kt: h_ready(fk, kt))
                for j in range(2, 2 * PEELED):
                    if j == 3 and l < DEPTH - 1:
                        mod_transpose(l + 1, 0)
                    column_tile(first[l, "in"] + j, (l, "in", j), N, hH, hL)
                with pe.Fori(0, TURNS) as i:
                    for j in range(2 * PEELED, 2 * PEELED + 2 * PAIRS):
                        column_tile(first[l, "in"] + j, (l, "in", j), N, hH, hL, i, 2 * PAIRS)

                def out_tiles(t0, n, i=0):
                    for t in range(t0, t0 + n):
                        if t < 2:
                            free_bank((l, "out", t))
                        else:
                            for s in (v_copy, a_sq):
                                pe.wait_ge(*s.paced(i, (l, "out", t - 2), n))
                        for kg in range(3):
                            c = first[l, "out"] + 3 * t + kg
                            kn = min(8, FT - 8 * kg)
                            wh, wl = slot(c, kn, 128)
                            pe.wait_ge(*lo_of(c, i, 3 * n))
                            if t == 0:
                                pe.wait_ge(*v_ffn.at((l, "lo", 8 * kg + kn - 1)))
                            for kt in range(kn):
                                kk = 8 * kg + kt
                                last = three(psum((l, "out", t))[:, 0:N], wh[:, kt, :], wl[:, kt, :],
                                             aH[:, kk, 0:N], aL[:, kk, 0:N], kk == 0, kk == FT - 1)
                            last.then_inc(w_used, 1)

                out_tiles(0, 2)
                with pe.Fori(0, out_turns(l)) as i:
                    out_tiles(2, 2, i)
                for t in range(2 + 2 * out_turns(l), DT, 2):
                    out_tiles(t, 2)
                norms(l, "out", N, (l + 1, "mix") if l < DEPTH - 1 else None)

            for t in range(DT):
                pe.wait_ge(*x_ready((DEPTH, "mix"), t))
            for i in range(2):
                for half in range(2):
                    for b in range(4):
                        last = nc.tensor.transpose(bank[2 * i + half][:, b * 128:b * 128 + 128],
                                                   x[:, 4 * half + b, i * 128:i * 128 + 128], ident)
                    last.then_inc(*pe_aux.mark(("out", i, half)))


def tables():
    import numpy as np
    c = np.zeros((128, C_END), np.float32)
    c[:, C_ID:C_ID + 128] = np.eye(128)
    rot = np.zeros((128, 128), np.float32)
    for m in range(128):
        if m % 64 < 32:
            rot[m + 32, m] = -1.0
        else:
            rot[m - 32, m] = 1.0
    c[:, C_ROT:C_ROT + 128] = rot
    t = np.arange(SEQ)
    n_freq = ROPE // 4
    inv = np.float32(ROPE_THETA) ** (-np.arange(n_freq, dtype=np.float32) / np.float32(n_freq))
    ang = np.concatenate([(t // GRID_W).astype(np.float32)[:, None] * inv,
                          (t % GRID_W).astype(np.float32)[:, None] * inv], -1)
    c[:, C_COS:C_COS + 256] = np.tile(np.cos(ang).T, (4, 1))
    c[:, C_SIN:C_SIN + 256] = np.tile(np.sin(ang).T, (4, 1))
    cols = np.arange(GRID_W)
    start = np.clip(cols - WIN_COLS // 2, 0, GRID_W - WIN_COLS)
    ok = (cols[None, :] >= start[:, None]) & (cols[None, :] < start[:, None] + WIN_COLS)
    c[:, C_NAM:C_NAM + 64] = np.tile(np.where(ok, 0.0, NEG)[::-1], (2, 1))
    i = np.arange(128)
    c[:, C_SWAM:C_SWAM + 128] = np.where(i[None, :] > i[:, None], NEG, 0.0)
    c[:, C_SWAM + 128:C_SWAM + 256] = np.where(i[None, :] < i[:, None], NEG, 0.0)
    c[:, C_PD] = 1.0 / D_MODEL
    c[:, C_PL] = 1.0 / LORA
    c[:, C_EXP:C_EXP + 8] = -0.5
    c[:, C_FLIP:C_FLIP + 128] = np.eye(128)[::-1]
    return c


_INS = ["x", "c", "ctx", "c_ctx", "w_mod", "b_mod", "g_pre_mix", "g_post_mix", "g_pre_ffn", "g_post_ffn",
        "w_ffn_in", "w_ffn_out", "mla_w_in", "mla_g_q", "mla_w_uq", "mla_g_kv", "mla_w_ukv", "mla_w_o",
        "na_w_qkv", "na_rpb", "na_w_o", "swa_w_qkv", "swa_sink", "swa_w_o"]


def kernel(**inputs):
    import numpy as _np
    import concourse.bacc as _bacc
    from concourse import mybir as _mybir
    from concourse.bass_utils import run_bass_kernel_spmd as _run

    arrays = {n: _np.ascontiguousarray(inputs[n]) for n in _INS}
    arrays["consts"] = tables()
    known = {}
    for tracing in range(2):
        nc = _bacc.Bacc("TRN2", target_bir_lowering=False, num_devices=1)
        args = {n: nc.dram_tensor(f"in_{n}", a.shape, _mybir.dt.from_np(a.dtype), kind="ExternalInput").ap()
                for n, a in arrays.items()}
        out = nc.dram_tensor("out_0", (1, SEQ, D_MODEL), F32, kind="ExternalOutput").ap()
        trunk(nc, args, out, known)
    r = _run(nc, [{f"in_{n}": a for n, a in arrays.items()}], core_ids=[0])
    return r.results[0]["out_0"]
```
